# Optimizing a Trainium2 kernel written in Bass

```python
import jax
import jax.numpy as jnp
from jax import lax
import numpy as np

D_MODEL = 1024
BATCH = 1
SEQ = 256
DEPTH = 2

D_MIX = D_MODEL
ML_WIDTH = D_MIX // 2
ML_HEADS = 4
ML_HEAD_DIM = ML_WIDTH // ML_HEADS
RG_WIDTH = D_MIX - ML_WIDTH
RG_BLOCKS = 8
RG_BLOCK_DIM = RG_WIDTH // RG_BLOCKS
RG_C = 8.0
CONV_WIDTH = 4
CHUNK = 128
D_IN = 4 * ML_WIDTH + 2 * ML_HEADS + 2 * RG_WIDTH
D_FF_DENSE = ((8 * D_MODEL // 3 + 127) // 128) * 128
N_EXPERTS = 8
TOP_K = 2
D_FF_EXPERT = 7 * D_MODEL // 2
N_DENSE = (DEPTH + 1) // 2
N_MOE = DEPTH // 2
EPS = 1e-6

kernel_name = 'hybrid_mlstm_rglru_moe'

def _rms(x):
    x = x.astype(jnp.float32)
    return x * lax.rsqrt(jnp.mean(x * x, axis=-1, keepdims=True) + EPS)

def rmsnorm(x, g):
    return (_rms(x) * g.astype(jnp.float32)).astype(x.dtype)

def mlstm_chunkwise(q, k, v, i_pre, f_pre):
    B, S, H, Dh = q.shape
    L = CHUNK
    NC = S // L

    def chunks(t):
        t = t.astype(jnp.float32).reshape((B, NC, L, H) + t.shape[3:])
        return jnp.moveaxis(t, 3, 1)

    q = chunks(q)
    k = chunks(k) * (Dh ** -0.5)
    v = chunks(v)
    log_i = chunks(i_pre)
    log_f = jax.nn.log_sigmoid(chunks(f_pre))
    b = jnp.cumsum(log_f, axis=-1)
    g = b[..., -1]

    a = g[..., None] - b + log_i
    m_loc = jnp.max(a, axis=-1)
    w = jnp.exp(a - m_loc[..., None])
    C_loc = jnp.einsum('bhcl,bhcld,bhcle->bhcde', w, k, v)
    n_loc = jnp.einsum('bhcl,bhcld->bhcd', w, k)

    def step(carry, xs):
        C, n, m = carry
        g_c, m_l, C_l, n_l = xs
        m_new = jnp.maximum(g_c + m, m_l)
        s_old = jnp.exp(g_c + m - m_new)
        s_loc = jnp.exp(m_l - m_new)
        C_new = s_old[..., None, None] * C + s_loc[..., None, None] * C_l
        n_new = s_old[..., None] * n + s_loc[..., None] * n_l
        return (C_new, n_new, m_new), (C, n, m)

    init = (jnp.zeros((B, H, Dh, Dh), jnp.float32),
            jnp.zeros((B, H, Dh), jnp.float32),
            jnp.zeros((B, H), jnp.float32))
    xs = (jnp.moveaxis(g, 2, 0), jnp.moveaxis(m_loc, 2, 0),
          jnp.moveaxis(C_loc, 2, 0), jnp.moveaxis(n_loc, 2, 0))
    _, (C_prev, n_prev, m_prev) = lax.scan(step, init, xs)
    C_prev = jnp.moveaxis(C_prev, 0, 2)
    n_prev = jnp.moveaxis(n_prev, 0, 2)
    m_prev = jnp.moveaxis(m_prev, 0, 2)

    causal = jnp.tril(jnp.ones((L, L), dtype=bool))
    d_log = b[..., :, None] - b[..., None, :] + log_i[..., None, :]
    d_log = jnp.where(causal, d_log, -jnp.inf)
    m_inter = b + m_prev[..., None]
    m_comb = jnp.maximum(m_inter, jnp.max(d_log, axis=-1))
    s_w = jnp.exp(d_log - m_comb[..., None]) * jnp.einsum('bhcld,bhcsd->bhcls', q, k)
    inter_scale = jnp.exp(m_inter - m_comb)
    num = (jnp.einsum('bhcls,bhcse->bhcle', s_w, v)
           + inter_scale[..., None] * jnp.einsum('bhcld,bhcde->bhcle', q, C_prev))
    den = jnp.sum(s_w, axis=-1) + inter_scale * jnp.einsum('bhcld,bhcd->bhcl', q, n_prev)
    h = num / jnp.maximum(jnp.abs(den), jnp.exp(-m_comb))[..., None]
    return jnp.moveaxis(h, 1, 3).reshape(B, S, H, Dh)

def causal_depthwise_conv(x, w, bias):
    K, C = w.shape
    y = lax.conv_general_dilated(x, w[:, None, :], window_strides=(1,),
                                 padding=[(K - 1, 0)],
                                 dimension_numbers=('NWC', 'WIO', 'NWC'),
                                 feature_group_count=C)
    return y + bias

def rg_lru(x, w_a, b_a, w_x, b_x, lam):
    B, S, _ = x.shape
    xf = x.astype(jnp.float32)
    xb = xf.reshape(B, S, RG_BLOCKS, RG_BLOCK_DIM)
    r = jax.nn.sigmoid(jnp.einsum('bsgi,gij->bsgj', xb, w_a.astype(jnp.float32)).reshape(B, S, RG_WIDTH)
                       + b_a.astype(jnp.float32))
    i = jax.nn.sigmoid(jnp.einsum('bsgi,gij->bsgj', xb, w_x.astype(jnp.float32)).reshape(B, S, RG_WIDTH)
                       + b_x.astype(jnp.float32))
    log_a = -RG_C * r * jax.nn.softplus(-lam.astype(jnp.float32))
    a = jnp.exp(log_a)
    u = jnp.sqrt(-jnp.expm1(2.0 * log_a)) * (i * xf)

    def combine(left, right):
        a1, b1 = left
        a2, b2 = right
        return a1 * a2, a2 * b1 + b2

    _, h = lax.associative_scan(combine, (a, u), axis=1)
    return h

def hybrid_mixer(h, w_in, ml_b_if, ml_norm_g, rg_conv_w, rg_conv_b, rg_w_a, rg_b_a,
                 rg_w_x, rg_b_x, rg_lam, rg_norm_g, w_out):
    B, S, _ = h.shape
    z = h @ w_in
    o0 = 0
    q = z[..., o0:o0 + ML_WIDTH]; o0 += ML_WIDTH
    k = z[..., o0:o0 + ML_WIDTH]; o0 += ML_WIDTH
    v = z[..., o0:o0 + ML_WIDTH]; o0 += ML_WIDTH
    o = z[..., o0:o0 + ML_WIDTH]; o0 += ML_WIDTH
    if_pre = z[..., o0:o0 + 2 * ML_HEADS].astype(jnp.float32) + ml_b_if.astype(jnp.float32); o0 += 2 * ML_HEADS
    rx = z[..., o0:o0 + RG_WIDTH]; o0 += RG_WIDTH
    rgate = z[..., o0:o0 + RG_WIDTH]

    shp = (B, S, ML_HEADS, ML_HEAD_DIM)
    ht = mlstm_chunkwise(q.reshape(shp), k.reshape(shp), v.reshape(shp),
                         if_pre[..., :ML_HEADS], if_pre[..., ML_HEADS:])
    ht = _rms(ht) * ml_norm_g.astype(jnp.float32).reshape(ML_HEADS, ML_HEAD_DIM)
    y_ml = jax.nn.sigmoid(o.astype(jnp.float32)) * ht.reshape(B, S, ML_WIDTH)

    xc = causal_depthwise_conv(rx, rg_conv_w, rg_conv_b)
    hr = rg_lru(xc, rg_w_a, rg_b_a, rg_w_x, rg_b_x, rg_lam)
    y_rg = hr * jax.nn.gelu(rgate.astype(jnp.float32), approximate=True)
    y_rg = _rms(y_rg) * rg_norm_g.astype(jnp.float32)

    y = jnp.concatenate([y_ml, y_rg], axis=-1).astype(h.dtype)
    return y @ w_out

def swiglu(x, w_gate, w_up, w_down):
    return (jax.nn.silu(x @ w_gate) * (x @ w_up)) @ w_down

def moe_swiglu(x, w_router, w_gate, w_up, w_down):
    B, S, D = x.shape
    t = x.reshape(B * S, D)
    logits = (t @ w_router).astype(jnp.float32)
    top_val, top_idx = lax.top_k(logits, TOP_K)
    top_w = jax.nn.softmax(top_val, axis=-1)
    gates = jnp.sum(jax.nn.one_hot(top_idx, N_EXPERTS, dtype=jnp.float32) * top_w[..., None], axis=1)
    out = jnp.zeros((B * S, D), jnp.float32)
    for e in range(N_EXPERTS):
        out = out + gates[:, e:e + 1] * swiglu(t, w_gate[e], w_up[e], w_down[e]).astype(jnp.float32)
    return out.astype(x.dtype).reshape(B, S, D)

def setup_inputs(seed: int = 0) -> dict:
    key = jax.random.key(seed)
    ks = jax.random.split(key, 32)

    def nrm(k, shape, scale):
        return scale * jax.random.normal(k, shape, jnp.float32)

    def gain(k, shape):
        return 1.0 + 0.02 * jax.random.normal(k, shape, jnp.float32)

    f_bias = jnp.linspace(3.0, 6.0, ML_HEADS, dtype=jnp.float32)
    ml_b_if = jnp.concatenate([nrm(ks[3], (DEPTH, ML_HEADS), 0.1),
                               f_bias + nrm(ks[4], (DEPTH, ML_HEADS), 0.1)], axis=-1)
    u = jax.random.uniform(ks[10], (DEPTH, RG_WIDTH), jnp.float32, 0.9, 0.999)
    a0 = u ** (1.0 / RG_C)
    rg_lam = jnp.log(a0) - jnp.log1p(-a0)
    return {
        'x': nrm(ks[0], (BATCH, SEQ, D_MODEL), 1.0),
        'norm_mix_g': gain(ks[1], (DEPTH, D_MODEL)),
        'w_in': nrm(ks[2], (DEPTH, D_MODEL, D_IN), D_MODEL ** -0.5),
        'ml_b_if': ml_b_if,
        'ml_norm_g': gain(ks[5], (DEPTH, ML_WIDTH)),
        'rg_conv_w': nrm(ks[6], (DEPTH, CONV_WIDTH, RG_WIDTH), CONV_WIDTH ** -0.5),
        'rg_conv_b': nrm(ks[7], (DEPTH, RG_WIDTH), 0.01),
        'rg_w_a': nrm(ks[8], (DEPTH, RG_BLOCKS, RG_BLOCK_DIM, RG_BLOCK_DIM), RG_BLOCK_DIM ** -0.5),
        'rg_b_a': nrm(ks[9], (DEPTH, RG_WIDTH), 0.01),
        'rg_w_x': nrm(ks[11], (DEPTH, RG_BLOCKS, RG_BLOCK_DIM, RG_BLOCK_DIM), RG_BLOCK_DIM ** -0.5),
        'rg_b_x': nrm(ks[12], (DEPTH, RG_WIDTH), 0.01),
        'rg_lam': rg_lam,
        'rg_norm_g': gain(ks[13], (DEPTH, RG_WIDTH)),
        'w_out': nrm(ks[14], (DEPTH, D_MIX, D_MODEL), D_MIX ** -0.5),
        'norm_ffn_g': gain(ks[15], (DEPTH, D_MODEL)),
        'ffn_w_gate': nrm(ks[16], (N_DENSE, D_MODEL, D_FF_DENSE), D_MODEL ** -0.5),
        'ffn_w_up': nrm(ks[17], (N_DENSE, D_MODEL, D_FF_DENSE), D_MODEL ** -0.5),
        'ffn_w_down': nrm(ks[18], (N_DENSE, D_FF_DENSE, D_MODEL), D_FF_DENSE ** -0.5),
        'moe_w_router': nrm(ks[19], (N_MOE, D_MODEL, N_EXPERTS), D_MODEL ** -0.5),
        'moe_w_gate': nrm(ks[20], (N_MOE, N_EXPERTS, D_MODEL, D_FF_EXPERT), D_MODEL ** -0.5),
        'moe_w_up': nrm(ks[21], (N_MOE, N_EXPERTS, D_MODEL, D_FF_EXPERT), D_MODEL ** -0.5),
        'moe_w_down': nrm(ks[22], (N_MOE, N_EXPERTS, D_FF_EXPERT, D_MODEL), D_FF_EXPERT ** -0.5),
        'norm_final_g': gain(ks[23], (D_MODEL,)),
    }

def reference(x, norm_mix_g, w_in, ml_b_if, ml_norm_g, rg_conv_w, rg_conv_b, rg_w_a, rg_b_a,
              rg_w_x, rg_b_x, rg_lam, rg_norm_g, w_out, norm_ffn_g, ffn_w_gate, ffn_w_up,
              ffn_w_down, moe_w_router, moe_w_gate, moe_w_up, moe_w_down, norm_final_g):
    h = x
    for l in range(DEPTH):
        h = h + hybrid_mixer(rmsnorm(h, norm_mix_g[l]), w_in[l], ml_b_if[l], ml_norm_g[l],
                             rg_conv_w[l], rg_conv_b[l], rg_w_a[l], rg_b_a[l], rg_w_x[l],
                             rg_b_x[l], rg_lam[l], rg_norm_g[l], w_out[l])
        u = rmsnorm(h, norm_ffn_g[l])
        j = l // 2
        if l % 2 == 0:
            h = h + swiglu(u, ffn_w_gate[j], ffn_w_up[j], ffn_w_down[j])
        else:
            h = h + moe_swiglu(u, moe_w_router[j], moe_w_gate[j], moe_w_up[j], moe_w_down[j])
    return rmsnorm(h, norm_final_g)


_drawn_inputs = setup_inputs


def setup_inputs(seed=0):
    import zlib

    import numpy as np

    out = dict(_drawn_inputs(seed))
    spreads = {}
    factors = {'ml_norm_g': 2.922, 'rg_b_a': 21.59, 'rg_b_x': 10.694, 'norm_final_g': 8.479}
    for name, (base, spread) in spreads.items():
        noise = np.random.default_rng([zlib.crc32(name.encode()), seed]).standard_normal(out[name].shape)
        drawn = base * np.exp(spread * noise) if base else spread * noise
        out[name] = jnp.asarray(drawn.astype(out[name].dtype))
    for name, factor in factors.items():
        out[name] = (out[name] * factor).astype(out[name].dtype)
    return out
```

```python
from contextlib import ExitStack

import numpy as np
import concourse.bass as bass
from concourse import mybir

F32 = mybir.dt.float32
F32R = mybir.dt.float32r
I32 = mybir.dt.int32
U32 = mybir.dt.uint32
ALU = mybir.AluOpType
ACT = mybir.ActivationFunctionType
AX = mybir.AxisListType

P = 128
BANK = 512
RAW = 6
SPLIT = 3
UNIT = 2048
EPS = 1e-6
NEG = -1e30
GELU_C = 0.7978845608028654


class Counted:

    def __init__(self, sem):
        self.sem, self.value = sem, 0

    def after(self, eng, ins):
        ins.then_inc(self.sem, 1)
        self.value += 1
        eng.wait_ge(self.sem, self.value)


def hybrid_kernel(nc, x, norm_mix_g, w_in, ml_b_if, ml_norm_g, rg_conv_w, rg_conv_b, rg_w_a, rg_b_a,
                  rg_w_x, rg_b_x, rg_lam, rg_norm_g, w_out, norm_ffn_g, ffn_w_gate, ffn_w_up,
                  ffn_w_down, moe_w_router, moe_w_gate, moe_w_up, moe_w_down, norm_final_g, out):
    _, S, D = x.shape
    LAYERS = w_in.shape[0]
    ML = ml_norm_g.shape[1]
    RG = rg_lam.shape[1]
    H = ml_b_if.shape[1] // 2
    DH = ML // H
    TAPS = rg_conv_w.shape[1]
    FD = ffn_w_gate.shape[2]
    E = moe_w_router.shape[2]
    FE = moe_w_gate.shape[3]
    TT = S // P
    KD = D // P
    KR = RG // P
    GB = rg_w_a.shape[2]
    CONV_PAD = TAPS - 1
    assert (LAYERS, TT, KD, KR, H, DH, E) == (2, 2, 8, 4, 4, P, 8)

    COLS = UNIT // KD
    MIX_UNITS = (4 * ML + 2 * RG) // COLS
    OUT_UNITS = D * D // (P * UNIT)
    FFN_STEPS = FD // COLS
    MIX0 = 0
    FFN0 = MIX0 + MIX_UNITS + OUT_UNITS
    MIX1 = FFN0 + 3 * FFN_STEPS
    MOE0 = MIX1 + MIX_UNITS + OUT_UNITS
    FB = FE // BANK
    ITEM_UNITS = 6 * FB
    OVER = E
    assert MIX_UNITS == 12 and OUT_UNITS == 4 and FFN_STEPS % 2 == 1 and ITEM_UNITS % RAW == 0

    with ExitStack() as ctx:
        def sb(name, shape, dt=F32):
            return ctx.enter_context(nc.sbuf_tensor(name, shape, dt))

        def sem(name):
            return ctx.enter_context(nc.semaphore(name))

        raw = [sb(f"raw{i}", [P, UNIT]) for i in range(RAW)]
        w_hi = [sb(f"w_hi{i}", [P, UNIT], F32R) for i in range(SPLIT)]
        w_lo = [sb(f"w_lo{i}", [P, UNIT], F32R) for i in range(SPLIT)]
        resid = sb("resid", [P, TT, D])
        xn = sb("xn", [P, TT, D])
        u_hi = sb("u_hi", [P, KD, S], F32R)
        u_lo = sb("u_lo", [P, KD, S], F32R)
        hid_hi = sb("hid_hi", [P, 2, BANK], F32R)
        hid_lo = sb("hid_lo", [P, 2, BANK], F32R)
        y_hi = sb("y_hi", [P, D], F32R)
        y_lo = sb("y_lo", [P, D], F32R)
        slotT = sb("slotT", [P, TT, P], F32R)
        small_hi = sb("small_hi", [P, 3, KD * E], F32R)
        small_lo = sb("small_lo", [P, 3, KD * E], F32R)
        small_raw = sb("small_raw", [P, 3, KD * E])
        ident = sb("ident", [P, P])
        tri = sb("tri", [P, P])
        ones = sb("ones", [P, P])
        last = sb("last", [P, P])
        acausal = sb("acausal", [P, P])
        iota = sb("iota", [P, P])
        block_a = sb("block_a", [P, KR, P])
        block_x = sb("block_x", [P, KR, P])
        gain_row = sb("gain_row", [P, D])
        if_bias = sb("if_bias", [P, LAYERS, 2 * H])
        arena = [sb(f"arena{i}", [P, 1024]) for i in range(10)]
        x_pad = sb("x_pad", [P, KR, S + CONV_PAD])
        PR = 2 * KD + (TAPS + 5) * KR
        pcol = sb("pcol", [P, LAYERS, PR])
        sml = sb("sml", [P, 512])

        qT, kT, v_tok, sig_o, w_dec, decT, num_s, kwc, r_g, i_g = arena
        c4 = lambda t: t[:, :].rearrange("p (c h s) -> p c h s", c=TT, h=H)
        hv = lambda t: t.rearrange("p (h s) -> p h s", h=H)
        rv = lambda t: t[:, :].rearrange("p (k s) -> p k s", k=KR)
        hv4 = lambda bank: bank.rearrange("p (h s) -> p h s", h=H)
        num_s_half = lambda c: num_s[:, c * BANK:(c + 1) * BANK]
        kw_tok = kwc[:, 0:BANK].rearrange("p (h s) -> p h s", h=H)
        c_st = kwc[:, BANK:2 * BANK].rearrange("p (h s) -> p h s", h=H)
        xc = xn[:, 0, :].rearrange("p (k s) -> p k s", k=KR)
        gate_g = xn[:, 1, :].rearrange("p (k s) -> p k s", k=KR)
        silu_s = qT[:, :].rearrange("p (b n) -> p b n", b=2)
        hid = kT[:, :].rearrange("p (b n) -> p b n", b=2)
        slot1h = v_tok[:, 0:TT * P].rearrange("p (t s) -> p t s", t=TT)
        prow = num_s[:, 0:P]

        _at = [0]

        def cols(n):
            _at[0] += n
            assert _at[0] <= 512
            return sml[:, _at[0] - n:_at[0]]

        ssq, std, rstd = cols(TT), cols(TT), cols(TT)
        z_if = cols(TT * 2 * H).rearrange("p (c n) -> p c n", c=TT)
        nabs, e_f, ls_a, ls_b, ls_c = (cols(TT * H) for _ in range(5))
        log_f, b_cum, r_in, cmax, m_run = (cols(TT * H) for _ in range(5))
        sel_in = cols(2 * H)
        sel_out = cols(2 * H)
        m_prev = cols(H)
        exp_in, exp_out = cols(4 * H), cols(4 * H)
        den, n_st = cols(TT * H), cols(H)
        qn = cols(H)
        hsq, hstd, hrstd = cols(TT * H), cols(TT * H), cols(TT * H)
        rstd_rg, std_rg = cols(TT), cols(TT)
        lam_n, lam_e, lam_a, lam_b, lam_c, decay = (cols(KR) for _ in range(6))
        nb_a, nb_x = cols(KR), cols(KR)
        eps_c = cols(1)
        logit = cols(TT * E).rearrange("p (t e) -> p t e", t=TT)
        top8 = cols(TT * E).rearrange("p (t e) -> p t e", t=TT)
        topf = cols(TT * E).rearrange("p (t e) -> p t e", t=TT)
        gdiff, gexp, gw1, gw2 = cols(TT), cols(TT), cols(TT), cols(TT)
        hot1 = cols(TT * E).rearrange("p (t e) -> p t e", t=TT)
        hot2 = cols(TT * E).rearrange("p (t e) -> p t e", t=TT)
        chosen = cols(TT * E).rearrange("p (t e) -> p t e", t=TT)
        gate2 = cols(TT * 2 * E).rearrange("p (t q) -> p t q", t=TT)
        slot_of = cols(TT * 2 * E).rearrange("p (t q) -> p t q", t=TT)
        cnt, ov, ovc, zero8 = cols(E), cols(E), cols(E), cols(E)
        tabf = cols(32)
        topi = sb("topi", [P, TT, E], U32)
        tab = sb("tab", [1, 32], I32)
        ovm = sb("ovm", [1, E, E])
        TAB_N, TAB_E = 25, 17

        def pc(l, name, k=0):
            first = dict(mix=0, ffn=KD, conv=2 * KD)
            for i, n in enumerate(("conv_b", "b_a", "b_x", "lam", "rgn")):
                first[n] = 2 * KD + (TAPS + i) * KR
            return pcol[:, l, first[name] + k:first[name] + k + 1]

        def pcs(l, name):
            i = ("conv_b", "b_a", "b_x", "lam", "rgn").index(name)
            a = 2 * KD + (TAPS + i) * KR
            return pcol[:, l, a:a + KR]

        ps = ctx.enter_context(nc.psum_tensor("ps", [P, 8, BANK], F32))
        SM = 2

        loaded = [sem(f"unit_loaded{i}") for i in range(RAW)]
        hi_done, lo_done = sem("unit_hi_done"), sem("unit_lo_done")
        used = sem("unit_used")
        x_loaded, rows_loaded, small_loaded = sem("x_loaded"), sem("rows_loaded"), sem("small_loaded")
        block_loaded, final_loaded = sem("block_loaded"), sem("final_gain_loaded")
        consts_s, rows_zero, block_zero = sem("consts"), sem("rows_zero"), sem("block_zero")
        pool_own, dve_own, act_own = (Counted(sem(n)) for n in ("pool_own", "dve_own", "act_own"))
        rows_T, pcol_s = sem("rows_transposed"), sem("pcol_ready")
        small_hi_s, small_lo_s = sem("small_hi_s"), sem("small_lo_s")
        resid_ready, std_ready, xn_ready = sem("resid_ready"), sem("std_ready"), sem("xn_ready")
        xT_ps, u_hi_s, u_lo_s = sem("xT_in_psum"), sem("u_hi_s"), sem("u_lo_s")
        proj_out = sem("projection_evacuated")
        gates_ps, nabs_s, ef_s, logf_s = sem("gates_ps"), sem("nabs_s"), sem("exp_f_s"), sem("log_f_s")
        cum_ps, diag_s, r_ps = sem("cumsum_ps"), sem("diag_s"), sem("r_ps")
        qk_ps, sel_s, sel_ps, kt_ps = sem("qk_ps"), sem("chunk_end_s"), sem("chunk_end_ps"), sem("k_tok_ps")
        expin_s, expout_s = sem("exp_in_s"), sem("exp_out_s")
        wm_s, wexp_s, dec_s = sem("decay_log_s"), sem("decay_exp_s"), sem("decay_qk_s")
        dt_ps, decT_s, kw_s, c_ps, c_s = sem("decT_ps"), sem("decT_s"), sem("kw_s"), sem("c_ps"), sem("c_s")
        num_ps, inter_ps = sem("num_ps"), sem("inter_ps")
        hsq_s, hstd_s, yml_s, yT_ps, yT_hi, yT_lo = (sem("head_sq_s"), sem("head_std_s"), sem("y_ml_s"),
                                                     sem("y_ml_T_ps"), sem("y_ml_T_hi"), sem("y_ml_T_lo"))
        lamn_s, lame_s, conv_s = sem("lam_neg_s"), sem("lam_exp_s"), sem("conv_s")
        ga_ps, ga_read, gx_ps, gx_read = sem("rg_a_ps"), sem("rg_a_read"), sem("rg_x_ps"), sem("rg_x_read")
        rsig_s, tanh_s, sqrt_in, sqrt_out = sem("r_gate_s"), sem("tanh_s"), sem("sqrt_in"), sem("sqrt_out")
        gelu_in, gelu_exp = sem("gelu_in"), sem("gelu_exp")
        ysq_s, ssq_ps, rgstd_s = sem("y_rg_sq_s"), sem("y_rg_ssq_ps"), sem("rg_std_s")
        yrg_s, yr_hi, yr_lo = sem("y_rg_s"), sem("y_rg_hi"), sem("y_rg_lo")
        silu_done, hid_s, hT_hi, hT_lo = sem("silu_done"), sem("hidden_s"), sem("hidden_hi"), sem("hidden_lo")
        logit_ps, gdiff_s, gexp_s, chosen_s = sem("logit_ps"), sem("gate_diff_s"), sem("gate_exp_s"), sem("chosen_s")
        pos_ps, tab_s, slots_s, moe_zero = sem("pos_ps"), sem("table_ready"), sem("slots_ready"), sem("moe_zero")
        mhT_ps, msilu, mhid, mhT_hi, mhT_lo = (sem("moe_hT_ps"), sem("moe_silu"), sem("moe_hid"),
                                               sem("moe_hT_hi"), sem("moe_hT_lo"))
        gat_ps, g_hi, g_lo = sem("gather_ps"), sem("gather_hi"), sem("gather_lo")
        sT_ps, sT_s, yh_s, yl_s = sem("slotT_ps"), sem("slotT_s"), sem("y_hi_s"), sem("y_lo_s")
        sc_ps, sc_add = sem("scatter_ps"), sem("scatter_added")
        fin_s, out_s = sem("final_ready"), sem("out_stored")

        x_v = x[0].rearrange("(t p) d -> p t d", p=P)
        out_v = out[0].rearrange("(t p) d -> p t d", p=P)
        deep = lambda w: w.rearrange("(k p) n -> p k n", p=P)

        def mix_cols(l, j):
            starts = [0, ML, 4 * ML + 2 * H, 2 * ML, 4 * ML + 2 * H + RG, 3 * ML]
            if j < MIX_UNITS:
                c = starts[j // 2] + COLS * (j % 2)
                return deep(w_in[l])[:, :, c:c + COLS]
            r = (j - MIX_UNITS) * 2
            return deep(w_out[l])[:, r:r + 2, :]

        unit3 = lambda t, k: t[:, :].rearrange("p (k n) -> p k n", k=k)

        block = ctx.enter_context(nc.Block())

        @block.sync
        def _(sp):
            def load(n, src, k, extra=0):
                if n >= RAW:
                    sp.wait_ge(lo_done, extra + (n - RAW + 1))
                sp.dma_start(unit3(raw[n % RAW], k), src).then_inc(loaded[n % RAW], 16)

            def mixer(l, base, first=0):
                for j in range(first, MIX_UNITS + OUT_UNITS):
                    load(base + j, mix_cols(l, j), KD if j < MIX_UNITS else 2)

            def blocks(l):
                for h in range(2):
                    for w, t in ((rg_w_a, block_a), (rg_w_x, block_x)):
                        sp.dma_start(t[GB * h:GB * h + GB, :, GB * h:GB * h + GB],
                                     w[l].rearrange("(k h) i j -> h i k j", h=2)[h]).then_inc(block_loaded, 16)

            sp.dma_start(resid[:, :, :], x_v).then_inc(x_loaded, 16)
            sp.wait_ge(rows_zero, 1)
            for l in range(LAYERS):
                r = l * PR
                for src, n in ((norm_mix_g[l], KD), (norm_ffn_g[l], KD), (rg_conv_w[l].rearrange("j c -> (j c)"), TAPS * KR),
                               (rg_conv_b[l], KR), (rg_b_a[l], KR), (rg_b_x[l], KR), (rg_lam[l], KR), (rg_norm_g[l], KR)):
                    sp.dma_start(prow[r:r + n, :], src.rearrange("(k p) -> k p", p=P)).then_inc(rows_loaded, 16)
                    r += n
            for j in range(2):
                load(j, mix_cols(0, j), KD)
            for l in range(LAYERS):
                c = 4 * ML
                sp.dma_start(small_raw[:, l, :].rearrange("p (k n) -> p k n", k=KD),
                             deep(w_in[l])[:, :, c:c + 2 * H]).then_inc(small_loaded, 16)
            sp.dma_start(small_raw[:, 2, :].rearrange("p (k n) -> p k n", k=KD),
                         deep(moe_w_router[0])).then_inc(small_loaded, 16)
            for l in range(LAYERS):
                sp.dma_start(if_bias[:, l, :], ml_b_if[l].partition_broadcast(P)).then_inc(small_loaded, 16)
                sp.dma_start(gain_row[:, l * ML:(l + 1) * ML], ml_norm_g[l].partition_broadcast(P)).then_inc(small_loaded, 16)
            sp.wait_ge(block_zero, 2)
            blocks(0)
            mixer(0, MIX0, 2)

            gate_v, up_v, down_v = deep(ffn_w_gate[0]), deep(ffn_w_up[0]), deep(ffn_w_down[0])
            load(FFN0, gate_v[:, :, 0:COLS], KD)
            load(FFN0 + 1, up_v[:, :, 0:COLS], KD)
            with sp.Fori(0, FFN_STEPS // 2) as it:
                for a in range(2):
                    n, i = FFN0 + 2 + 3 * a, it * 2 + (1 + a)
                    load(n, gate_v[:, :, bass.ds(i * COLS, COLS)], KD, it * 6)
                    load(n + 1, up_v[:, :, bass.ds(i * COLS, COLS)], KD, it * 6)
                    load(n + 2, down_v[:, bass.ds(it * 4 + 2 * a, 2), :], 2, it * 6)
            load(MIX1 - 1, down_v[:, 2 * FFN_STEPS - 2:2 * FFN_STEPS, :], 2)

            sp.wait_ge(gx_ps, 1)
            blocks(1)
            mixer(1, MIX1)
            sp.wait_ge(yml_s, LAYERS)
            sp.dma_start(gain_row[:, :], norm_final_g.partition_broadcast(P)).then_inc(final_loaded, 16)

            half = KD // 2

            def expert_units(e, extra):
                g_v = moe_w_gate[0].rearrange("e (k p) n -> p e k n", p=P)
                u_v = moe_w_up[0].rearrange("e (k p) n -> p e k n", p=P)
                d_v = moe_w_down[0].rearrange("e (k p) n -> p e k n", p=P)

                def gate_up(n, i, extra):
                    for m, v in enumerate((g_v, u_v)):
                        for a in range(2):
                            load(n + 2 * m + a, v[:, bass.ds(e, 1), half * a:half * a + half, bass.ds(i * BANK, BANK)]
                                 .rearrange("p e k n -> p (e k) n"), half, extra)

                def down(n, i, extra):
                    for a in range(2):
                        load(n + a, d_v[:, bass.ds(e, 1), bass.ds(i * 4 + 2 * a, 2), :]
                             .rearrange("p e k n -> p (e k) n"), 2, extra)

                gate_up(MOE0, 0, extra)
                with sp.Fori(1, FB) as i:
                    gate_up(MOE0 + 4, i, extra + (i - 1) * 6)
                    down(MOE0 + 8, i - 1, extra + (i - 1) * 6)
                down(MOE0 + ITEM_UNITS - 2, FB - 1, extra)

            with sp.Fori(0, E) as j:
                expert_units(j, j * ITEM_UNITS)
            sp.wait_ge(tab_s, 1)
            n_over = sp.value_load(tab[0:1, TAB_N:TAB_N + 1], min_val=0, max_val=E)
            with sp.If(n_over > 0):
                with sp.Fori(0, n_over) as j:
                    e = sp.value_load(tab[0:1, bass.ds(j + TAB_E, 1)], min_val=0, max_val=E - 1)
                    expert_units(e, j * ITEM_UNITS + E * ITEM_UNITS)
            for a in range(2):
                load(MOE0 + a, deep(moe_w_gate[0, 0])[:, 0:half, 0:BANK], half, (n_over + E) * ITEM_UNITS)
            sp.wait_ge(fin_s, 2)
            for t in range(TT):
                sp.dma_start(out_v[:, t, :], xn[:, t, :]).then_inc(out_s, 16)
            sp.wait_ge(out_s, 16 * TT)

        @block.gpsimd
        def _(pool):
            g = nc.gpsimd
            g.memset(prow, 0.0).then_inc(rows_zero, 1)
            g.memset(block_a[:, :, :], 0.0).then_inc(block_zero, 1)
            g.memset(block_x[:, :, :], 0.0).then_inc(block_zero, 1)
            g.memset(ident[:, :], 0.0)
            g.memset(tri[:, :], 1.0)
            g.memset(ones[:, :], 1.0)
            g.memset(last[:, :], 0.0)
            g.memset(eps_c, EPS)
            g.memset(zero8, 0.0)
            g.memset(x_pad[:, :, 0:CONV_PAD], 0.0)
            pool_own.after(pool, g.memset(acausal[:, :], 0.0))
            sel = lambda t, **kw: g.affine_select(out=t[:, :], in_=t[:, :], **kw)
            sel(ident, compare_op=ALU.not_equal, fill=1.0, base=0, pattern=[[-1, P]], channel_multiplier=1)
            sel(tri, compare_op=ALU.is_ge, fill=0.0, base=0, pattern=[[1, P]], channel_multiplier=-1)
            sel(last, compare_op=ALU.not_equal, fill=1.0, base=1 - P, pattern=[[0, P]], channel_multiplier=1)
            sel(acausal, compare_op=ALU.is_ge, fill=NEG, base=0, pattern=[[-1, P]], channel_multiplier=1)
            g.iota(iota[:, :], pattern=[[1, P]], base=0, channel_multiplier=0,
                   allow_small_or_imprecise_dtypes=True).then_inc(consts_s, 1)
            for l in range(LAYERS):
                pool.wait_ge(proj_out, l * MIX_UNITS + 10)
                gi = rv(kT)
                pool_own.after(pool, g.tensor_tensor(gi, gate_g, gate_g, ALU.mult))
                pool_own.after(pool, g.tensor_scalar(gi, gi, 0.044715, 1.0, ALU.mult, ALU.add))
                g.tensor_tensor(gi, gi, gate_g, ALU.mult).then_inc(gelu_in, 1)

        @block.scalar
        def _(act):
            a = nc.scalar

            def hi(n, extra=0, turns=0):
                act.wait_ge(loaded[n % RAW], turns * 16 + 16 * (n // RAW + 1))
                if n >= SPLIT:
                    act.wait_ge(used, extra + (n - SPLIT + 1))
                a.copy(w_hi[n % SPLIT][:, :], raw[n % RAW][:, :]).then_inc(hi_done, 1)

            def norm_std(m):
                if m == 0:
                    act.wait_ge(x_loaded, 16)
                    act.wait_ge(consts_s, 1)
                else:
                    act.wait_ge(resid_ready, m)
                for t in range(TT):
                    ins = a.activation(xn[:, t, :], resid[:, t, :], ACT.Square, accum_out=ssq[:, t:t + 1])
                act_own.after(act, ins)
                a.activation(std, ssq, ACT.Sqrt, bias=eps_c, scale=1.0 / D).then_inc(std_ready, 1)

            def norm_hi(m, l, which):
                act.wait_ge(pcol_s, 1)
                for b in range(4):
                    act.wait_ge(xT_ps, 4 * m + b + 1)
                    for k in (2 * b, 2 * b + 1):
                        ins = a.activation(u_hi[:, k, :], ps[:, 4 + b, (k % 2) * S:(k % 2) * S + S], ACT.Copy,
                                           scale=pc(l, which, k))
                    ins.then_inc(u_hi_s, 1)

            def mixer(l, base):
                if l == 0:
                    hi(base)
                    hi(base + 1)
                    hi(base + 2)
                else:
                    hi(base + 1)
                    hi(base + 2)
                norm_std(2 * l)
                norm_hi(2 * l, l, "mix")
                act.wait_ge(nabs_s, l + 1)
                a.activation(e_f, nabs, ACT.Exp).then_inc(ef_s, 1)
                act.wait_ge(lamn_s, l + 1)
                a.activation(lam_e, lam_n, ACT.Exp).then_inc(lame_s, 1)

                def evac(j):
                    act.wait_ge(used, base + j + 1)
                    bank, part = ps[:, j % 2, :], j // 2
                    if part in (0, 1):
                        t = (qT, kT)[part]
                        ins = a.copy(t[:, (j % 2) * BANK:(j % 2) * BANK + BANK], bank)
                    elif part == 2:
                        ins = a.copy(x_pad[:, 2 * (j % 2):2 * (j % 2) + 2, CONV_PAD:], bank.rearrange("p (k s) -> p k s", k=2))
                    elif part == 3:
                        ins = a.copy(v_tok[:, :].rearrange("p (c n) -> p c n", c=TT)[:, :, (j % 2) * COLS:(j % 2) * COLS + COLS],
                                     bank.rearrange("p (c n) -> p c n", c=TT))
                    elif part == 4:
                        ins = a.copy(gate_g[:, 2 * (j % 2):2 * (j % 2) + 2, :], bank.rearrange("p (k s) -> p k s", k=2))
                    else:
                        ins = a.activation(sig_o[:, :].rearrange("p (c n) -> p c n", c=TT)[:, :, (j % 2) * COLS:(j % 2) * COLS + COLS],
                                           bank.rearrange("p (c n) -> p c n", c=TT), ACT.Exp, scale=-1.0)
                    ins.then_inc(proj_out, 1)

                for j in range(9):
                    hi(base + j + 3)
                    evac(j)
                    if j == 6:
                        act.wait_ge(expin_s, l + 1)
                        a.activation(exp_out, exp_in, ACT.Exp).then_inc(expout_s, 1)
                        act.wait_ge(wm_s, l + 1)
                        a.activation(w_dec[:, :], w_dec[:, :], ACT.Exp).then_inc(wexp_s, 1)
                    if j == 7:
                        for c in range(TT):
                            act.wait_ge(dt_ps, 2 * l + c + 1)
                            ins = a.copy(decT[:, c * BANK:(c + 1) * BANK], ps[:, 4 + c, :])
                        ins.then_inc(decT_s, 1)
                        act.wait_ge(c_ps, l + 1)
                        a.copy(c_st, ps[:, 3, :].rearrange("p (h s) -> p h s", h=H))
                        a.copy(n_st, ps[:, SM, 32:32 + H]).then_inc(c_s, 1)
                act.wait_ge(ga_ps, l + 1)
                for k in range(KR):
                    ins = a.activation(rv(r_g)[:, k, :], ps[:, 3 + 2 * (k // 2), (k % 2) * S:(k % 2) * S + S], ACT.Exp,
                                       bias=nb_a[:, k:k + 1], scale=-1.0)
                ins.then_inc(ga_read, 1)
                hi(base + 12)
                evac(9)
                act.wait_ge(gx_ps, l + 1)
                for k in range(KR):
                    ins = a.activation(rv(i_g)[:, k, :], ps[:, 3 + 2 * (k // 2), (k % 2) * S:(k % 2) * S + S], ACT.Exp,
                                       bias=nb_x[:, k:k + 1], scale=-1.0)
                ins.then_inc(gx_read, 1)
                hi(base + 13)
                act.wait_ge(rsig_s, l + 1)
                for k in range(KR):
                    a.activation(x_pad[:, k, CONV_PAD:], rv(r_g)[:, k, :], ACT.Tanh, scale=decay[:, k:k + 1])
                for k in range(KR):
                    ins = a.activation(rv(qT)[:, k, :], rv(r_g)[:, k, :], ACT.Exp, scale=lam_c[:, k:k + 1])
                ins.then_inc(tanh_s, 1)
                act.wait_ge(gelu_in, l + 1)
                a.activation(rv(kT), rv(kT), ACT.Exp, scale=-2.0 * GELU_C).then_inc(gelu_exp, 1)
                evac(10)
                hi(base + 14)
                evac(11)
                act.wait_ge(hsq_s, l + 1)
                a.activation(hstd, hsq, ACT.Sqrt, bias=eps_c, scale=1.0 / DH).then_inc(hstd_s, 1)
                act.wait_ge(sqrt_in, l + 1)
                a.activation(rv(r_g), rv(r_g), ACT.Sqrt, scale=2.0).then_inc(sqrt_out, 1)
                for b in range(2):
                    act.wait_ge(yT_ps, 2 * l + b + 1)
                    a.copy(u_hi[:, 2 * b:2 * b + 2, :], ps[:, b, :].rearrange("p (k s) -> p k s", k=2)).then_inc(yT_hi, 1)
                hi(base + 15)
                act.wait_ge(yrg_s, l + 1)
                a.copy(u_hi[:, 4:8, :], rv(i_g)).then_inc(yr_hi, 1)
                act.wait_ge(ssq_ps, l + 1)
                a.activation(std_rg, ps[:, SM, 48:48 + TT], ACT.Sqrt, bias=eps_c, scale=1.0 / RG).then_inc(rgstd_s, 1)

            act.wait_ge(small_loaded, 16 * (3 + 2 * LAYERS))
            a.copy(small_hi[:, :, :], small_raw[:, :, :]).then_inc(small_hi_s, 1)
            mixer(0, MIX0)

            hi(FFN0)
            hi(FFN0 + 1)
            norm_std(1)
            norm_hi(1, 0, "ffn")

            def ffn_step(n, par, i, extra, turns, has_down):
                if has_down:
                    hi(n + 2, extra, turns)
                act.wait_ge(used, extra + n + 1)
                if has_down:
                    act.wait_ge(hid_s, i - 1)
                a.activation(silu_s[:, par, :], ps[:, par, :], ACT.Silu).then_inc(silu_done, 1)
                nxt = n + (3 if has_down else 2)
                hi(nxt, extra, turns)
                act.wait_ge(hid_s, i + 1)
                if has_down:
                    act.wait_ge(used, extra + n)
                a.copy(hid_hi[:, par, :], hid[:, par, :]).then_inc(hT_hi, 1)
                hi(nxt + 1, extra, turns)

            ffn_step(FFN0, 0, 0, 0, 0, False)
            with act.Fori(0, FFN_STEPS // 2) as it:
                for b in range(2):
                    ffn_step(FFN0 + 2 + 3 * b, (1 + b) % 2, it * 2 + (1 + b), it * 6, it, True)

            mixer(1, MIX1)
            hi(MOE0)
            hi(MOE0 + 1)
            norm_std(3)
            norm_hi(3, 1, "ffn")
            act.wait_ge(gdiff_s, 1)
            a.activation(gexp, gdiff, ACT.Exp).then_inc(gexp_s, 1)

            def gather_hi(count):
                for b in range(2):
                    act.wait_ge(gat_ps, count * 2 + (b + 1))
                    for k in range(4 * b, 4 * b + 4):
                        ins = a.activation(u_hi[:, k, 0:P], ps[:, 5 + b, (k % 4) * P:(k % 4) * P + P], ACT.Copy,
                                           scale=pc(1, "ffn", k))
                    ins.then_inc(g_hi, 1)

            act.wait_ge(tab_s, 1)
            n_over = act.value_load(tab[0:1, TAB_N:TAB_N + 1], min_val=0, max_val=E)
            gather_hi(0)
            with act.Fori(0, n_over + E) as j:
                ju, jt = j * ITEM_UNITS, j * (ITEM_UNITS // RAW)

                def silu(n, k, extra=0):
                    act.wait_ge(used, ju + extra + (n + 1))
                    act.wait_ge(mhid, j * FB + k)
                    a.activation(silu_s[:, 0, :], ps[:, 0, :], ACT.Silu).then_inc(msilu, 1)

                def hT(k):
                    act.wait_ge(mhT_ps, j * FB + k + 1)
                    a.copy(hid_hi[:, 0, :], ps[:, 2, :]).then_inc(mhT_hi, 1)

                h = lambda n, extra=0, turns=0: hi(MOE0 + n, ju + extra, jt + turns)
                h(2)
                h(3)
                h(4)
                silu(MOE0 + 1, 0)
                h(5)
                h(6)
                h(7)
                hT(0)
                h(8)
                silu(MOE0 + 5, 1)
                h(9)
                act.wait_ge(sT_ps, j + 1)
                a.copy(slotT[:, :, :], ps[:, 7, 0:TT * P].rearrange("p (t s) -> p t s", t=TT)).then_inc(sT_s, 1)
                h(10)
                h(11)
                with act.Fori(2, FB) as i:
                    x6, t1 = (i - 2) * 6, i - 2
                    h(12, x6, t1)
                    h(13, x6, t1)
                    hT(i - 1)
                    h(14, x6, t1)
                    silu(MOE0 + 11, i, x6)
                    h(15, x6, t1)
                    h(16, x6, t1)
                    h(17, x6, t1)
                gather_hi(j + 1)
                hT(FB - 1)
                h(42)
                h(43)
                for b in range(2):
                    act.wait_ge(used, ju + (MOE0 + ITEM_UNITS))
                    a.copy(y_hi[:, b * BANK:(b + 1) * BANK], ps[:, 3 + b, :]).then_inc(yh_s, 1)
            act.wait_ge(sc_add, (n_over + (E + 1)) * 4)
            for t in range(TT):
                ins = a.activation(xn[:, t, :], resid[:, t, :], ACT.Square, accum_out=ssq[:, t:t + 1])
            act_own.after(act, ins)
            a.activation(std, ssq, ACT.Sqrt, bias=eps_c, scale=1.0 / D).then_inc(std_ready, 1)

        @block.vector
        def _(dve):
            v = nc.vector
            own = lambda ins: dve_own.after(dve, ins)
            bc = lambda ap, axis, shape: ap.unsqueeze(axis).broadcast_to(shape)

            def lo(n, extra=0):
                dve.wait_ge(hi_done, extra + (n + 1))
                v.tensor_tensor(w_lo[n % SPLIT][:, :], raw[n % RAW][:, :], w_hi[n % SPLIT][:, :].bitcast(F32),
                                ALU.subtract).then_inc(lo_done, 1)

            def norm(m, l, which):
                dve.wait_ge(std_ready, m + 1)
                own(v.reciprocal(rstd, std))
                for t in range(TT):
                    ins = v.tensor_scalar(xn[:, t, :], resid[:, t, :], rstd[:, t:t + 1], None, ALU.mult)
                ins.then_inc(xn_ready, 1)
                for b in range(4):
                    dve.wait_ge(u_hi_s, 4 * m + b + 1)
                    for k in (2 * b, 2 * b + 1):
                        ins = v.scalar_tensor_tensor(u_lo[:, k, :], ps[:, 4 + b, (k % 2) * S:(k % 2) * S + S],
                                                     pc(l, which, k), u_hi[:, k, :].bitcast(F32), ALU.mult, ALU.subtract)
                    ins.then_inc(u_lo_s, 1)

            def log1p(z, s_, s2, p):
                own(v.tensor_scalar(s_, z, 2.0, None, ALU.add))
                own(v.reciprocal(s_, s_))
                own(v.tensor_tensor(s_, z, s_, ALU.mult))
                own(v.tensor_tensor(s2, s_, s_, ALU.mult))
                own(v.tensor_scalar(p, s2, 1.0 / 15, None, ALU.mult))
                for n in (13, 11, 9, 7, 5, 3):
                    own(v.scalar_tensor_tensor(p, p, 1.0 / n, s2, ALU.add, ALU.mult))
                own(v.scalar_tensor_tensor(p, p, 1.0, s_, ALU.add, ALU.mult))

            def mixer(l, base):
                if l == 0:
                    lo(base)
                lo(base + 1)
                lo(base + 2)
                norm(2 * l, l, "mix")
                dve.wait_ge(gates_ps, l + 1)
                own(v.tensor_tensor(z_if, ps[:, SM, 0:TT * 2 * H].rearrange("p (c n) -> p c n", c=TT),
                                    bc(if_bias[:, l, :], 1, [P, TT, 2 * H]), ALU.add))
                ig, fg = z_if[:, :, 0:H], z_if[:, :, H:2 * H]
                c2 = lambda t: t.rearrange("p (c h) -> p c h", c=TT)
                v.scalar_tensor_tensor(c2(nabs), fg, -1.0, fg, ALU.mult, ALU.min).then_inc(nabs_s, 1)
                v.scalar_tensor_tensor(lam_n, pcs(l, "lam"), -1.0, pcs(l, "lam"), ALU.mult, ALU.min).then_inc(lamn_s, 1)
                v.tensor_scalar(nb_a, pcs(l, "b_a"), -1.0, None, ALU.mult)
                v.tensor_scalar(nb_x, pcs(l, "b_x"), -1.0, None, ALU.mult)
                dve.wait_ge(ef_s, l + 1)
                log1p(e_f, ls_a, ls_b, ls_c)
                own(v.tensor_scalar(c2(ls_a), fg, 0.0, None, ALU.min))
                v.scalar_tensor_tensor(log_f, ls_c, -2.0, ls_a, ALU.mult, ALU.add).then_inc(logf_s, 1)
                lo(base + 3)
                dve.wait_ge(lame_s, l + 1)
                log1p(lam_e, lam_a, lam_b, decay)
                own(v.tensor_scalar(lam_a, pcs(l, "lam"), -1.0, 0.0, ALU.mult, ALU.max))
                own(v.scalar_tensor_tensor(lam_b, decay, 2.0, lam_a, ALU.mult, ALU.add))
                v.tensor_scalar(decay, lam_b, 8.0, None, ALU.mult)
                v.tensor_scalar(lam_c, lam_b, -8.0, None, ALU.mult)
                lo(base + 4)
                lo(base + 5)
                dve.wait_ge(cum_ps, l + 1)
                own(v.tensor_copy(b_cum, ps[:, SM, 16:16 + TT * H]))
                own(v.tensor_tensor(c2(r_in), ig, c2(b_cum), ALU.subtract))
                v.tensor_tensor(decT[:, :].rearrange("p (n s) -> p n s", s=P), bc(ident[:, :], 1, [P, TT * H, P]),
                                bc(r_in, 2, [P, TT * H, P]), ALU.mult).then_inc(diag_s, 1)
                lo(base + 6)
                lo(base + 7)
                dve.wait_ge(r_ps, l + 1)
                for c in range(TT):
                    ins = v.tensor_tensor(c4(w_dec)[:, c], hv4(ps[:, 4 + c, :]), bc(acausal[:, :], 1, [P, H, P]), ALU.add)
                own(ins)
                own(v.tensor_reduce(cmax, w_dec[:, :].rearrange("p (n s) -> p n s", s=P), AX.X, ALU.max))
                own(v.tensor_scalar(m_run[:, 0:H], cmax[:, 0:H], 0.0, None, ALU.max))
                v.tensor_copy(sel_in[:, 0:H], m_run[:, 0:H])
                v.tensor_copy(sel_in[:, H:2 * H], b_cum[:, 0:H]).then_inc(sel_s, 1)
                lo(base + 8)
                dve.wait_ge(sel_ps, l + 1)
                own(v.tensor_copy(sel_out, ps[:, SM, 24:24 + 2 * H]))
                own(v.tensor_tensor(m_prev, sel_out[:, 0:H], sel_out[:, H:2 * H], ALU.add))
                own(v.tensor_tensor(m_run[:, H:2 * H], cmax[:, H:2 * H], m_prev, ALU.max))
                v.tensor_tensor(exp_in[:, 0:H], r_in[:, 0:H], sel_out[:, 0:H], ALU.subtract)
                v.tensor_tensor(exp_in[:, H:2 * H], m_prev, m_run[:, H:2 * H], ALU.subtract)
                v.scalar_tensor_tensor(exp_in[:, 2 * H:4 * H], b_cum, -1.0, m_run, ALU.mult,
                                       ALU.subtract).then_inc(expin_s, 1)
                v.tensor_tensor(w_dec[:, :].rearrange("p (n s) -> p n s", s=P), w_dec[:, :].rearrange("p (n s) -> p n s", s=P),
                                bc(m_run, 2, [P, TT * H, P]), ALU.subtract).then_inc(wm_s, 1)
                dve.wait_ge(proj_out, l * MIX_UNITS + 6)
                for j in range(TAPS):
                    for k in range(KR):
                        row = x_pad[:, k, j:j + S]
                        tap = pc(l, "conv", j * KR + k)
                        if j == 0:
                            ins = v.tensor_scalar(xc[:, k, :], row, tap, pc(l, "conv_b", k), ALU.mult, ALU.add)
                        else:
                            ins = v.scalar_tensor_tensor(xc[:, k, :], row, tap, xc[:, k, :], ALU.mult, ALU.add)
                    if j < TAPS - 1:
                        own(ins)
                ins.then_inc(conv_s, 1)
                lo(base + 9)
                dve.wait_ge(wexp_s, l + 1)
                dve.wait_ge(qk_ps, l + 1)
                for c in range(TT):
                    w = w_dec[:, c * BANK:(c + 1) * BANK]
                    ins = v.scalar_tensor_tensor(w, ps[:, 6 + c, :], float(DH) ** -0.5, w, ALU.mult, ALU.mult)
                ins.then_inc(dec_s, 1)
                dve.wait_ge(dec_s, l + 1)
                own(v.tensor_reduce(den, w_dec[:, :].rearrange("p (n s) -> p n s", s=P), AX.X, ALU.add))
                dve.wait_ge(kt_ps, l + 1)
                dve.wait_ge(expout_s, l + 1)
                own(v.tensor_scalar(exp_out[:, 0:H], exp_out[:, 0:H], float(DH) ** -0.5, None, ALU.mult))
                v.tensor_tensor(kw_tok, hv4(ps[:, 3, :]), bc(exp_out[:, 0:H], 2, [P, H, P]), ALU.mult).then_inc(kw_s, 1)
                lo(base + 10)
                lo(base + 11)
                dve.wait_ge(inter_ps, l + 1)
                isc = exp_out[:, H:2 * H]
                v.tensor_tensor(qn, ps[:, SM, 36:36 + H], isc, ALU.mult)
                own(v.tensor_tensor(hv(num_s_half(1)), hv4(ps[:, 4, :]), bc(isc, 2, [P, H, P]), ALU.mult))
                v.tensor_tensor(num_s_half(1), ps[:, 7, :], num_s_half(1), ALU.add)
                own(v.tensor_tensor(den[:, H:2 * H], den[:, H:2 * H], qn, ALU.add))
                own(v.scalar_tensor_tensor(den, den, -1.0, den, ALU.mult, ALU.max))
                own(v.tensor_tensor(den, den, exp_out[:, 2 * H:4 * H], ALU.max))
                own(v.reciprocal(den, den))
                v.tensor_tensor(hv(num_s_half(0)), hv4(ps[:, 6, :]), bc(den[:, 0:H], 2, [P, H, P]), ALU.mult)
                own(v.tensor_tensor(hv(num_s_half(1)), hv(num_s_half(1)), bc(den[:, H:2 * H], 2, [P, H, P]), ALU.mult))
                own(v.tensor_tensor(decT[:, :], num_s[:, :], num_s[:, :], ALU.mult))
                v.tensor_reduce(hsq, decT[:, :].rearrange("p (n s) -> p n s", s=P), AX.X, ALU.add).then_inc(hsq_s, 1)
                dve.wait_ge(ga_read, l + 1)
                own(v.tensor_scalar(r_g[:, :], r_g[:, :], 1.0, None, ALU.add))
                v.reciprocal(r_g[:, :], r_g[:, :]).then_inc(rsig_s, 1)
                lo(base + 12)
                dve.wait_ge(gx_read, l + 1)
                own(v.tensor_scalar(i_g[:, :], i_g[:, :], 1.0, None, ALU.add))
                own(v.reciprocal(i_g[:, :], i_g[:, :]))
                own(v.tensor_tensor(rv(i_g), rv(i_g), xc, ALU.mult))
                lo(base + 13)
                dve.wait_ge(tanh_s, l + 1)
                th = x_pad[:, :, CONV_PAD:]
                own(v.tensor_scalar(rv(r_g), th, 1.0, None, ALU.add))
                own(v.reciprocal(r_g[:, :], r_g[:, :]))
                v.tensor_tensor(rv(r_g), rv(r_g), th, ALU.mult).then_inc(sqrt_in, 1)
                dve.wait_ge(gelu_exp, l + 1)
                own(v.tensor_scalar(kT[:, :], kT[:, :], 1.0, None, ALU.add))
                own(v.reciprocal(kT[:, :], kT[:, :]))
                own(v.tensor_tensor(rv(kT), rv(kT), gate_g, ALU.mult))
                dve.wait_ge(proj_out, (l + 1) * MIX_UNITS)
                own(v.tensor_scalar(sig_o[:, :], sig_o[:, :], 1.0, None, ALU.add))
                own(v.reciprocal(sig_o[:, :], sig_o[:, :]))
                lo(base + 14)
                dve.wait_ge(hstd_s, l + 1)
                own(v.reciprocal(hrstd, hstd))
                own(v.tensor_tensor(num_s[:, :].rearrange("p (n s) -> p n s", s=P), num_s[:, :].rearrange("p (n s) -> p n s", s=P),
                                    bc(hrstd, 2, [P, TT * H, P]), ALU.mult))
                nv = num_s[:, :].rearrange("p (c n) -> p c n", c=TT)
                own(v.tensor_tensor(nv, nv, bc(gain_row[:, l * ML:(l + 1) * ML], 1, [P, TT, ML]), ALU.mult))
                v.tensor_tensor(num_s[:, :], num_s[:, :], sig_o[:, :], ALU.mult).then_inc(yml_s, 1)
                for b in range(2):
                    dve.wait_ge(yT_hi, 2 * l + b + 1)
                    v.tensor_tensor(u_lo[:, 2 * b:2 * b + 2, :], ps[:, b, :].rearrange("p (k s) -> p k s", k=2),
                                    u_hi[:, 2 * b:2 * b + 2, :].bitcast(F32), ALU.subtract).then_inc(yT_lo, 1)
                dve.wait_ge(sqrt_out, l + 1)
                own(v.tensor_tensor(i_g[:, :], i_g[:, :], r_g[:, :], ALU.mult))
                for k in range(KR):
                    ins = v.tensor_tensor_scan(rv(r_g)[:, k, :], rv(qT)[:, k, :], rv(i_g)[:, k, :], 0.0, ALU.mult, ALU.add)
                own(ins)
                lo(base + 15)
                own(v.tensor_tensor(i_g[:, :], r_g[:, :], kT[:, :], ALU.mult))
                v.tensor_tensor(r_g[:, :], i_g[:, :], i_g[:, :], ALU.mult).then_inc(ysq_s, 1)
                dve.wait_ge(ysq_s, l + 1)
                v.tensor_tensor(rv(i_g), rv(i_g), bc(pcs(l, "rgn"), 2, [P, KR, S]), ALU.mult).then_inc(yrg_s, 1)
                dve.wait_ge(yr_hi, l + 1)
                v.tensor_tensor(u_lo[:, 4:8, :], rv(i_g), u_hi[:, 4:8, :].bitcast(F32), ALU.subtract).then_inc(yr_lo, 1)
                lo(base + 16)
                dve.wait_ge(used, base + 14)
                for t in range(TT):
                    for h in range(2):
                        r = resid[:, t, h * BANK:(h + 1) * BANK]
                        ins = v.tensor_tensor(r, ps[:, 4 + 2 * t + h, :], r, ALU.add)
                own(ins)
                dve.wait_ge(rgstd_s, l + 1)
                own(v.reciprocal(rstd_rg, std_rg))
                lo(base + 17)
                dve.wait_ge(used, base + 16)
                for t in range(TT):
                    for h in range(2):
                        r = resid[:, t, h * BANK:(h + 1) * BANK]
                        ins = v.scalar_tensor_tensor(r, ps[:, 2 * t + h, :], rstd_rg[:, t:t + 1], r, ALU.mult, ALU.add)
                ins.then_inc(resid_ready, 1)
                dve.wait_ge(resid_ready, 2 * l + 1)

            dve.wait_ge(rows_T, 1)
            v.tensor_copy(pcol[:, :, :], ps[:, 4, 0:LAYERS * PR].rearrange("p (l n) -> p l n", l=LAYERS)).then_inc(pcol_s, 1)
            dve.wait_ge(pcol_s, 1)
            dve.wait_ge(small_hi_s, 1)
            v.tensor_tensor(small_lo[:, :, :], small_raw[:, :, :], small_hi[:, :, :].bitcast(F32),
                            ALU.subtract).then_inc(small_lo_s, 1)
            mixer(0, MIX0)
            norm(1, 0, "ffn")

            def ffn_step(n, par, i, extra, has_down):
                if has_down:
                    lo(n + 2, extra)
                dve.wait_ge(used, extra + (n + 2))
                dve.wait_ge(silu_done, i + 1)
                v.tensor_tensor(hid[:, par, :], silu_s[:, par, :], ps[:, 2 + par, :], ALU.mult).then_inc(hid_s, 1)
                nxt = n + (3 if has_down else 2)
                lo(nxt, extra)
                dve.wait_ge(hT_hi, i + 1)
                v.tensor_tensor(hid_lo[:, par, :], hid[:, par, :], hid_hi[:, par, :].bitcast(F32),
                                ALU.subtract).then_inc(hT_lo, 1)
                lo(nxt + 1, extra)

            ffn_step(FFN0, 0, 0, 0, False)
            with dve.Fori(0, FFN_STEPS // 2) as it:
                for b in range(2):
                    ffn_step(FFN0 + 2 + 3 * b, (1 + b) % 2, it * 2 + (1 + b), it * 6, True)
            dve.wait_ge(used, MIX1)
            for t in range(TT):
                for h in range(2):
                    r = resid[:, t, h * BANK:(h + 1) * BANK]
                    ins = v.tensor_tensor(r, ps[:, 4 + 2 * t + h, :], r, ALU.add)
            ins.then_inc(resid_ready, 1)
            dve.wait_ge(resid_ready, 2)

            mixer(1, MIX1)
            norm(3, 1, "ffn")
            v.memset(y_hi[:, :].bitcast(F32), 0.0)
            v.memset(y_lo[:, :].bitcast(F32), 0.0)
            v.memset(slotT[:, :, :].bitcast(F32), 0.0).then_inc(moe_zero, 1)
            dve.wait_ge(logit_ps, 1)
            own(v.tensor_copy(logit, ps[:, SM, 0:TT * E].rearrange("p (t e) -> p t e", t=TT)))
            for t in range(TT):
                ins = v.max(top8[:, t, :], logit[:, t, :])
            own(ins)
            v.tensor_tensor(gdiff.unsqueeze(2), top8[:, :, 1:2], top8[:, :, 0:1], ALU.subtract).then_inc(gdiff_s, 1)
            for t in range(TT):
                ins = v.max_index(topi[:, t, :], top8[:, t, :], logit[:, t, :])
            own(ins)
            own(v.tensor_copy(topf, topi[:, :, :]))
            for t in range(TT):
                v.tensor_scalar(hot1[:, t, :], iota[:, 0:E], topf[:, t, 0:1], None, ALU.is_equal)
                ins = v.tensor_scalar(hot2[:, t, :], iota[:, 0:E], topf[:, t, 1:2], None, ALU.is_equal)
            own(ins)
            v.tensor_tensor(chosen, hot1, hot2, ALU.add).then_inc(chosen_s, 1)
            dve.wait_ge(chosen_s, 1)
            dve.wait_ge(gexp_s, 1)
            own(v.tensor_scalar(gw1, gexp, 1.0, None, ALU.add))
            own(v.reciprocal(gw1, gw1))
            own(v.tensor_tensor(gw2, gexp, gw1, ALU.mult))
            for t in range(TT):
                v.tensor_scalar(hot1[:, t, :], hot1[:, t, :], gw1[:, t:t + 1], None, ALU.mult)
                ins = v.tensor_scalar(hot2[:, t, :], hot2[:, t, :], gw2[:, t:t + 1], None, ALU.mult)
            own(ins)
            for q in range(2):
                ins = v.tensor_tensor(gate2[:, :, q * E:(q + 1) * E], hot1, hot2, ALU.add)
            own(ins)
            dve.wait_ge(pos_ps, 1)
            own(v.tensor_tensor(hot1, ps[:, SM, 16:16 + TT * E].rearrange("p (t e) -> p t e", t=TT), chosen, ALU.mult))
            v.tensor_scalar(slot_of[:, :, 0:E], hot1, -1.0, None, ALU.add)
            v.tensor_scalar(slot_of[:, :, E:2 * E], hot1, -1.0 - P, None, ALU.add)
            v.memset(tabf, 0.0)
            own(v.tensor_scalar(ov, ps[:, SM, 32:32 + E], float(P), None, ALU.is_gt))
            own(v.tensor_tensor_scan(ovc, ov, zero8, 0.0, ALU.add, ALU.add))
            row = [1, E, E]
            own(v.tensor_tensor(ovm[:, :, :], bc(ovc[0:1, :], 1, row), bc(iota[0:1, 1:1 + E], 2, row), ALU.is_equal))
            own(v.tensor_tensor(ovm[:, :, :], ovm[:, :, :], bc(ov[0:1, :], 1, row), ALU.mult))
            own(v.tensor_tensor(ovm[:, :, :], ovm[:, :, :], bc(iota[0:1, 0:E], 1, row), ALU.mult))
            own(v.tensor_reduce(tabf[0:1, TAB_E:TAB_E + E], ovm[:, :, :], AX.X, ALU.add))
            v.tensor_copy(tabf[0:1, 1:1 + E], iota[0:1, 0:E])
            v.tensor_scalar(tabf[0:1, 1 + E:1 + 2 * E], tabf[0:1, TAB_E:TAB_E + E], float(OVER), None, ALU.add)
            own(v.tensor_copy(tabf[0:1, TAB_N:TAB_N + 1], ovc[0:1, E - 1:E]))
            v.tensor_copy(tab[:, :], tabf[0:1, :]).then_inc(tab_s, 1)
            dve.wait_ge(tab_s, 1)
            n_over = dve.value_load(tab[0:1, TAB_N:TAB_N + 1], min_val=0, max_val=E)

            def slots(q):
                for t in range(TT):
                    ins = v.tensor_scalar(slot1h[:, t, :], iota[:, :], slot_of[:, t, q], None, ALU.is_equal)
                ins.then_inc(slots_s, 1)

            def gather_lo(count):
                for b in range(2):
                    dve.wait_ge(g_hi, count * 2 + (b + 1))
                    for k in range(4 * b, 4 * b + 4):
                        ins = v.scalar_tensor_tensor(u_lo[:, k, 0:P], ps[:, 5 + b, (k % 4) * P:(k % 4) * P + P],
                                                     pc(1, "ffn", k), u_hi[:, k, 0:P].bitcast(F32), ALU.mult, ALU.subtract)
                    ins.then_inc(g_lo, 1)

            SCATTER = (5, 6, 7, 2)

            def scatter_add(j, q):
                for n, b in enumerate(SCATTER):
                    t, h = n // 2, n % 2
                    r = resid[:, t, h * BANK:(h + 1) * BANK]
                    dve.wait_ge(sc_ps, j * 4 + (n + 1))
                    v.scalar_tensor_tensor(r, ps[:, b, :], gate2[:, t, q], r, ALU.mult, ALU.add).then_inc(sc_add, 1)

            slots(slice(0, 1))
            gather_lo(0)
            with dve.Fori(0, n_over + E) as j:
                ju = j * ITEM_UNITS
                q_prev = dve.value_load(tab[0:1, bass.ds(j, 1)], min_val=0, max_val=2 * E - 1)
                q_next = dve.value_load(tab[0:1, bass.ds(j + 2, 1)], min_val=0, max_val=2 * E - 1)

                def mult(n, k, extra=0):
                    dve.wait_ge(used, ju + extra + (n + 1))
                    dve.wait_ge(msilu, j * FB + (k + 1))
                    v.tensor_tensor(hid[:, 0, :], silu_s[:, 0, :], ps[:, 1, :], ALU.mult).then_inc(mhid, 1)

                def hT(k):
                    dve.wait_ge(mhT_hi, j * FB + (k + 1))
                    v.tensor_tensor(hid_lo[:, 0, :], ps[:, 2, :], hid_hi[:, 0, :].bitcast(F32), ALU.subtract).then_inc(mhT_lo, 1)

                l_ = lambda n, extra=0: lo(MOE0 + n, ju + extra)
                l_(2)
                l_(3)
                scatter_add(j, bass.ds(q_prev, 1))
                l_(4)
                l_(5)
                mult(MOE0 + 3, 0)
                l_(6)
                l_(7)
                hT(0)
                l_(8)
                l_(9)
                mult(MOE0 + 7, 1)
                l_(10)
                l_(11)
                dve.wait_ge(sT_ps, j + 1)
                slots(bass.ds(q_next, 1))
                with dve.Fori(2, FB) as i:
                    x6 = (i - 2) * 6
                    l_(12, x6)
                    l_(13, x6)
                    hT(i - 1)
                    l_(14, x6)
                    l_(15, x6)
                    mult(MOE0 + 13, i, x6)
                    l_(16, x6)
                    l_(17, x6)
                gather_lo(j + 1)
                hT(FB - 1)
                l_(42)
                l_(43)
                for b in range(2):
                    dve.wait_ge(yh_s, j * 2 + (b + 1))
                    v.tensor_tensor(y_lo[:, b * BANK:(b + 1) * BANK], ps[:, 3 + b, :],
                                    y_hi[:, b * BANK:(b + 1) * BANK].bitcast(F32), ALU.subtract).then_inc(yl_s, 1)
            q_last = dve.value_load(tab[0:1, bass.ds(n_over + E, 1)], min_val=0, max_val=2 * E - 1)
            scatter_add(n_over + E, bass.ds(q_last, 1))
            dve.wait_ge(std_ready, 5)
            own(v.reciprocal(rstd, std))
            dve.wait_ge(final_loaded, 16)
            for t in range(TT):
                v.scalar_tensor_tensor(xn[:, t, :], resid[:, t, :], rstd[:, t:t + 1], gain_row[:, :],
                                       ALU.mult, ALU.mult).then_inc(fin_s, 1)

        @block.tensor
        def _(pe):
            T = nc.tensor
            PASSES = 3

            def triple(out_ap, x_of, w_of, first, final, x_stationary=True):
                for n, (xa, wa) in enumerate(((0, 0), (1, 0), (0, 1))):
                    xs, ws = x_of(xa), w_of(wa)
                    lhsT, rhs = (xs, ws) if x_stationary else (ws, xs)
                    ins = T.matmul(out_ap, lhsT, rhs, start=first and n == 0, stop=final and n == PASSES - 1)
                return ins

            u_ = (u_hi, u_lo)
            hid_ = (hid_hi, hid_lo)

            def split(n, k):
                w = unit3(w_hi[n % SPLIT], k), unit3(w_lo[n % SPLIT], k)
                return lambda a: w[a]

            def ready(n, extra=0):
                pe.wait_ge(lo_done, extra + (n + 1))

            def norm_T(m):
                pe.wait_ge(xn_ready, m + 1)
                for b in range(4):
                    for k in (2 * b, 2 * b + 1):
                        for t in range(TT):
                            c = (k % 2) * S + t * P
                            ins = T.transpose(ps[:, 4 + b, c:c + P], xn[:, t, k * P:(k + 1) * P], ident[:, :])
                    ins.then_inc(xT_ps, 1)

            def small_product(which, signal):
                for t in range(TT):
                    for k in range(KD):
                        ins = triple(ps[:, SM, t * E:(t + 1) * E], lambda a: u_[a][:, k, t * P:(t + 1) * P],
                                     lambda a: (small_hi, small_lo)[a][:, which, k * E:(k + 1) * E], k == 0, k == KD - 1)
                ins.then_inc(signal, 1)

            def by_column(n, bank, extra=0):
                ready(n, extra)
                w = split(n, KD)
                for c in range(2):
                    for k in range(KD):
                        ins = triple(ps[:, bank, c * S:(c + 1) * S], lambda a: u_[a][:, k, :],
                                     lambda a: w(a)[:, k, c * P:(c + 1) * P], k == 0, k == KD - 1, False)
                ins.then_inc(used, 1)

            def by_token(n, bank):
                ready(n)
                w = split(n, KD)
                for t in range(TT):
                    for k in range(KD):
                        ins = triple(ps[:, bank, t * COLS:(t + 1) * COLS], lambda a: u_[a][:, k, t * P:(t + 1) * P],
                                     lambda a: w(a)[:, k, :], k == 0, k == KD - 1)
                ins.then_inc(used, 1)

            def rows_product(n, x_of, bank, first, final, extra=0, tiles=TT):
                w = split(n, 2)
                for r in range(2):
                    for t in range(tiles):
                        for h in range(2):
                            ins = triple(ps[:, bank + 2 * t + h, :], lambda a: x_of(a, r, t),
                                         lambda a: w(a)[:, r, h * BANK:(h + 1) * BANK],
                                         first and r == 0, final and r == 1)
                ins.then_inc(used, 1)

            def mixer(l, base):
                norm_T(2 * l)
                pe.wait_ge(u_lo_s, 8 * l + 4)
                if l == 0:
                    pe.wait_ge(small_lo_s, 1)
                small_product(l, gates_ps)

                def unit(j):
                    if j >= 2:
                        pe.wait_ge(proj_out, l * MIX_UNITS + j - 1)
                    (by_token if j // 2 in (3, 5) else by_column)(base + j, j % 2)

                for j in range(4):
                    unit(j)
                pe.wait_ge(logf_s, l + 1)
                T.matmul(ps[:, SM, 16:16 + TT * H], tri[:, :], log_f, start=True, stop=True).then_inc(cum_ps, 1)
                unit(4)
                pe.wait_ge(diag_s, l + 1)
                for c in range(TT):
                    ins = T.matmul(ps[:, 4 + c, :], ones[:, :], decT[:, c * BANK:(c + 1) * BANK], start=True, stop=True)
                ins.then_inc(r_ps, 1)
                unit(5)
                head = lambda t, h, c: t[:, h * S + c * P:h * S + (c + 1) * P]
                col = lambda b, h: ps[:, b, h * P:(h + 1) * P]
                for c in range(TT):
                    for h in range(H):
                        ins = T.matmul(col(6 + c, h), head(qT, h, c), head(kT, h, c), start=True, stop=True)
                ins.then_inc(qk_ps, 1)
                pe.wait_ge(sel_s, l + 1)
                T.matmul(ps[:, SM, 24:24 + 2 * H], last[:, :], sel_in, start=True, stop=True).then_inc(sel_ps, 1)
                for h in range(H):
                    ins = T.transpose(col(3, h), head(kT, h, 0), ident[:, :])
                ins.then_inc(kt_ps, 1)
                unit(6)
                unit(7)
                pe.wait_ge(dec_s, l + 1)
                for c in range(TT):
                    for h in range(H):
                        ins = T.transpose(col(4 + c, h), c4(w_dec)[:, c, h, :], ident[:, :])
                    ins.then_inc(dt_ps, 1)
                pe.wait_ge(kw_s, l + 1)
                pe.wait_ge(proj_out, l * MIX_UNITS + 8)
                vt = lambda c, h: v_tok[:, c * ML + h * P:c * ML + (h + 1) * P]
                for h in range(H):
                    T.matmul(col(3, h), kw_tok[:, h, :], vt(0, h), start=True, stop=True)
                for h in range(H):
                    ins = T.matmul(ps[:, SM, 32 + h:33 + h], kw_tok[:, h, :], ones[:, 0:1], start=True, stop=True)
                ins.then_inc(c_ps, 1)
                unit(8)
                pe.wait_ge(decT_s, l + 1)
                for c in range(TT):
                    for h in range(H):
                        ins = T.matmul(col(6 + c, h), c4(decT)[:, c, h, :], vt(c, h), start=True, stop=True)
                ins.then_inc(num_ps, 1)
                pe.wait_ge(c_s, l + 1)
                for h in range(H):
                    T.matmul(col(4, h), head(qT, h, 1), c_st[:, h, :], start=True, stop=True)
                for h in range(H):
                    ins = T.matmul(ps[:, SM, 36 + h:37 + h], head(qT, h, 1), n_st[:, h:h + 1], start=True, stop=True)
                ins.then_inc(inter_ps, 1)
                pe.wait_ge(conv_s, l + 1)
                pe.wait_ge(block_loaded, 64 * (l + 1))
                rg = lambda k: ps[:, 3 + 2 * (k // 2), (k % 2) * S:(k % 2) * S + S]
                for k in range(KR):
                    ins = T.matmul(rg(k), block_a[:, k, :], xc[:, k, :], start=True, stop=True)
                ins.then_inc(ga_ps, 1)
                unit(9)
                pe.wait_ge(ga_read, l + 1)
                for k in range(KR):
                    ins = T.matmul(rg(k), block_x[:, k, :], xc[:, k, :], start=True, stop=True)
                ins.then_inc(gx_ps, 1)
                unit(10)
                unit(11)
                pe.wait_ge(yml_s, l + 1)
                pe.wait_ge(proj_out, (l + 1) * MIX_UNITS)
                for b in range(2):
                    for k in (2 * b, 2 * b + 1):
                        for t in range(TT):
                            c = (k % 2) * S + t * P
                            ins = T.transpose(ps[:, b, c:c + P], num_s[:, t * ML + k * P:t * ML + (k + 1) * P], ident[:, :])
                    ins.then_inc(yT_ps, 1)
                pe.wait_ge(gx_read, l + 1)
                for j in (12, 13):
                    pe.wait_ge(yT_lo, 2 * l + (j - 11))
                    ready(base + j)
                    rows_product(base + j, lambda a, r, t: u_[a][:, 2 * (j - 12) + r, t * P:(t + 1) * P], 4, j == 12, j == 13)
                pe.wait_ge(ysq_s, l + 1)
                for t in range(TT):
                    for k in range(KR):
                        ins = T.matmul(ps[:, SM, 48 + t:49 + t], rv(r_g)[:, k, t * P:(t + 1) * P], ones[:, 0:1],
                                       start=k == 0, stop=k == KR - 1)
                ins.then_inc(ssq_ps, 1)
                pe.wait_ge(yr_lo, l + 1)
                pe.wait_ge(rgstd_s, l + 1)
                for j in (14, 15):
                    ready(base + j)
                    rows_product(base + j, lambda a, r, t: u_[a][:, 2 * (j - 12) + r, t * P:(t + 1) * P], 0, j == 14, j == 15)

            pe.wait_ge(consts_s, 1)
            pe.wait_ge(rows_loaded, 16 * 8 * LAYERS)
            n = LAYERS * PR
            T.transpose(ps[:, 4, 0:n], prow[0:n, :], ident[0:n, 0:n]).then_inc(rows_T, 1)
            pe.wait_ge(pcol_s, 1)
            mixer(0, MIX0)

            norm_T(1)
            pe.wait_ge(u_lo_s, 8)

            def down(n, par, i, first=False, final=False, extra=0):
                ready(n, extra)
                pe.wait_ge(hT_lo, i + 1)
                rows_product(n, lambda a, r, t: hid_[a][:, par, r * S + t * P:r * S + (t + 1) * P], 4, first, final)

            def ffn_step(n, par, i, first, extra=0):
                pe.wait_ge(silu_done, i - 1)
                by_column(n, par, extra)
                pe.wait_ge(hid_s, i - 1)
                by_column(n + 1, 2 + par, extra)
                down(n + 2, 1 - par, i - 1, first=first, extra=extra)

            by_column(FFN0, 0)
            by_column(FFN0 + 1, 2)
            ffn_step(FFN0 + 2, 1, 1, True)
            ffn_step(FFN0 + 5, 0, 2, False)
            with pe.Fori(1, FFN_STEPS // 2) as it:
                for b in range(2):
                    ffn_step(FFN0 + 2 + 3 * b, 1 - b, it * 2 + (1 + b), False, it * 6)
            down(MIX1 - 1, 0, FFN_STEPS - 1, final=True)

            mixer(1, MIX1)
            norm_T(3)
            pe.wait_ge(u_lo_s, 16)
            small_product(2, logit_ps)
            pe.wait_ge(chosen_s, 1)
            T.matmul(ps[:, SM, 16:16 + E], tri[:, :], chosen[:, 0, :], start=True, stop=True)
            T.matmul(ps[:, SM, 16 + E:16 + 2 * E], ones[:, :], chosen[:, 0, :], start=True, stop=False)
            T.matmul(ps[:, SM, 16 + E:16 + 2 * E], tri[:, :], chosen[:, 1, :], start=False, stop=True)
            T.matmul(ps[:, SM, 32:32 + E], ones[:, :], chosen[:, 0, :], start=True, stop=False)
            T.matmul(ps[:, SM, 32:32 + E], ones[:, :], chosen[:, 1, :], start=False, stop=True).then_inc(pos_ps, 1)

            def gather(count):
                pe.wait_ge(slots_s, count + 1)
                for b in range(2):
                    for k in range(4 * b, 4 * b + 4):
                        for t in range(TT):
                            ins = T.matmul(ps[:, 5 + b, (k % 4) * P:(k % 4) * P + P], xn[:, t, k * P:(k + 1) * P],
                                           slot1h[:, t, :], start=t == 0, stop=t == TT - 1)
                    ins.then_inc(gat_ps, 1)

            def scatter():
                for n, b in enumerate((5, 6, 7, 2)):
                    t, h = n // 2, n % 2
                    T.matmul(ps[:, b, :], slotT[:, t, :], y_hi[:, h * BANK:(h + 1) * BANK], start=True, stop=False)
                    T.matmul(ps[:, b, :], slotT[:, t, :], y_lo[:, h * BANK:(h + 1) * BANK], start=False,
                             stop=True).then_inc(sc_ps, 1)

            pe.wait_ge(tab_s, 1)
            n_over = pe.value_load(tab[0:1, TAB_N:TAB_N + 1], min_val=0, max_val=E)
            gather(0)
            pe.wait_ge(moe_zero, 1)
            with pe.Fori(0, n_over + E) as j:
                ju = j * ITEM_UNITS
                half = KD // 2

                def half_depth(n, bank, a, extra):
                    ready(n, ju + extra)
                    w = split(n, half)
                    for k in range(half):
                        ins = triple(ps[:, bank, :], lambda x_: u_[x_][:, half * a + k, 0:P], lambda x_: w(x_)[:, k, :],
                                     a == 0 and k == 0, a == 1 and k == half - 1)
                    ins.then_inc(used, 1)

                def gate(n, k, extra=0):
                    pe.wait_ge(msilu, j * FB + k)
                    for a in range(2):
                        half_depth(n + a, 0, a, extra)

                def up(n, k, extra=0):
                    pe.wait_ge(mhid, j * FB + k)
                    for a in range(2):
                        half_depth(n + a, 1, a, extra)

                def hidden_T(k):
                    pe.wait_ge(mhid, j * FB + (k + 1))
                    pe.wait_ge(mhT_lo, j * FB + k)
                    for c in range(4):
                        ins = T.transpose(ps[:, 2, c * P:(c + 1) * P], hid[:, 0, c * P:(c + 1) * P], ident[:, :])
                    ins.then_inc(mhT_ps, 1)

                def down_block(n, k, first=False, final=False, extra=0):
                    pe.wait_ge(mhT_lo, j * FB + (k + 1))
                    for a in range(2):
                        ready(n + a, ju + extra)
                        rows_product(n + a, lambda x_, r, t: hid_[x_][:, 0, (2 * a + r) * P:(2 * a + r + 1) * P], 3,
                                     first and a == 0, final and a == 1, tiles=1)

                pe.wait_ge(g_lo, j * 2 + 2)
                gate(MOE0, 0)
                pe.wait_ge(yl_s, j * 2)
                pe.wait_ge(sT_s, j)
                pe.wait_ge(mhT_lo, j * FB)
                scatter()
                up(MOE0 + 2, 0)
                gate(MOE0 + 4, 1)
                pe.wait_ge(sc_add, j * 4 + 4)
                hidden_T(0)
                up(MOE0 + 6, 1)
                for t in range(TT):
                    ins = T.transpose(ps[:, 7, t * P:(t + 1) * P], slot1h[:, t, :], ident[:, :])
                ins.then_inc(sT_ps, 1)
                down_block(MOE0 + 8, 0, first=True)
                with pe.Fori(2, FB) as i:
                    x6 = (i - 2) * 6
                    gate(MOE0 + 10, i, x6)
                    hidden_T(i - 1)
                    up(MOE0 + 12, i, x6)
                    down_block(MOE0 + 14, i - 1, extra=x6)
                gather(j + 1)
                hidden_T(FB - 1)
                down_block(MOE0 + 40, FB - 1, final=True)
            pe.wait_ge(yl_s, (n_over + E) * 2)
            pe.wait_ge(sT_s, n_over + E)
            pe.wait_ge(g_lo, (n_over + (E + 1)) * 2)
            scatter()


_INS = ["x", "norm_mix_g", "w_in", "ml_b_if", "ml_norm_g", "rg_conv_w", "rg_conv_b", "rg_w_a", "rg_b_a", "rg_w_x",
        "rg_b_x", "rg_lam", "rg_norm_g", "w_out", "norm_ffn_g", "ffn_w_gate", "ffn_w_up", "ffn_w_down", "moe_w_router",
        "moe_w_gate", "moe_w_up", "moe_w_down", "norm_final_g"]


def kernel(**inputs):
    import concourse.bacc as bacc
    from concourse.bass_utils import run_bass_kernel_spmd

    nc = bacc.Bacc("TRN2", target_bir_lowering=False, num_devices=1)
    arrays, args = {}, {}
    for name in _INS:
        a = np.ascontiguousarray(inputs[name])
        arrays[f"in_{name}"] = a
        args[name] = nc.dram_tensor(f"in_{name}", a.shape, mybir.dt.from_np(a.dtype), kind="ExternalInput").ap()
    out = nc.dram_tensor("out_y", inputs["x"].shape, F32, kind="ExternalOutput").ap()
    hybrid_kernel(nc, out=out, **args)
    r = run_bass_kernel_spmd(nc, [arrays], core_ids=[0])
    return r.results[0]["out_y"]
```

```python
from contextlib import ExitStack

import numpy as np
import concourse.bass as bass
from concourse import mybir

F32 = mybir.dt.float32
F32R = mybir.dt.float32r
I32 = mybir.dt.int32
U32 = mybir.dt.uint32
ALU = mybir.AluOpType
ACT = mybir.ActivationFunctionType
AX = mybir.AxisListType

P = 128
BANK = 512
RAW = 6
SPLIT = 3
UNIT = 2048
EPS = 1e-6
NEG = -1e30
GELU_C = 0.7978845608028654


class Counted:

    def __init__(self, sem):
        self.sem, self.value = sem, 0

    def after(self, eng, ins):
        ins.then_inc(self.sem, 1)
        self.value += 1
        eng.wait_ge(self.sem, self.value)


def hybrid_kernel(nc, x, norm_mix_g, w_in, ml_b_if, ml_norm_g, rg_conv_w, rg_conv_b, rg_w_a, rg_b_a,
                  rg_w_x, rg_b_x, rg_lam, rg_norm_g, w_out, norm_ffn_g, ffn_w_gate, ffn_w_up,
                  ffn_w_down, moe_w_router, moe_w_gate, moe_w_up, moe_w_down, norm_final_g, out):
    _, S, D = x.shape
    LAYERS = w_in.shape[0]
    ML = ml_norm_g.shape[1]
    RG = rg_lam.shape[1]
    H = ml_b_if.shape[1] // 2
    DH = ML // H
    TAPS = rg_conv_w.shape[1]
    FD = ffn_w_gate.shape[2]
    E = moe_w_router.shape[2]
    FE = moe_w_gate.shape[3]
    TT = S // P
    KD = D // P
    KR = RG // P
    GB = rg_w_a.shape[2]
    CONV_PAD = TAPS - 1
    assert (LAYERS, TT, KD, KR, H, DH, E) == (2, 2, 8, 4, 4, P, 8)

    COLS = UNIT // KD
    MIX_UNITS = (4 * ML + 2 * RG) // COLS
    OUT_UNITS = D * D // (P * UNIT)
    FFN_STEPS = FD // COLS
    MIX0 = 0
    FFN0 = MIX0 + MIX_UNITS + OUT_UNITS
    MIX1 = FFN0 + 3 * FFN_STEPS
    MOE0 = MIX1 + MIX_UNITS + OUT_UNITS
    FB = FE // BANK
    ITEM_UNITS = 6 * FB
    OVER = E
    assert MIX_UNITS == 12 and OUT_UNITS == 4 and FFN_STEPS % 2 == 1 and ITEM_UNITS % RAW == 0

    with ExitStack() as ctx:
        def sb(name, shape, dt=F32):
            return ctx.enter_context(nc.sbuf_tensor(name, shape, dt))

        def sem(name):
            return ctx.enter_context(nc.semaphore(name))

        raw = [sb(f"raw{i}", [P, UNIT]) for i in range(RAW)]
        w_hi = [sb(f"w_hi{i}", [P, UNIT], F32R) for i in range(SPLIT)]
        w_lo = [sb(f"w_lo{i}", [P, UNIT], F32R) for i in range(SPLIT)]
        resid = sb("resid", [P, TT, D])
        xn = sb("xn", [P, TT, D])
        u_hi = sb("u_hi", [P, KD, S], F32R)
        u_lo = sb("u_lo", [P, KD, S], F32R)
        hid_hi = sb("hid_hi", [P, 2, BANK], F32R)
        hid_lo = sb("hid_lo", [P, 2, BANK], F32R)
        y_hi = sb("y_hi", [P, D], F32R)
        y_lo = sb("y_lo", [P, D], F32R)
        slotT = sb("slotT", [P, TT, P], F32R)
        SMALL = 3 * KD * E
        small_hi = sb("small_hi", [P, SMALL + P], F32R)
        small_lo = sb("small_lo", [P, SMALL + P], F32R)
        small_raw = sb("small_raw", [P, SMALL + P])
        smallT = sb("smallT", [E, S])
        ident = sb("ident", [P, P])
        tri = sb("tri", [P, P])
        ones = sb("ones", [P, P])
        last = sb("last", [P, P])
        acausal = sb("acausal", [P, P])
        iota = sb("iota", [P, P])
        block_a = sb("block_a", [P, KR, P])
        block_x = sb("block_x", [P, KR, P])
        gain_row = sb("gain_row", [P, D])
        if_bias = sb("if_bias", [P, LAYERS, 2 * H])
        arena = [sb(f"arena{i}", [P, 1024]) for i in range(10)]
        x_pad = sb("x_pad", [P, KR, S + CONV_PAD])
        PROWS = LAYERS * (2 * KD + (TAPS + 5) * KR)
        pcol = sb("pcol", [P, PROWS])
        sml = sb("sml", [P, 512])

        qT, kT, v_tok, sig_o, w_dec, decT, num_s, kwc, r_g, i_g = arena
        c4 = lambda t: t[:, :].rearrange("p (c h s) -> p c h s", c=TT, h=H)
        hv = lambda t: t.rearrange("p (h s) -> p h s", h=H)
        rv = lambda t: t[:, :].rearrange("p (k s) -> p k s", k=KR)
        hv4 = lambda bank: bank.rearrange("p (h s) -> p h s", h=H)
        num_s_half = lambda c: num_s[:, c * BANK:(c + 1) * BANK]
        kw_tok = kwc[:, 0:BANK].rearrange("p (h s) -> p h s", h=H)
        c_st = kwc[:, BANK:2 * BANK].rearrange("p (h s) -> p h s", h=H)
        xc = xn[:, 0, :].rearrange("p (k s) -> p k s", k=KR)
        gate_g = xn[:, 1, :].rearrange("p (k s) -> p k s", k=KR)
        silu_s = qT[:, :].rearrange("p (b n) -> p b n", b=2)
        hid = kT[:, :].rearrange("p (b n) -> p b n", b=2)
        slot1h = v_tok[:, 0:TT * P].rearrange("p (t s) -> p t s", t=TT)
        prow = num_s[:, 0:P]

        _at = [0]

        def cols(n):
            _at[0] += n
            assert _at[0] <= 512
            return sml[:, _at[0] - n:_at[0]]

        ssq, std, rstd = cols(TT), cols(TT), cols(TT)
        z_if = cols(TT * 2 * H).rearrange("p (c n) -> p c n", c=TT)
        nabs, e_f, ls_a, ls_b, ls_c = (cols(TT * H) for _ in range(5))
        log_f, b_cum, r_in, cmax, m_run = (cols(TT * H) for _ in range(5))
        sel_in = cols(2 * H)
        sel_out = cols(2 * H)
        m_prev = cols(H)
        exp_in, exp_out = cols(4 * H), cols(4 * H)
        den, n_st = cols(TT * H), cols(H)
        qn = cols(H)
        hsq, hstd, hrstd = cols(TT * H), cols(TT * H), cols(TT * H)
        rstd_rg, std_rg = cols(TT), cols(TT)
        lam_n, lam_e, lam_a, lam_b, lam_c, decay = (cols(KR) for _ in range(6))
        nb_a, nb_x = cols(KR), cols(KR)
        eps_c = cols(1)
        logit = cols(TT * E).rearrange("p (t e) -> p t e", t=TT)
        top8 = cols(TT * E).rearrange("p (t e) -> p t e", t=TT)
        topf = cols(TT * E).rearrange("p (t e) -> p t e", t=TT)
        gdiff, gexp, gw1, gw2 = cols(TT), cols(TT), cols(TT), cols(TT)
        hot1 = cols(TT * E).rearrange("p (t e) -> p t e", t=TT)
        hot2 = cols(TT * E).rearrange("p (t e) -> p t e", t=TT)
        chosen = cols(TT * E).rearrange("p (t e) -> p t e", t=TT)
        gate2 = cols(TT * 2 * E).rearrange("p (t q) -> p t q", t=TT)
        slot_of = cols(TT * 2 * E).rearrange("p (t q) -> p t q", t=TT)
        cnt, ov, ovc, zero8 = cols(E), cols(E), cols(E), cols(E)
        tabf = cols(32)
        topi = sb("topi", [P, TT, E], U32)
        tab = sb("tab", [1, 32], I32)
        ovm = sb("ovm", [1, E, E])
        TAB_N, TAB_E = 25, 17

        FIRST, at = {}, 0
        PARAMS = (("mix", norm_mix_g, KD), ("ffn", norm_ffn_g, KD), ("conv", rg_conv_w, TAPS * KR), ("conv_b", rg_conv_b, KR),
                  ("b_a", rg_b_a, KR), ("b_x", rg_b_x, KR), ("lam", rg_lam, KR), ("rgn", rg_norm_g, KR))
        for name, _, n in PARAMS:
            FIRST[name] = (at, n)
            at += LAYERS * n
        assert at == PROWS

        def pcs(l, name):
            a, n = FIRST[name]
            return pcol[:, a + l * n:a + (l + 1) * n]

        def pc(l, name, k=0):
            return pcs(l, name)[:, k:k + 1]

        ps = ctx.enter_context(nc.psum_tensor("ps", [P, 8, BANK], F32))
        SM = 2

        loaded = [sem(f"unit_loaded{i}") for i in range(RAW)]
        hi_done, lo_done = sem("unit_hi_done"), sem("unit_lo_done")
        used = sem("unit_used")
        x_loaded, rows_loaded, small_loaded = sem("x_loaded"), sem("rows_loaded"), sem("small_loaded")
        block_loaded, final_loaded = sem("block_loaded"), sem("final_gain_loaded")
        consts_s, block_zero, small_zero = sem("consts"), sem("block_zero"), sem("small_zero")
        pool_own, dve_own, act_own = (Counted(sem(n)) for n in ("pool_own", "dve_own", "act_own"))
        rows_T, pcol_s = sem("rows_transposed"), sem("pcol_ready")
        small_hi_s, small_lo_s = sem("small_hi_s"), sem("small_lo_s")
        resid_ready, std_ready, xn_ready = sem("resid_ready"), sem("std_ready"), sem("xn_ready")
        xT_ps, u_hi_s, u_lo_s = sem("xT_in_psum"), sem("u_hi_s"), sem("u_lo_s")
        proj_out = sem("projection_evacuated")
        small_ps, smallT_s = sem("small_ps"), sem("smallT_s")
        acc_half = sem("acc_first_tile")
        gates_ps, nabs_s, ef_s, logf_s = sem("gates_ps"), sem("nabs_s"), sem("exp_f_s"), sem("log_f_s")
        cum_ps, diag_s, r_ps = sem("cumsum_ps"), sem("diag_s"), sem("r_ps")
        qk_ps, sel_s, sel_ps, kt_ps = sem("qk_ps"), sem("chunk_end_s"), sem("chunk_end_ps"), sem("k_tok_ps")
        expin_s, expout_s = sem("exp_in_s"), sem("exp_out_s")
        wm_s, wexp_s, dec_s = sem("decay_log_s"), sem("decay_exp_s"), sem("decay_qk_s")
        dt_ps, decT_s, kw_s, c_ps, c_s = sem("decT_ps"), sem("decT_s"), sem("kw_s"), sem("c_ps"), sem("c_s")
        num_ps, inter_ps = sem("num_ps"), sem("inter_ps")
        hsq_s, hstd_s, yml_s, yT_ps, yT_hi, yT_lo = (sem("head_sq_s"), sem("head_std_s"), sem("y_ml_s"),
                                                     sem("y_ml_T_ps"), sem("y_ml_T_hi"), sem("y_ml_T_lo"))
        lamn_s, lame_s, conv_s = sem("lam_neg_s"), sem("lam_exp_s"), sem("conv_s")
        ga_ps, ga_read, gx_ps, gx_read = sem("rg_a_ps"), sem("rg_a_read"), sem("rg_x_ps"), sem("rg_x_read")
        a_s, a2_s, sqrt_in, sqrt_out = sem("decay_s"), sem("decay_sq_s"), sem("sqrt_in"), sem("sqrt_out")
        ix_s, y_s = sem("gated_input_s"), sem("y_rg_raw_s")
        ysq_s, ssq_ps, rgstd_s = sem("y_rg_sq_s"), sem("y_rg_ssq_ps"), sem("rg_std_s")
        yrg_s, yr_hi, yr_lo = sem("y_rg_s"), sem("y_rg_hi"), sem("y_rg_lo")
        silu_done, hid_s, hT_hi, hT_lo = sem("silu_done"), sem("hidden_s"), sem("hidden_hi"), sem("hidden_lo")
        logit_ps, gdiff_s, gexp_s, chosen_s = sem("logit_ps"), sem("gate_diff_s"), sem("gate_exp_s"), sem("chosen_s")
        pos_ps, tab_s, slots_s, moe_zero = sem("pos_ps"), sem("table_ready"), sem("slots_ready"), sem("moe_zero")
        mhT_ps, msilu, mhid, mhT_hi, mhT_lo = (sem("moe_hT_ps"), sem("moe_silu"), sem("moe_hid"),
                                               sem("moe_hT_hi"), sem("moe_hT_lo"))
        gat_ps, g_hi, g_lo = sem("gather_ps"), sem("gather_hi"), sem("gather_lo")
        sT_ps, sT_s, yh_s, yl_s = sem("slotT_ps"), sem("slotT_s"), sem("y_hi_s"), sem("y_lo_s")
        sc_ps, sc_add = sem("scatter_ps"), sem("scatter_added")
        fin_s, out_s = sem("final_ready"), sem("out_stored")

        x_v = x[0].rearrange("(t p) d -> p t d", p=P)
        out_v = out[0].rearrange("(t p) d -> p t d", p=P)
        deep = lambda w: w.rearrange("(k p) n -> p k n", p=P)

        def mix_cols(l, j):
            starts = [4 * ML + 2 * H, 0, ML, 2 * ML, 4 * ML + 2 * H + RG, 3 * ML]
            if j < MIX_UNITS:
                c = starts[j // 2] + COLS * (j % 2)
                return deep(w_in[l])[:, :, c:c + COLS]
            r = ((j - MIX_UNITS) * 2 + ML // P) % KD
            return deep(w_out[l])[:, r:r + 2, :]

        unit3 = lambda t, k: t[:, :].rearrange("p (k n) -> p k n", k=k)

        def load_blocks(eng, l):
            for h in range(2):
                for w, t in ((rg_w_a, block_a), (rg_w_x, block_x)):
                    eng.dma_start(t[GB * h:GB * h + GB, :, GB * h:GB * h + GB],
                                  w[l].rearrange("(k h) i j -> h i k j", h=2)[h]).then_inc(block_loaded, 16)

        block = ctx.enter_context(nc.Block())

        @block.sync
        def _(sp):
            def load(n, src, k, extra=0):
                if n >= RAW:
                    sp.wait_ge(lo_done, extra + (n - RAW + 1))
                sp.dma_start(unit3(raw[n % RAW], k), src).then_inc(loaded[n % RAW], 16)

            def mixer(l, base, first=0):
                for j in range(first, MIX_UNITS + OUT_UNITS):
                    load(base + j, mix_cols(l, j), KD if j < MIX_UNITS else 2)

            sp.dma_start(resid[:, :, :], x_v).then_inc(x_loaded, 16)
            mixer(0, MIX0)

            gate_v, up_v, down_v = deep(ffn_w_gate[0]), deep(ffn_w_up[0]), deep(ffn_w_down[0])
            load(FFN0, gate_v[:, :, 0:COLS], KD)
            load(FFN0 + 1, up_v[:, :, 0:COLS], KD)
            with sp.Fori(0, FFN_STEPS // 2) as it:
                for a in range(2):
                    n, i = FFN0 + 2 + 3 * a, it * 2 + (1 + a)
                    load(n, gate_v[:, :, bass.ds(i * COLS, COLS)], KD, it * 6)
                    load(n + 1, up_v[:, :, bass.ds(i * COLS, COLS)], KD, it * 6)
                    load(n + 2, down_v[:, bass.ds(it * 4 + 2 * a, 2), :], 2, it * 6)
            load(MIX1 - 1, down_v[:, 2 * FFN_STEPS - 2:2 * FFN_STEPS, :], 2)

            sp.wait_ge(gx_ps, 1)
            load_blocks(sp, 1)
            mixer(1, MIX1)
            sp.wait_ge(yml_s, LAYERS)
            sp.dma_start(gain_row[:, :], norm_final_g.partition_broadcast(P)).then_inc(final_loaded, 16)

            half = KD // 2

            def expert_units(e, extra):
                g_v = moe_w_gate[0].rearrange("e (k p) n -> p e k n", p=P)
                u_v = moe_w_up[0].rearrange("e (k p) n -> p e k n", p=P)
                d_v = moe_w_down[0].rearrange("e (k p) n -> p e k n", p=P)

                def gate_up(n, i, extra):
                    for m, v in enumerate((g_v, u_v)):
                        for a in range(2):
                            load(n + 2 * m + a, v[:, bass.ds(e, 1), half * a:half * a + half, bass.ds(i * BANK, BANK)]
                                 .rearrange("p e k n -> p (e k) n"), half, extra)

                def down(n, i, extra):
                    for a in range(2):
                        load(n + a, d_v[:, bass.ds(e, 1), bass.ds(i * 4 + 2 * a, 2), :]
                             .rearrange("p e k n -> p (e k) n"), 2, extra)

                gate_up(MOE0, 0, extra)
                with sp.Fori(1, FB) as i:
                    gate_up(MOE0 + 4, i, extra + (i - 1) * 6)
                    down(MOE0 + 8, i - 1, extra + (i - 1) * 6)
                down(MOE0 + ITEM_UNITS - 2, FB - 1, extra)

            with sp.Fori(0, E) as j:
                expert_units(j, j * ITEM_UNITS)
            sp.wait_ge(tab_s, 1)
            n_over = sp.value_load(tab[0:1, TAB_N:TAB_N + 1], min_val=0, max_val=E)
            with sp.If(n_over > 0):
                with sp.Fori(0, n_over) as j:
                    e = sp.value_load(tab[0:1, bass.ds(j + TAB_E, 1)], min_val=0, max_val=E - 1)
                    expert_units(e, j * ITEM_UNITS + E * ITEM_UNITS)
            for a in range(2):
                load(MOE0 + a, deep(moe_w_gate[0, 0])[:, 0:half, 0:BANK], half, (n_over + E) * ITEM_UNITS)
            sp.wait_ge(fin_s, 2)
            for t in range(TT):
                sp.dma_start(out_v[:, t, :], xn[:, t, :]).then_inc(out_s, 16)
            sp.wait_ge(out_s, 16 * TT)

        @block.gpsimd
        def _(pool):
            g = nc.gpsimd
            g.memset(small_raw[:, SMALL:], 0.0).then_inc(small_zero, 1)
            g.memset(block_a[:, :, :], 0.0).then_inc(block_zero, 1)
            g.memset(block_x[:, :, :], 0.0).then_inc(block_zero, 1)
            g.memset(ident[:, :], 0.0)
            g.memset(tri[:, :], 1.0)
            g.memset(ones[:, :], 1.0)
            g.memset(last[:, :], 0.0)
            g.memset(eps_c, EPS)
            g.memset(zero8, 0.0)
            g.memset(x_pad[:, :, 0:CONV_PAD], 0.0)
            pool_own.after(pool, g.memset(acausal[:, :], 0.0))
            sel = lambda t, **kw: g.affine_select(out=t[:, :], in_=t[:, :], **kw)
            sel(ident, compare_op=ALU.not_equal, fill=1.0, base=0, pattern=[[-1, P]], channel_multiplier=1)
            sel(tri, compare_op=ALU.is_ge, fill=0.0, base=0, pattern=[[1, P]], channel_multiplier=-1)
            sel(last, compare_op=ALU.not_equal, fill=1.0, base=1 - P, pattern=[[0, P]], channel_multiplier=1)
            sel(acausal, compare_op=ALU.is_ge, fill=NEG, base=0, pattern=[[-1, P]], channel_multiplier=1)
            g.iota(iota[:, :], pattern=[[1, P]], base=0, channel_multiplier=0,
                   allow_small_or_imprecise_dtypes=True).then_inc(consts_s, 1)
            for l in range(LAYERS):
                pool.wait_ge(conv_s, l + 1)
                pool.wait_ge(gx_read, l + 1)
                g.tensor_tensor(rv(i_g), rv(i_g), xc, ALU.mult).then_inc(ix_s, 1)
                pool.wait_ge(a_s, l + 1)
                g.tensor_tensor(kT[:, :], r_g[:, :], r_g[:, :], ALU.mult).then_inc(a2_s, 1)
                pool.wait_ge(y_s, l + 1)
                g.tensor_tensor(r_g[:, :], i_g[:, :], i_g[:, :], ALU.mult).then_inc(ysq_s, 1)

        @block.scalar
        def _(act):
            a = nc.scalar

            def hi(n, extra=0, turns=0):
                act.wait_ge(loaded[n % RAW], turns * 16 + 16 * (n // RAW + 1))
                if n >= SPLIT:
                    act.wait_ge(used, extra + (n - SPLIT + 1))
                a.copy(w_hi[n % SPLIT][:, :], raw[n % RAW][:, :]).then_inc(hi_done, 1)

            def norm_std(m):
                for t in range(TT):
                    if m == 0:
                        if t == 0:
                            act.wait_ge(x_loaded, 16)
                            act.wait_ge(consts_s, 1)
                    else:
                        act.wait_ge(resid_ready, 2 * m - 1 + t)
                    std_tile(t)

            def std_tile(t):
                act_own.after(act, a.activation(xn[:, t, :], resid[:, t, :], ACT.Square, accum_out=ssq[:, t:t + 1]))
                a.activation(std[:, t:t + 1], ssq[:, t:t + 1], ACT.Sqrt, bias=eps_c, scale=1.0 / D).then_inc(std_ready, 1)

            def norm_hi(m, l, which):
                act.wait_ge(pcol_s, 1)
                for b in range(4):
                    act.wait_ge(xT_ps, 4 * m + b + 1)
                    for k in (2 * b, 2 * b + 1):
                        ins = a.activation(u_hi[:, k, :], ps[:, 4 + b, (k % 2) * S:(k % 2) * S + S], ACT.Copy,
                                           scale=pc(l, which, k))
                    ins.then_inc(u_hi_s, 1)

            def mixer(l, base):
                if l == 0:
                    norm_std(0)
                    hi(base)
                    act.wait_ge(small_loaded, 16 * (3 + 2 * LAYERS))
                    act.wait_ge(small_zero, 1)
                    a.copy(small_hi[:, :], small_raw[:, :]).then_inc(small_hi_s, 1)
                    norm_hi(0, 0, "mix")
                    hi(base + 1)
                    hi(base + 2)
                else:
                    hi(base + 1)
                    hi(base + 2)
                    norm_std(2 * l)
                    norm_hi(2 * l, l, "mix")

                def evac(j):
                    act.wait_ge(used, base + j + 1)
                    bank, part, second = ps[:, j % 2, :], j // 2, j % 2
                    tiles = bank.rearrange("p (k s) -> p k s", k=2)
                    by_tok = lambda t: t[:, :].rearrange("p (c n) -> p c n", c=TT)[:, :, second * COLS:(second + 1) * COLS]
                    if part == 0:
                        ins = a.copy(x_pad[:, 2 * second:2 * second + 2, CONV_PAD:], tiles)
                    elif part in (1, 2):
                        ins = a.copy((qT, kT)[part - 1][:, second * BANK:(second + 1) * BANK], bank)
                    elif part == 3:
                        ins = a.copy(by_tok(v_tok), tiles)
                    elif part == 4:
                        ins = a.activation(gate_g[:, 2 * second:2 * second + 2, :], tiles, ACT.Gelu_apprx_tanh)
                    else:
                        ins = a.activation(by_tok(sig_o), tiles, ACT.Sigmoid)
                    ins.then_inc(proj_out, 1)

                def recurrent_gate(out_t, bias):
                    for k in range(KR):
                        ins = a.activation(rv(out_t)[:, k, :], ps[:, 4 + k // 2, (k % 2) * S:(k % 2) * S + S], ACT.Sigmoid,
                                           bias=pc(l, bias, k))
                    return ins

                hi(base + 3)
                evac(0)
                act.wait_ge(nabs_s, l + 1)
                a.activation(e_f, nabs, ACT.Exp).then_inc(ef_s, 1)
                act.wait_ge(lamn_s, l + 1)
                a.activation(lam_e, lam_n, ACT.Exp).then_inc(lame_s, 1)
                for j in range(1, 5):
                    hi(base + j + 3)
                    evac(j)
                act.wait_ge(expin_s, l + 1)
                a.activation(exp_out, exp_in, ACT.Exp).then_inc(expout_s, 1)
                act.wait_ge(wm_s, l + 1)
                a.activation(w_dec[:, :], w_dec[:, :], ACT.Exp).then_inc(wexp_s, 1)
                hi(base + 8)
                evac(5)
                act.wait_ge(ga_ps, l + 1)
                recurrent_gate(r_g, "b_a").then_inc(ga_read, 1)
                hi(base + 9)
                evac(6)
                act.wait_ge(gx_ps, l + 1)
                recurrent_gate(i_g, "b_x").then_inc(gx_read, 1)
                act.wait_ge(conv_s, l + 1)
                for k in range(KR):
                    ins = a.activation(x_pad[:, k, CONV_PAD:], rv(r_g)[:, k, :], ACT.Tanh, scale=decay[:, k:k + 1])
                act_own.after(act, ins)
                hi(base + 10)
                evac(7)
                for k in range(KR):
                    ins = a.activation(rv(r_g)[:, k, :], rv(r_g)[:, k, :], ACT.Exp, scale=lam_c[:, k:k + 1])
                ins.then_inc(a_s, 1)
                for c in range(TT):
                    act.wait_ge(dt_ps, 2 * l + c + 1)
                    ins = a.copy(decT[:, c * BANK:(c + 1) * BANK], ps[:, 4 + c, :])
                ins.then_inc(decT_s, 1)
                act.wait_ge(c_ps, l + 1)
                a.copy(c_st, ps[:, 3, :].rearrange("p (h s) -> p h s", h=H))
                a.copy(n_st, ps[:, SM, 32:32 + H]).then_inc(c_s, 1)
                act.wait_ge(sqrt_in, l + 1)
                a.activation(kT[:, :], kT[:, :], ACT.Sqrt).then_inc(sqrt_out, 1)
                hi(base + 11)
                evac(8)
                hi(base + 12)
                evac(9)
                act.wait_ge(hsq_s, l + 1)
                a.activation(hstd, hsq, ACT.Sqrt, bias=eps_c, scale=1.0 / DH).then_inc(hstd_s, 1)
                hi(base + 13)
                evac(10)
                hi(base + 14)
                evac(11)
                act.wait_ge(yrg_s, l + 1)
                a.copy(u_hi[:, 4:8, :], rv(kT)).then_inc(yr_hi, 1)
                act.wait_ge(ssq_ps, l + 1)
                a.activation(std_rg, ps[:, SM, 48:48 + TT], ACT.Sqrt, bias=eps_c, scale=1.0 / RG).then_inc(rgstd_s, 1)
                hi(base + 15)
                for b in range(2):
                    act.wait_ge(yT_ps, 2 * l + b + 1)
                    a.copy(u_hi[:, 2 * b:2 * b + 2, :], ps[:, 4 + b, :].rearrange("p (k s) -> p k s", k=2)).then_inc(yT_hi, 1)

            at = 0
            for _, src, n in PARAMS:
                flat = src.rearrange("l j c -> (l j c)") if len(src.shape) == 3 else src.rearrange("l c -> (l c)")
                act.dma_start(prow[at:at + LAYERS * n, :], flat.rearrange("(k p) -> k p", p=P)).then_inc(rows_loaded, 16)
                at += LAYERS * n
            sm = lambda i: small_raw[:, i * KD * E:(i + 1) * KD * E].rearrange("p (k n) -> p k n", k=KD)
            for l in range(LAYERS):
                act.dma_start(sm(l), deep(w_in[l])[:, :, 4 * ML:4 * ML + 2 * H]).then_inc(small_loaded, 16)
            act.dma_start(sm(2), deep(moe_w_router[0])).then_inc(small_loaded, 16)
            for l in range(LAYERS):
                act.dma_start(if_bias[:, l, :], ml_b_if[l].partition_broadcast(P)).then_inc(small_loaded, 16)
                act.dma_start(gain_row[:, l * ML:(l + 1) * ML], ml_norm_g[l].partition_broadcast(P)).then_inc(small_loaded, 16)
            act.wait_ge(block_zero, 2)
            load_blocks(act, 0)
            mixer(0, MIX0)

            hi(FFN0)
            hi(FFN0 + 1)
            norm_std(1)
            norm_hi(1, 0, "ffn")

            def ffn_step(n, par, i, extra, turns, has_down):
                if has_down:
                    hi(n + 2, extra, turns)
                act.wait_ge(used, extra + n + 1)
                if has_down:
                    act.wait_ge(hid_s, i - 1)
                a.activation(silu_s[:, par, :], ps[:, par, :], ACT.Silu).then_inc(silu_done, 1)
                nxt = n + (3 if has_down else 2)
                hi(nxt, extra, turns)
                act.wait_ge(hid_s, i + 1)
                if has_down:
                    act.wait_ge(used, extra + n)
                a.copy(hid_hi[:, par, :], hid[:, par, :]).then_inc(hT_hi, 1)
                hi(nxt + 1, extra, turns)

            ffn_step(FFN0, 0, 0, 0, 0, False)
            with act.Fori(0, FFN_STEPS // 2) as it:
                for b in range(2):
                    ffn_step(FFN0 + 2 + 3 * b, (1 + b) % 2, it * 2 + (1 + b), it * 6, it, True)

            mixer(1, MIX1)
            hi(MOE0)
            hi(MOE0 + 1)
            norm_std(3)
            norm_hi(3, 1, "ffn")
            act.wait_ge(gdiff_s, 1)
            a.activation(gexp, gdiff, ACT.Exp).then_inc(gexp_s, 1)

            def gather_hi(count):
                for b in range(2):
                    act.wait_ge(gat_ps, count * 2 + (b + 1))
                    for k in range(4 * b, 4 * b + 4):
                        ins = a.activation(u_hi[:, k, 0:P], ps[:, 5 + b, (k % 4) * P:(k % 4) * P + P], ACT.Copy,
                                           scale=pc(1, "ffn", k))
                    ins.then_inc(g_hi, 1)

            gather_hi(0)
            act.wait_ge(tab_s, 1)
            n_over = act.value_load(tab[0:1, TAB_N:TAB_N + 1], min_val=0, max_val=E)
            with act.Fori(0, n_over + E) as j:
                ju, jt = j * ITEM_UNITS, j * (ITEM_UNITS // RAW)

                def silu(n, k, extra=0):
                    act.wait_ge(used, ju + extra + (n + 1))
                    act.wait_ge(mhid, j * FB + k)
                    a.activation(silu_s[:, 0, :], ps[:, 0, :], ACT.Silu).then_inc(msilu, 1)

                def hT(k):
                    act.wait_ge(mhT_ps, j * FB + k + 1)
                    a.copy(hid_hi[:, 0, :], ps[:, 2, :]).then_inc(mhT_hi, 1)

                h = lambda n, extra=0, turns=0: hi(MOE0 + n, ju + extra, jt + turns)
                h(2)
                h(3)
                h(4)
                silu(MOE0 + 1, 0)
                h(5)
                h(6)
                h(7)
                hT(0)
                h(8)
                silu(MOE0 + 5, 1)
                h(9)
                act.wait_ge(sT_ps, j + 1)
                a.copy(slotT[:, :, :], ps[:, 7, 0:TT * P].rearrange("p (t s) -> p t s", t=TT)).then_inc(sT_s, 1)
                h(10)
                h(11)
                with act.Fori(2, FB) as i:
                    x6, t1 = (i - 2) * 6, i - 2
                    h(12, x6, t1)
                    h(13, x6, t1)
                    hT(i - 1)
                    h(14, x6, t1)
                    silu(MOE0 + 11, i, x6)
                    h(15, x6, t1)
                    h(16, x6, t1)
                    h(17, x6, t1)
                gather_hi(j + 1)
                hT(FB - 1)
                h(42)
                h(43)
                for b in range(2):
                    act.wait_ge(used, ju + (MOE0 + ITEM_UNITS))
                    a.copy(y_hi[:, b * BANK:(b + 1) * BANK], ps[:, 3 + b, :]).then_inc(yh_s, 1)
            act.wait_ge(sc_add, (n_over + (E + 1)) * 4)
            for t in range(TT):
                std_tile(t)

        @block.vector
        def _(dve):
            v = nc.vector
            own = lambda ins: dve_own.after(dve, ins)
            bc = lambda ap, axis, shape: ap.unsqueeze(axis).broadcast_to(shape)

            def lo(n, extra=0):
                dve.wait_ge(hi_done, extra + (n + 1))
                v.tensor_tensor(w_lo[n % SPLIT][:, :], raw[n % RAW][:, :], w_hi[n % SPLIT][:, :].bitcast(F32),
                                ALU.subtract).then_inc(lo_done, 1)

            def norm(m, l, which):
                for t in range(TT):
                    dve.wait_ge(std_ready, 2 * m + t + 1)
                    own(v.reciprocal(rstd[:, t:t + 1], std[:, t:t + 1]))
                    v.tensor_scalar(xn[:, t, :], resid[:, t, :], rstd[:, t:t + 1], None, ALU.mult).then_inc(xn_ready, 1)
                for b in range(4):
                    dve.wait_ge(u_hi_s, 4 * m + b + 1)
                    for k in (2 * b, 2 * b + 1):
                        ins = v.scalar_tensor_tensor(u_lo[:, k, :], ps[:, 4 + b, (k % 2) * S:(k % 2) * S + S],
                                                     pc(l, which, k), u_hi[:, k, :].bitcast(F32), ALU.mult, ALU.subtract)
                    ins.then_inc(u_lo_s, 1)

            def log1p(z, s_, s2, p):
                own(v.tensor_scalar(s_, z, 2.0, None, ALU.add))
                own(v.reciprocal(s_, s_))
                own(v.tensor_tensor(s_, z, s_, ALU.mult))
                own(v.tensor_tensor(s2, s_, s_, ALU.mult))
                own(v.tensor_scalar(p, s2, 1.0 / 15, None, ALU.mult))
                for n in (13, 11, 9, 7, 5, 3):
                    own(v.scalar_tensor_tensor(p, p, 1.0 / n, s2, ALU.add, ALU.mult))
                own(v.scalar_tensor_tensor(p, p, 1.0, s_, ALU.add, ALU.mult))

            def transpose_small(i):
                dve.wait_ge(small_ps, i)
                v.tensor_copy(smallT[:, :], ps[0:E, 3, 0:S]).then_inc(smallT_s, 1)

            def add_tile(t, bank):
                for h in range(2):
                    r = resid[:, t, h * BANK:(h + 1) * BANK]
                    ins = v.tensor_tensor(r, ps[:, bank + 2 * t + h, :], r, ALU.add)
                ins.then_inc(resid_ready, 1)

            def mixer(l, base):
                if l == 0:
                    lo(base)
                    norm(0, 0, "mix")
                    dve.wait_ge(small_hi_s, 1)
                    v.tensor_tensor(small_lo[:, :], small_raw[:, :], small_hi[:, :].bitcast(F32),
                                    ALU.subtract).then_inc(small_lo_s, 1)
                    lo(base + 1)
                    lo(base + 2)
                else:
                    lo(base + 1)
                    lo(base + 2)
                    norm(2 * l, l, "mix")
                transpose_small(l + 1)
                lo(base + 3)
                dve.wait_ge(gates_ps, l + 1)
                own(v.tensor_tensor(z_if, ps[:, SM, 0:TT * 2 * H].rearrange("p (c n) -> p c n", c=TT),
                                    bc(if_bias[:, l, :], 1, [P, TT, 2 * H]), ALU.add))
                ig, fg = z_if[:, :, 0:H], z_if[:, :, H:2 * H]
                c2 = lambda t: t.rearrange("p (c h) -> p c h", c=TT)
                v.scalar_tensor_tensor(c2(nabs), fg, -1.0, fg, ALU.mult, ALU.min).then_inc(nabs_s, 1)
                v.scalar_tensor_tensor(lam_n, pcs(l, "lam"), -1.0, pcs(l, "lam"), ALU.mult, ALU.min).then_inc(lamn_s, 1)
                dve.wait_ge(ef_s, l + 1)
                log1p(e_f, ls_a, ls_b, ls_c)
                own(v.tensor_scalar(c2(ls_a), fg, 0.0, None, ALU.min))
                v.scalar_tensor_tensor(log_f, ls_c, -2.0, ls_a, ALU.mult, ALU.add).then_inc(logf_s, 1)
                lo(base + 4)
                dve.wait_ge(lame_s, l + 1)
                log1p(lam_e, lam_a, lam_b, decay)
                own(v.tensor_scalar(lam_a, pcs(l, "lam"), -1.0, 0.0, ALU.mult, ALU.max))
                own(v.scalar_tensor_tensor(lam_b, decay, 2.0, lam_a, ALU.mult, ALU.add))
                v.tensor_scalar(decay, lam_b, 8.0, None, ALU.mult)
                v.tensor_scalar(lam_c, lam_b, -8.0, None, ALU.mult)
                lo(base + 5)
                dve.wait_ge(cum_ps, l + 1)
                own(v.tensor_copy(b_cum, ps[:, SM, 16:16 + TT * H]))
                own(v.tensor_tensor(c2(r_in), ig, c2(b_cum), ALU.subtract))
                v.tensor_tensor(decT[:, :].rearrange("p (n s) -> p n s", s=P), bc(ident[:, :], 1, [P, TT * H, P]),
                                bc(r_in, 2, [P, TT * H, P]), ALU.mult).then_inc(diag_s, 1)
                dve.wait_ge(proj_out, l * MIX_UNITS + 2)
                for j in range(TAPS):
                    for k in range(KR):
                        row = x_pad[:, k, j:j + S]
                        tap = pc(l, "conv", j * KR + k)
                        if j == 0:
                            ins = v.tensor_scalar(xc[:, k, :], row, tap, pc(l, "conv_b", k), ALU.mult, ALU.add)
                        else:
                            ins = v.scalar_tensor_tensor(xc[:, k, :], row, tap, xc[:, k, :], ALU.mult, ALU.add)
                    if j < TAPS - 1:
                        own(ins)
                ins.then_inc(conv_s, 1)
                lo(base + 6)
                dve.wait_ge(r_ps, l + 1)
                for c in range(TT):
                    ins = v.tensor_tensor(c4(w_dec)[:, c], hv4(ps[:, 4 + c, :]), bc(acausal[:, :], 1, [P, H, P]), ALU.add)
                own(ins)
                own(v.tensor_reduce(cmax, w_dec[:, :].rearrange("p (n s) -> p n s", s=P), AX.X, ALU.max))
                own(v.tensor_scalar(m_run[:, 0:H], cmax[:, 0:H], 0.0, None, ALU.max))
                v.tensor_copy(sel_in[:, 0:H], m_run[:, 0:H])
                v.tensor_copy(sel_in[:, H:2 * H], b_cum[:, 0:H]).then_inc(sel_s, 1)
                lo(base + 7)
                dve.wait_ge(sel_ps, l + 1)
                own(v.tensor_copy(sel_out, ps[:, SM, 24:24 + 2 * H]))
                own(v.tensor_tensor(m_prev, sel_out[:, 0:H], sel_out[:, H:2 * H], ALU.add))
                own(v.tensor_tensor(m_run[:, H:2 * H], cmax[:, H:2 * H], m_prev, ALU.max))
                v.tensor_tensor(exp_in[:, 0:H], r_in[:, 0:H], sel_out[:, 0:H], ALU.subtract)
                v.tensor_tensor(exp_in[:, H:2 * H], m_prev, m_run[:, H:2 * H], ALU.subtract)
                v.scalar_tensor_tensor(exp_in[:, 2 * H:4 * H], b_cum, -1.0, m_run, ALU.mult,
                                       ALU.subtract).then_inc(expin_s, 1)
                v.tensor_tensor(w_dec[:, :].rearrange("p (n s) -> p n s", s=P), w_dec[:, :].rearrange("p (n s) -> p n s", s=P),
                                bc(m_run, 2, [P, TT * H, P]), ALU.subtract).then_inc(wm_s, 1)
                lo(base + 8)
                dve.wait_ge(wexp_s, l + 1)
                dve.wait_ge(qk_ps, l + 1)
                for c in range(TT):
                    w = w_dec[:, c * BANK:(c + 1) * BANK]
                    ins = v.scalar_tensor_tensor(w, ps[:, 6 + c, :], float(DH) ** -0.5, w, ALU.mult, ALU.mult)
                ins.then_inc(dec_s, 1)
                dve.wait_ge(kt_ps, l + 1)
                dve.wait_ge(expout_s, l + 1)
                own(v.tensor_scalar(exp_out[:, 0:H], exp_out[:, 0:H], float(DH) ** -0.5, None, ALU.mult))
                v.tensor_tensor(kw_tok, hv4(ps[:, 3, :]), bc(exp_out[:, 0:H], 2, [P, H, P]), ALU.mult).then_inc(kw_s, 1)
                lo(base + 9)
                dve.wait_ge(dec_s, l + 1)
                own(v.tensor_reduce(den, w_dec[:, :].rearrange("p (n s) -> p n s", s=P), AX.X, ALU.add))
                lo(base + 10)
                dve.wait_ge(a2_s, l + 1)
                v.scalar_tensor_tensor(rv(kT), rv(kT), 1.0, x_pad[:, :, CONV_PAD:], ALU.add, ALU.mult).then_inc(sqrt_in, 1)
                lo(base + 11)
                dve.wait_ge(inter_ps, l + 1)
                isc = exp_out[:, H:2 * H]
                v.tensor_tensor(qn, ps[:, SM, 36:36 + H], isc, ALU.mult)
                own(v.tensor_tensor(hv(num_s_half(1)), hv4(ps[:, 4, :]), bc(isc, 2, [P, H, P]), ALU.mult))
                v.tensor_tensor(num_s_half(1), ps[:, 7, :], num_s_half(1), ALU.add)
                own(v.tensor_tensor(den[:, H:2 * H], den[:, H:2 * H], qn, ALU.add))
                own(v.scalar_tensor_tensor(den, den, -1.0, den, ALU.mult, ALU.max))
                own(v.tensor_tensor(den, den, exp_out[:, 2 * H:4 * H], ALU.max))
                own(v.reciprocal(den, den))
                v.tensor_tensor(hv(num_s_half(0)), hv4(ps[:, 6, :]), bc(den[:, 0:H], 2, [P, H, P]), ALU.mult)
                own(v.tensor_tensor(hv(num_s_half(1)), hv(num_s_half(1)), bc(den[:, H:2 * H], 2, [P, H, P]), ALU.mult))
                own(v.tensor_tensor(decT[:, :], num_s[:, :], num_s[:, :], ALU.mult))
                v.tensor_reduce(hsq, decT[:, :].rearrange("p (n s) -> p n s", s=P), AX.X, ALU.add).then_inc(hsq_s, 1)
                lo(base + 12)
                dve.wait_ge(sqrt_out, l + 1)
                dve.wait_ge(ix_s, l + 1)
                own(v.tensor_tensor(i_g[:, :], i_g[:, :], kT[:, :], ALU.mult))
                for k in range(KR):
                    ins = v.tensor_tensor_scan(rv(kT)[:, k, :], rv(r_g)[:, k, :], rv(i_g)[:, k, :], 0.0, ALU.mult, ALU.add)
                own(ins)
                dve.wait_ge(proj_out, l * MIX_UNITS + 10)
                v.tensor_tensor(rv(i_g), rv(kT), gate_g, ALU.mult).then_inc(y_s, 1)
                dve.wait_ge(y_s, l + 1)
                v.tensor_tensor(rv(kT), rv(i_g), bc(pcs(l, "rgn"), 2, [P, KR, S]), ALU.mult).then_inc(yrg_s, 1)
                lo(base + 13)
                dve.wait_ge(hstd_s, l + 1)
                own(v.reciprocal(hrstd, hstd))
                own(v.tensor_tensor(num_s[:, :].rearrange("p (n s) -> p n s", s=P), num_s[:, :].rearrange("p (n s) -> p n s", s=P),
                                    bc(hrstd, 2, [P, TT * H, P]), ALU.mult))
                nv = num_s[:, :].rearrange("p (c n) -> p c n", c=TT)
                own(v.tensor_tensor(nv, nv, bc(gain_row[:, l * ML:(l + 1) * ML], 1, [P, TT, ML]), ALU.mult))
                lo(base + 14)
                dve.wait_ge(yr_hi, l + 1)
                v.tensor_tensor(u_lo[:, 4:8, :], rv(kT), u_hi[:, 4:8, :].bitcast(F32), ALU.subtract).then_inc(yr_lo, 1)
                dve.wait_ge(proj_out, (l + 1) * MIX_UNITS)
                v.tensor_tensor(num_s[:, :], num_s[:, :], sig_o[:, :], ALU.mult).then_inc(yml_s, 1)
                dve.wait_ge(rgstd_s, l + 1)
                own(v.reciprocal(rstd_rg, std_rg))
                lo(base + 15)
                for b in range(2):
                    dve.wait_ge(yT_hi, 2 * l + b + 1)
                    v.tensor_tensor(u_lo[:, 2 * b:2 * b + 2, :], ps[:, 4 + b, :].rearrange("p (k s) -> p k s", k=2),
                                    u_hi[:, 2 * b:2 * b + 2, :].bitcast(F32), ALU.subtract).then_inc(yT_lo, 1)
                lo(base + 16)
                dve.wait_ge(used, base + 14)
                for t in range(TT):
                    for h in range(2):
                        r = resid[:, t, h * BANK:(h + 1) * BANK]
                        ins = v.scalar_tensor_tensor(r, ps[:, 2 * t + h, :], rstd_rg[:, t:t + 1], r, ALU.mult, ALU.add)
                own(ins)
                lo(base + 17)
                dve.wait_ge(acc_half, 2 * l + 1)
                add_tile(0, 4)
                dve.wait_ge(used, base + 16)
                add_tile(1, 4)
                dve.wait_ge(resid_ready, 4 * l + 2)

            dve.wait_ge(rows_T, 1)
            v.tensor_copy(pcol[:, :], ps[:, 4, 0:PROWS]).then_inc(pcol_s, 1)
            dve.wait_ge(pcol_s, 1)
            mixer(0, MIX0)
            norm(1, 0, "ffn")

            def ffn_step(n, par, i, extra, has_down):
                if has_down:
                    lo(n + 2, extra)
                dve.wait_ge(used, extra + (n + 2))
                dve.wait_ge(silu_done, i + 1)
                v.tensor_tensor(hid[:, par, :], silu_s[:, par, :], ps[:, 2 + par, :], ALU.mult).then_inc(hid_s, 1)
                nxt = n + (3 if has_down else 2)
                lo(nxt, extra)
                dve.wait_ge(hT_hi, i + 1)
                v.tensor_tensor(hid_lo[:, par, :], hid[:, par, :], hid_hi[:, par, :].bitcast(F32),
                                ALU.subtract).then_inc(hT_lo, 1)
                lo(nxt + 1, extra)

            ffn_step(FFN0, 0, 0, 0, False)
            with dve.Fori(0, FFN_STEPS // 2) as it:
                for b in range(2):
                    ffn_step(FFN0 + 2 + 3 * b, (1 + b) % 2, it * 2 + (1 + b), it * 6, True)
            dve.wait_ge(acc_half, 2)
            add_tile(0, 4)
            dve.wait_ge(used, MIX1)
            add_tile(1, 4)
            dve.wait_ge(resid_ready, 4)

            mixer(1, MIX1)
            norm(3, 1, "ffn")
            v.memset(y_hi[:, :].bitcast(F32), 0.0)
            v.memset(y_lo[:, :].bitcast(F32), 0.0)
            v.memset(slotT[:, :, :].bitcast(F32), 0.0).then_inc(moe_zero, 1)
            def slots(q):
                for t in range(TT):
                    ins = v.tensor_scalar(slot1h[:, t, :], iota[:, :], slot_of[:, t, q], None, ALU.is_equal)
                ins.then_inc(slots_s, 1)

            transpose_small(LAYERS + 1)
            dve.wait_ge(logit_ps, 1)
            own(v.tensor_copy(logit, ps[:, SM, 0:TT * E].rearrange("p (t e) -> p t e", t=TT)))
            for t in range(TT):
                ins = v.max(top8[:, t, :], logit[:, t, :])
            own(ins)
            v.tensor_tensor(gdiff.unsqueeze(2), top8[:, :, 1:2], top8[:, :, 0:1], ALU.subtract).then_inc(gdiff_s, 1)
            for t in range(TT):
                ins = v.max_index(topi[:, t, :], top8[:, t, :], logit[:, t, :])
            own(ins)
            own(v.tensor_copy(topf, topi[:, :, :]))
            for t in range(TT):
                v.tensor_scalar(hot1[:, t, :], iota[:, 0:E], topf[:, t, 0:1], None, ALU.is_equal)
                ins = v.tensor_scalar(hot2[:, t, :], iota[:, 0:E], topf[:, t, 1:2], None, ALU.is_equal)
            own(ins)
            v.tensor_tensor(chosen, hot1, hot2, ALU.add).then_inc(chosen_s, 1)
            dve.wait_ge(chosen_s, 1)
            dve.wait_ge(pos_ps, 1)
            own(v.tensor_tensor(topf, ps[:, SM, 16:16 + TT * E].rearrange("p (t e) -> p t e", t=TT), chosen, ALU.mult))
            own(v.tensor_scalar(slot_of[:, :, 0:E], topf, -1.0, None, ALU.add))
            slots(slice(0, 1))
            v.tensor_scalar(slot_of[:, :, E:2 * E], topf, -1.0 - P, None, ALU.add)
            v.memset(tabf, 0.0)
            own(v.tensor_scalar(ov, ps[:, SM, 32:32 + E], float(P), None, ALU.is_gt))
            own(v.tensor_tensor_scan(ovc, ov, zero8, 0.0, ALU.add, ALU.add))
            row = [1, E, E]
            own(v.tensor_tensor(ovm[:, :, :], bc(ovc[0:1, :], 1, row), bc(iota[0:1, 1:1 + E], 2, row), ALU.is_equal))
            own(v.tensor_tensor(ovm[:, :, :], ovm[:, :, :], bc(ov[0:1, :], 1, row), ALU.mult))
            own(v.tensor_tensor(ovm[:, :, :], ovm[:, :, :], bc(iota[0:1, 0:E], 1, row), ALU.mult))
            own(v.tensor_reduce(tabf[0:1, TAB_E:TAB_E + E], ovm[:, :, :], AX.X, ALU.add))
            v.tensor_copy(tabf[0:1, 1:1 + E], iota[0:1, 0:E])
            v.tensor_scalar(tabf[0:1, 1 + E:1 + 2 * E], tabf[0:1, TAB_E:TAB_E + E], float(OVER), None, ALU.add)
            own(v.tensor_copy(tabf[0:1, TAB_N:TAB_N + 1], ovc[0:1, E - 1:E]))
            v.tensor_copy(tab[:, :], tabf[0:1, :]).then_inc(tab_s, 1)
            dve.wait_ge(tab_s, 1)
            dve.wait_ge(gexp_s, 1)
            own(v.tensor_scalar(gw1, gexp, 1.0, None, ALU.add))
            own(v.reciprocal(gw1, gw1))
            own(v.tensor_tensor(gw2, gexp, gw1, ALU.mult))
            for t in range(TT):
                v.tensor_scalar(hot1[:, t, :], hot1[:, t, :], gw1[:, t:t + 1], None, ALU.mult)
                ins = v.tensor_scalar(hot2[:, t, :], hot2[:, t, :], gw2[:, t:t + 1], None, ALU.mult)
            own(ins)
            for q in range(2):
                ins = v.tensor_tensor(gate2[:, :, q * E:(q + 1) * E], hot1, hot2, ALU.add)
            own(ins)
            n_over = dve.value_load(tab[0:1, TAB_N:TAB_N + 1], min_val=0, max_val=E)

            def gather_lo(count):
                for b in range(2):
                    dve.wait_ge(g_hi, count * 2 + (b + 1))
                    for k in range(4 * b, 4 * b + 4):
                        ins = v.scalar_tensor_tensor(u_lo[:, k, 0:P], ps[:, 5 + b, (k % 4) * P:(k % 4) * P + P],
                                                     pc(1, "ffn", k), u_hi[:, k, 0:P].bitcast(F32), ALU.mult, ALU.subtract)
                    ins.then_inc(g_lo, 1)

            SCATTER = (5, 6, 7, 2)

            def scatter_add(j, q):
                for n, b in enumerate(SCATTER):
                    t, h = n // 2, n % 2
                    r = resid[:, t, h * BANK:(h + 1) * BANK]
                    dve.wait_ge(sc_ps, j * 4 + (n + 1))
                    v.scalar_tensor_tensor(r, ps[:, b, :], gate2[:, t, q], r, ALU.mult, ALU.add).then_inc(sc_add, 1)

            gather_lo(0)
            with dve.Fori(0, n_over + E) as j:
                ju = j * ITEM_UNITS
                q_prev = dve.value_load(tab[0:1, bass.ds(j, 1)], min_val=0, max_val=2 * E - 1)
                q_next = dve.value_load(tab[0:1, bass.ds(j + 2, 1)], min_val=0, max_val=2 * E - 1)

                def mult(n, k, extra=0):
                    dve.wait_ge(used, ju + extra + (n + 1))
                    dve.wait_ge(msilu, j * FB + (k + 1))
                    v.tensor_tensor(hid[:, 0, :], silu_s[:, 0, :], ps[:, 1, :], ALU.mult).then_inc(mhid, 1)

                def hT(k):
                    dve.wait_ge(mhT_hi, j * FB + (k + 1))
                    v.tensor_tensor(hid_lo[:, 0, :], ps[:, 2, :], hid_hi[:, 0, :].bitcast(F32), ALU.subtract).then_inc(mhT_lo, 1)

                l_ = lambda n, extra=0: lo(MOE0 + n, ju + extra)
                l_(2)
                l_(3)
                scatter_add(j, bass.ds(q_prev, 1))
                l_(4)
                l_(5)
                mult(MOE0 + 3, 0)
                l_(6)
                l_(7)
                hT(0)
                l_(8)
                l_(9)
                mult(MOE0 + 7, 1)
                l_(10)
                l_(11)
                dve.wait_ge(sT_ps, j + 1)
                slots(bass.ds(q_next, 1))
                with dve.Fori(2, FB) as i:
                    x6 = (i - 2) * 6
                    l_(12, x6)
                    l_(13, x6)
                    hT(i - 1)
                    l_(14, x6)
                    l_(15, x6)
                    mult(MOE0 + 13, i, x6)
                    l_(16, x6)
                    l_(17, x6)
                gather_lo(j + 1)
                hT(FB - 1)
                l_(42)
                l_(43)
                for b in range(2):
                    dve.wait_ge(yh_s, j * 2 + (b + 1))
                    v.tensor_tensor(y_lo[:, b * BANK:(b + 1) * BANK], ps[:, 3 + b, :],
                                    y_hi[:, b * BANK:(b + 1) * BANK].bitcast(F32), ALU.subtract).then_inc(yl_s, 1)
            q_last = dve.value_load(tab[0:1, bass.ds(n_over + E, 1)], min_val=0, max_val=2 * E - 1)
            scatter_add(n_over + E, bass.ds(q_last, 1))
            dve.wait_ge(final_loaded, 16)
            for t in range(TT):
                dve.wait_ge(std_ready, 9 + t)
                own(v.reciprocal(rstd[:, t:t + 1], std[:, t:t + 1]))
                v.scalar_tensor_tensor(xn[:, t, :], resid[:, t, :], rstd[:, t:t + 1], gain_row[:, :],
                                       ALU.mult, ALU.mult).then_inc(fin_s, 1)

        @block.tensor
        def _(pe):
            T = nc.tensor
            PASSES = 3

            def triple(out_ap, x_of, w_of, first, final, x_stationary=True):
                for n, (xa, wa) in enumerate(((0, 0), (1, 0), (0, 1))):
                    xs, ws = x_of(xa), w_of(wa)
                    lhsT, rhs = (xs, ws) if x_stationary else (ws, xs)
                    ins = T.matmul(out_ap, lhsT, rhs, start=first and n == 0, stop=final and n == PASSES - 1)
                return ins

            u_ = (u_hi, u_lo)
            hid_ = (hid_hi, hid_lo)

            def split(n, k):
                w = unit3(w_hi[n % SPLIT], k), unit3(w_lo[n % SPLIT], k)
                return lambda a: w[a]

            def ready(n, extra=0):
                pe.wait_ge(lo_done, extra + (n + 1))

            def norm_T(m):
                for t in range(TT):
                    pe.wait_ge(xn_ready, 2 * m + t + 1)
                    for k in range(KD):
                        c = (k % 2) * S + t * P
                        ins = T.transpose(ps[:, 4 + k // 2, c:c + P], xn[:, t, k * P:(k + 1) * P], ident[:, :])
                        if t == TT - 1 and k % 2:
                            ins.then_inc(xT_ps, 1)

            def small_product(which):
                for k in range(KD):
                    c = (which * KD + k) * E
                    ins = triple(ps[:, 3, 0:S], lambda a: u_[a][:, k, :],
                                 lambda a: (small_hi, small_lo)[a][:, c:c + P], k == 0, k == KD - 1, False)
                ins.then_inc(small_ps, 1)

            def small_back(i, signal):
                pe.wait_ge(smallT_s, i)
                for t in range(TT):
                    ins = T.transpose(ps[:, SM, t * E:(t + 1) * E], smallT[:, t * P:(t + 1) * P], ident[0:E, 0:E])
                ins.then_inc(signal, 1)

            def by_column(n, bank, extra=0):
                ready(n, extra)
                w = split(n, KD)
                for c in range(2):
                    for k in range(KD):
                        ins = triple(ps[:, bank, c * S:(c + 1) * S], lambda a: u_[a][:, k, :],
                                     lambda a: w(a)[:, k, c * P:(c + 1) * P], k == 0, k == KD - 1, False)
                ins.then_inc(used, 1)

            def by_token(n, bank):
                ready(n)
                w = split(n, KD)
                for t in range(TT):
                    for k in range(KD):
                        ins = triple(ps[:, bank, t * COLS:(t + 1) * COLS], lambda a: u_[a][:, k, t * P:(t + 1) * P],
                                     lambda a: w(a)[:, k, :], k == 0, k == KD - 1)
                ins.then_inc(used, 1)

            def rows_product(n, x_of, bank, first, final, tiles=TT, half=False):
                w = split(n, 2)
                for t in range(tiles):
                    for r in range(2):
                        for h in range(2):
                            ins = triple(ps[:, bank + 2 * t + h, :], lambda a: x_of(a, r, t),
                                         lambda a: w(a)[:, r, h * BANK:(h + 1) * BANK],
                                         first and r == 0, final and r == 1)
                    if half and t == 0:
                        ins.then_inc(acc_half, 1)
                ins.then_inc(used, 1)

            def mixer(l, base):
                norm_T(2 * l)
                pe.wait_ge(u_lo_s, 8 * l + 4)
                if l == 0:
                    pe.wait_ge(small_lo_s, 1)
                small_product(l)

                def unit(j):
                    if j >= 2:
                        pe.wait_ge(proj_out, l * MIX_UNITS + j - 1)
                    (by_token if j // 2 in (3, 5) else by_column)(base + j, j % 2)

                unit(0)
                small_back(l + 1, gates_ps)
                unit(1)
                unit(2)
                pe.wait_ge(logf_s, l + 1)
                T.matmul(ps[:, SM, 16:16 + TT * H], tri[:, :], log_f, start=True, stop=True).then_inc(cum_ps, 1)
                unit(3)
                pe.wait_ge(diag_s, l + 1)
                for c in range(TT):
                    ins = T.matmul(ps[:, 4 + c, :], ones[:, :], decT[:, c * BANK:(c + 1) * BANK], start=True, stop=True)
                ins.then_inc(r_ps, 1)
                unit(4)
                pe.wait_ge(sel_s, l + 1)
                T.matmul(ps[:, SM, 24:24 + 2 * H], last[:, :], sel_in, start=True, stop=True).then_inc(sel_ps, 1)
                unit(5)
                pe.wait_ge(proj_out, l * MIX_UNITS + 6)
                head = lambda t, h, c: t[:, h * S + c * P:h * S + (c + 1) * P]
                col = lambda b, h: ps[:, b, h * P:(h + 1) * P]
                for c in range(TT):
                    for h in range(H):
                        ins = T.matmul(col(6 + c, h), head(qT, h, c), head(kT, h, c), start=True, stop=True)
                ins.then_inc(qk_ps, 1)
                for h in range(H):
                    ins = T.transpose(col(3, h), head(kT, h, 0), ident[:, :])
                ins.then_inc(kt_ps, 1)
                pe.wait_ge(sel_s, l + 1)
                pe.wait_ge(conv_s, l + 1)
                pe.wait_ge(block_loaded, 64 * (l + 1))
                rg = lambda k: ps[:, 4 + k // 2, (k % 2) * S:(k % 2) * S + S]
                for k in range(KR):
                    ins = T.matmul(rg(k), block_a[:, k, :], xc[:, k, :], start=True, stop=True)
                ins.then_inc(ga_ps, 1)
                unit(6)
                pe.wait_ge(ga_read, l + 1)
                for k in range(KR):
                    ins = T.matmul(rg(k), block_x[:, k, :], xc[:, k, :], start=True, stop=True)
                ins.then_inc(gx_ps, 1)
                unit(7)
                pe.wait_ge(dec_s, l + 1)
                pe.wait_ge(gx_read, l + 1)
                for c in range(TT):
                    for h in range(H):
                        ins = T.transpose(col(4 + c, h), c4(w_dec)[:, c, h, :], ident[:, :])
                    ins.then_inc(dt_ps, 1)
                pe.wait_ge(kw_s, l + 1)
                pe.wait_ge(proj_out, l * MIX_UNITS + 8)
                vt = lambda c, h: v_tok[:, c * ML + h * P:c * ML + (h + 1) * P]
                for h in range(H):
                    T.matmul(col(3, h), kw_tok[:, h, :], vt(0, h), start=True, stop=True)
                for h in range(H):
                    ins = T.matmul(ps[:, SM, 32 + h:33 + h], kw_tok[:, h, :], ones[:, 0:1], start=True, stop=True)
                ins.then_inc(c_ps, 1)
                unit(8)
                pe.wait_ge(decT_s, l + 1)
                for c in range(TT):
                    for h in range(H):
                        ins = T.matmul(col(6 + c, h), c4(decT)[:, c, h, :], vt(c, h), start=True, stop=True)
                ins.then_inc(num_ps, 1)
                pe.wait_ge(c_s, l + 1)
                for h in range(H):
                    T.matmul(col(4, h), head(qT, h, 1), c_st[:, h, :], start=True, stop=True)
                for h in range(H):
                    ins = T.matmul(ps[:, SM, 36 + h:37 + h], head(qT, h, 1), n_st[:, h:h + 1], start=True, stop=True)
                ins.then_inc(inter_ps, 1)
                unit(9)
                unit(10)
                unit(11)
                pe.wait_ge(ysq_s, l + 1)
                for t in range(TT):
                    for k in range(KR):
                        ins = T.matmul(ps[:, SM, 48 + t:49 + t], rv(r_g)[:, k, t * P:(t + 1) * P], ones[:, 0:1],
                                       start=k == 0, stop=k == KR - 1)
                ins.then_inc(ssq_ps, 1)
                pe.wait_ge(yr_lo, l + 1)
                pe.wait_ge(rgstd_s, l + 1)
                pe.wait_ge(proj_out, (l + 1) * MIX_UNITS)

                def out_unit(j, bank):
                    ready(base + j)
                    row = ((j - MIX_UNITS) * 2 + ML // P) % KD
                    rows_product(base + j, lambda a, r, t: u_[a][:, row + r, t * P:(t + 1) * P], bank, j % 2 == 0, j % 2 == 1,
                                 half=j == MIX_UNITS + OUT_UNITS - 1)

                out_unit(12, 0)
                out_unit(13, 0)
                pe.wait_ge(yml_s, l + 1)
                for b in range(2):
                    for k in (2 * b, 2 * b + 1):
                        for t in range(TT):
                            c = (k % 2) * S + t * P
                            ins = T.transpose(ps[:, 4 + b, c:c + P], num_s[:, t * ML + k * P:t * ML + (k + 1) * P], ident[:, :])
                    ins.then_inc(yT_ps, 1)
                pe.wait_ge(yT_lo, 2 * l + 2)
                out_unit(14, 4)
                out_unit(15, 4)

            pe.wait_ge(consts_s, 1)
            pe.wait_ge(rows_loaded, 16 * len(PARAMS))
            T.transpose(ps[:, 4, 0:PROWS], prow[0:PROWS, :], ident[0:PROWS, 0:PROWS]).then_inc(rows_T, 1)
            pe.wait_ge(pcol_s, 1)
            mixer(0, MIX0)

            norm_T(1)
            pe.wait_ge(u_lo_s, 8)

            def down(n, par, i, first=False, final=False, extra=0):
                ready(n, extra)
                pe.wait_ge(hT_lo, i + 1)
                rows_product(n, lambda a, r, t: hid_[a][:, par, r * S + t * P:r * S + (t + 1) * P], 4, first, final,
                             half=final)

            def ffn_step(n, par, i, first, extra=0):
                pe.wait_ge(silu_done, i - 1)
                by_column(n, par, extra)
                pe.wait_ge(hid_s, i - 1)
                by_column(n + 1, 2 + par, extra)
                down(n + 2, 1 - par, i - 1, first=first, extra=extra)

            by_column(FFN0, 0)
            by_column(FFN0 + 1, 2)
            ffn_step(FFN0 + 2, 1, 1, True)
            ffn_step(FFN0 + 5, 0, 2, False)
            with pe.Fori(1, FFN_STEPS // 2) as it:
                for b in range(2):
                    ffn_step(FFN0 + 2 + 3 * b, 1 - b, it * 2 + (1 + b), False, it * 6)
            down(MIX1 - 1, 0, FFN_STEPS - 1, final=True)

            mixer(1, MIX1)
            norm_T(3)
            pe.wait_ge(u_lo_s, 16)
            small_product(2)
            small_back(LAYERS + 1, logit_ps)
            pe.wait_ge(chosen_s, 1)
            T.matmul(ps[:, SM, 16:16 + E], tri[:, :], chosen[:, 0, :], start=True, stop=True)
            T.matmul(ps[:, SM, 16 + E:16 + 2 * E], ones[:, :], chosen[:, 0, :], start=True, stop=False)
            T.matmul(ps[:, SM, 16 + E:16 + 2 * E], tri[:, :], chosen[:, 1, :], start=False, stop=True)
            T.matmul(ps[:, SM, 32:32 + E], ones[:, :], chosen[:, 0, :], start=True, stop=False)
            T.matmul(ps[:, SM, 32:32 + E], ones[:, :], chosen[:, 1, :], start=False, stop=True).then_inc(pos_ps, 1)

            def gather(count):
                pe.wait_ge(slots_s, count + 1)
                for b in range(2):
                    for k in range(4 * b, 4 * b + 4):
                        for t in range(TT):
                            ins = T.matmul(ps[:, 5 + b, (k % 4) * P:(k % 4) * P + P], xn[:, t, k * P:(k + 1) * P],
                                           slot1h[:, t, :], start=t == 0, stop=t == TT - 1)
                    ins.then_inc(gat_ps, 1)

            def scatter():
                for n, b in enumerate((5, 6, 7, 2)):
                    t, h = n // 2, n % 2
                    T.matmul(ps[:, b, :], slotT[:, t, :], y_hi[:, h * BANK:(h + 1) * BANK], start=True, stop=False)
                    T.matmul(ps[:, b, :], slotT[:, t, :], y_lo[:, h * BANK:(h + 1) * BANK], start=False,
                             stop=True).then_inc(sc_ps, 1)

            gather(0)
            pe.wait_ge(tab_s, 1)
            n_over = pe.value_load(tab[0:1, TAB_N:TAB_N + 1], min_val=0, max_val=E)
            pe.wait_ge(moe_zero, 1)
            with pe.Fori(0, n_over + E) as j:
                ju = j * ITEM_UNITS
                half = KD // 2

                def half_depth(n, bank, a, extra):
                    ready(n, ju + extra)
                    w = split(n, half)
                    for k in range(half):
                        ins = triple(ps[:, bank, :], lambda x_: u_[x_][:, half * a + k, 0:P], lambda x_: w(x_)[:, k, :],
                                     a == 0 and k == 0, a == 1 and k == half - 1)
                    ins.then_inc(used, 1)

                def gate(n, k, extra=0):
                    pe.wait_ge(msilu, j * FB + k)
                    for a in range(2):
                        half_depth(n + a, 0, a, extra)

                def up(n, k, extra=0):
                    pe.wait_ge(mhid, j * FB + k)
                    for a in range(2):
                        half_depth(n + a, 1, a, extra)

                def hidden_T(k):
                    pe.wait_ge(mhid, j * FB + (k + 1))
                    pe.wait_ge(mhT_lo, j * FB + k)
                    for c in range(4):
                        ins = T.transpose(ps[:, 2, c * P:(c + 1) * P], hid[:, 0, c * P:(c + 1) * P], ident[:, :])
                    ins.then_inc(mhT_ps, 1)

                def down_block(n, k, first=False, final=False, extra=0):
                    pe.wait_ge(mhT_lo, j * FB + (k + 1))
                    for a in range(2):
                        ready(n + a, ju + extra)
                        rows_product(n + a, lambda x_, r, t: hid_[x_][:, 0, (2 * a + r) * P:(2 * a + r + 1) * P], 3,
                                     first and a == 0, final and a == 1, tiles=1)

                pe.wait_ge(g_lo, j * 2 + 2)
                gate(MOE0, 0)
                pe.wait_ge(yl_s, j * 2)
                pe.wait_ge(sT_s, j)
                pe.wait_ge(mhT_lo, j * FB)
                scatter()
                up(MOE0 + 2, 0)
                gate(MOE0 + 4, 1)
                pe.wait_ge(sc_add, j * 4 + 4)
                hidden_T(0)
                up(MOE0 + 6, 1)
                for t in range(TT):
                    ins = T.transpose(ps[:, 7, t * P:(t + 1) * P], slot1h[:, t, :], ident[:, :])
                ins.then_inc(sT_ps, 1)
                down_block(MOE0 + 8, 0, first=True)
                with pe.Fori(2, FB) as i:
                    x6 = (i - 2) * 6
                    gate(MOE0 + 10, i, x6)
                    hidden_T(i - 1)
                    up(MOE0 + 12, i, x6)
                    down_block(MOE0 + 14, i - 1, extra=x6)
                gather(j + 1)
                hidden_T(FB - 1)
                down_block(MOE0 + 40, FB - 1, final=True)
            pe.wait_ge(yl_s, (n_over + E) * 2)
            pe.wait_ge(sT_s, n_over + E)
            pe.wait_ge(g_lo, (n_over + (E + 1)) * 2)
            scatter()


_INS = ["x", "norm_mix_g", "w_in", "ml_b_if", "ml_norm_g", "rg_conv_w", "rg_conv_b", "rg_w_a", "rg_b_a", "rg_w_x",
        "rg_b_x", "rg_lam", "rg_norm_g", "w_out", "norm_ffn_g", "ffn_w_gate", "ffn_w_up", "ffn_w_down", "moe_w_router",
        "moe_w_gate", "moe_w_up", "moe_w_down", "norm_final_g"]


def kernel(**inputs):
    import concourse.bacc as bacc
    from concourse.bass_utils import run_bass_kernel_spmd

    nc = bacc.Bacc("TRN2", target_bir_lowering=False, num_devices=1)
    arrays, args = {}, {}
    for name in _INS:
        a = np.ascontiguousarray(inputs[name])
        arrays[f"in_{name}"] = a
        args[name] = nc.dram_tensor(f"in_{name}", a.shape, mybir.dt.from_np(a.dtype), kind="ExternalInput").ap()
    out = nc.dram_tensor("out_y", inputs["x"].shape, F32, kind="ExternalOutput").ap()
    hybrid_kernel(nc, out=out, **args)
    r = run_bass_kernel_spmd(nc, [arrays], core_ids=[0])
    return r.results[0]["out_y"]
```

```python
from contextlib import ExitStack

import numpy as np
import concourse.bass as bass
from concourse import mybir

F32 = mybir.dt.float32
F32R = mybir.dt.float32r
I32 = mybir.dt.int32
U32 = mybir.dt.uint32
ALU = mybir.AluOpType
ACT = mybir.ActivationFunctionType
AX = mybir.AxisListType

P = 128
BANK = 512
RAW = 6
MORE = 3
SPLIT = 3
UNIT = 2048
EPS = 1e-6
NEG = -1e30


class Counted:

    def __init__(self, sem):
        self.sem, self.value = sem, 0

    def after(self, eng, ins):
        ins.then_inc(self.sem, 1)
        self.value += 1
        eng.wait_ge(self.sem, self.value)


def hybrid_kernel(nc, x, norm_mix_g, w_in, ml_b_if, ml_norm_g, rg_conv_w, rg_conv_b, rg_w_a, rg_b_a,
                  rg_w_x, rg_b_x, rg_lam, rg_norm_g, w_out, norm_ffn_g, ffn_w_gate, ffn_w_up,
                  ffn_w_down, moe_w_router, moe_w_gate, moe_w_up, moe_w_down, norm_final_g, out):
    _, S, D = x.shape
    LAYERS = w_in.shape[0]
    ML = ml_norm_g.shape[1]
    RG = rg_lam.shape[1]
    H = ml_b_if.shape[1] // 2
    DH = ML // H
    TAPS = rg_conv_w.shape[1]
    FD = ffn_w_gate.shape[2]
    E = moe_w_router.shape[2]
    FE = moe_w_gate.shape[3]
    TT = S // P
    KD = D // P
    KR = RG // P
    GB = rg_w_a.shape[2]
    CONV_PAD = TAPS - 1
    assert (LAYERS, TT, KD, KR, H, DH, E) == (2, 2, 8, 4, 4, P, 8)

    COLS = UNIT // KD
    MIX_UNITS = (4 * ML + 2 * RG) // COLS
    OUT_UNITS = D * D // (P * UNIT)
    FFN_STEPS = FD // COLS
    MIX0 = 0
    FFN0 = MIX0 + MIX_UNITS + OUT_UNITS
    MIX1 = FFN0 + 3 * FFN_STEPS
    MOE0 = MIX1 + MIX_UNITS + OUT_UNITS
    FB = FE // BANK
    ITEM_UNITS = 6 * FB
    MOE1 = MOE0 + ITEM_UNITS
    OVER = E
    assert MIX_UNITS == 12 and OUT_UNITS == 4 and FFN_STEPS % 2 == 1 and ITEM_UNITS % RAW == 0

    with ExitStack() as ctx:
        def sb(name, shape, dt=F32):
            return ctx.enter_context(nc.sbuf_tensor(name, shape, dt))

        def sem(name):
            return ctx.enter_context(nc.semaphore(name))

        raw = [sb(f"raw{i}", [P, UNIT]) for i in range(RAW)]
        w_hi = [sb(f"w_hi{i}", [P, UNIT], F32R) for i in range(SPLIT + 1)]
        w_lo = [sb(f"w_lo{i}", [P, UNIT], F32R) for i in range(SPLIT + 1)]
        resid = sb("resid", [P, TT, D])
        xn = sb("xn", [P, TT, D])
        u_hi = sb("u_hi", [P, KD, S], F32R)
        u_lo = sb("u_lo", [P, KD, S], F32R)
        hid_hi = w_hi[SPLIT][:, 0:2 * BANK].rearrange("p (b n) -> p b n", b=2)
        hid_lo = w_hi[SPLIT][:, 2 * BANK:].rearrange("p (b n) -> p b n", b=2)
        y_hi, y_lo = w_lo[SPLIT][:, 0:D], w_lo[SPLIT][:, D:2 * D]
        slotT = sb("slotT", [P, TT, P], F32R)
        SMALL = 3 * KD * E
        small_hi = sb("small_hi", [P, SMALL + P], F32R)
        small_lo = sb("small_lo", [P, SMALL + P], F32R)
        small_raw = sb("small_raw", [P, SMALL + P])
        smallT = sb("smallT", [E, S])
        ident = sb("ident", [P, P])
        tri = sb("tri", [P, P])
        ones = sb("ones", [P, P])
        last = sb("last", [P, P])
        acausal = sb("acausal", [P, P])
        iota = sb("iota", [P, P])
        block_a = sb("block_a", [P, KR, P])
        block_x = sb("block_x", [P, KR, P])
        gain_row = sb("gain_row", [P, D])
        if_bias = sb("if_bias", [P, LAYERS, 2 * H])
        arena = [sb(f"arena{i}", [P, 1024]) for i in range(4)]
        x_pad = sb("x_pad", [P, KR, S + CONV_PAD])
        PROWS = LAYERS * (2 * KD + (TAPS + 5) * KR)
        pcol = sb("pcol", [P, PROWS])
        sml = sb("sml", [P, 512])

        with ExitStack() as tiles:
            w_dec, kwc, decT, num_s, r_g, i_g = (tiles.enter_context(nc.sbuf_tensor(n, [P, 1024], F32))
                                                 for n in ("w_dec", "kwc", "decT", "num_s", "r_g", "i_g"))
        with ExitStack() as output:
            yr = [output.enter_context(nc.sbuf_tensor(n, [P, 1024], F32R))[:, :].rearrange("p (k s) -> p k s", k=KR)
                  for n in ("y_rg_hi", "y_rg_lo")]
        raw += [sb(f"raw_more{i}", [P, UNIT]) for i in range(MORE)]

        qT, kT, v_tok, sig_o = arena
        c4 = lambda t: t[:, :].rearrange("p (c h s) -> p c h s", c=TT, h=H)
        hv = lambda t: t.rearrange("p (h s) -> p h s", h=H)
        rv = lambda t: t[:, :].rearrange("p (k s) -> p k s", k=KR)
        hv4 = lambda bank: bank.rearrange("p (h s) -> p h s", h=H)
        num_s_half = lambda c: num_s[:, c * BANK:(c + 1) * BANK]
        kw_tok = kwc[:, 0:BANK].rearrange("p (h s) -> p h s", h=H)
        c_st = kwc[:, BANK:2 * BANK].rearrange("p (h s) -> p h s", h=H)
        xc = xn[:, 0, :].rearrange("p (k s) -> p k s", k=KR)
        gate_g = xn[:, 1, :].rearrange("p (k s) -> p k s", k=KR)
        silu_s = qT[:, :].rearrange("p (b n) -> p b n", b=2)
        hid = kT[:, :].rearrange("p (b n) -> p b n", b=2)
        slot1h = v_tok[:, 0:TT * P].rearrange("p (t s) -> p t s", t=TT)
        prow = num_s[:, 0:P]

        _at = [0]

        def cols(n):
            _at[0] += n
            assert _at[0] <= 512
            return sml[:, _at[0] - n:_at[0]]

        msq = cols(TT * 2).rearrange("p (t h o) -> p t h o", t=TT, h=2)
        msq_eps, std, rstd = cols(TT), cols(TT), cols(TT)
        z_if = cols(TT * 2 * H).rearrange("p (c n) -> p c n", c=TT)
        nabs, e_f, ls_a, ls_b, ls_c = (cols(TT * H) for _ in range(5))
        log_f, b_cum, r_in, cmax, m_run = (cols(TT * H) for _ in range(5))
        sel_in = cols(2 * H)
        sel_out = cols(2 * H)
        m_prev = cols(H)
        exp_in, exp_out = cols(4 * H), cols(4 * H)
        den, n_st = cols(TT * H), cols(H)
        qn = cols(H)
        hsq, hstd, hrstd = cols(TT * H), cols(TT * H), cols(TT * H)
        rstd_rg, std_rg = cols(TT), cols(TT)
        lam_n, lam_e, lam_a, lam_b, lam_c, decay = (cols(KR) for _ in range(6))
        eps_c = cols(1)
        logit = cols(TT * E).rearrange("p (t e) -> p t e", t=TT)
        top8 = cols(TT * E).rearrange("p (t e) -> p t e", t=TT)
        topf = cols(TT * E).rearrange("p (t e) -> p t e", t=TT)
        gdiff, gexp, gw1, gw2 = cols(TT), cols(TT), cols(TT), cols(TT)
        hot1 = cols(TT * E).rearrange("p (t e) -> p t e", t=TT)
        hot2 = cols(TT * E).rearrange("p (t e) -> p t e", t=TT)
        chosen = cols(TT * E).rearrange("p (t e) -> p t e", t=TT)
        gate2 = cols(TT * 2 * E).rearrange("p (t q) -> p t q", t=TT)
        slot_of = cols(TT * 2 * E).rearrange("p (t q) -> p t q", t=TT)
        ov, ovc, zero8 = cols(E), cols(E), cols(E)
        tabf = cols(32)
        topi = sb("topi", [P, TT, E], U32)
        tab = sb("tab", [1, 32], I32)
        ovm = sb("ovm", [1, E, E])
        TAB_N, TAB_E = 25, 17

        FIRST, at = {}, 0
        PARAMS = (("mix", norm_mix_g, KD), ("ffn", norm_ffn_g, KD), ("conv", rg_conv_w, TAPS * KR), ("conv_b", rg_conv_b, KR),
                  ("b_a", rg_b_a, KR), ("b_x", rg_b_x, KR), ("lam", rg_lam, KR), ("rgn", rg_norm_g, KR))
        for name, _, n in PARAMS:
            FIRST[name] = (at, n)
            at += LAYERS * n
        assert at == PROWS

        def pcs(l, name):
            a, n = FIRST[name]
            return pcol[:, a + l * n:a + (l + 1) * n]

        def pc(l, name, k=0):
            return pcs(l, name)[:, k:k + 1]

        ps = ctx.enter_context(nc.psum_tensor("ps", [P, 8, BANK], F32))
        SM = 2

        loaded = [sem(f"unit_loaded{i}") for i in range(RAW + MORE)]
        hi_done, lo_done = sem("unit_hi_done"), sem("unit_lo_done")
        used = sem("unit_used")
        x_loaded = [sem(f"x_loaded{t}") for t in range(TT)]
        rows_loaded, small_loaded = sem("rows_loaded"), sem("small_loaded")
        bias_loaded, gain_loaded = sem("gate_bias_loaded"), sem("ml_gain_loaded")
        block_loaded, final_loaded = sem("block_loaded"), sem("final_gain_loaded")
        consts_s, block_zero, small_zero = sem("consts"), sem("block_zero"), sem("small_zero")
        pool_own, dve_own, act_own = (Counted(sem(n)) for n in ("pool_own", "dve_own", "act_own"))
        rows_T, pcol_s = sem("rows_transposed"), sem("pcol_ready")
        small_hi_s, small_lo_s = sem("small_hi_s"), sem("small_lo_s")
        resid_ready, std_ready, xn_ready = sem("resid_ready"), sem("std_ready"), sem("xn_ready")
        xT_ps, u_hi_s, u_lo_s = sem("xT_in_psum"), sem("u_hi_s"), sem("u_lo_s")
        proj_out = sem("projection_evacuated")
        small_ps, smallT_s = sem("small_ps"), sem("smallT_s")
        acc_part = sem("acc_part")
        gates_ps, nabs_s, ef_s, logf_s = sem("gates_ps"), sem("nabs_s"), sem("exp_f_s"), sem("log_f_s")
        cum_ps, diag_s, r_ps = sem("cumsum_ps"), sem("diag_s"), sem("r_ps")
        qk_ps, sel_s, sel_ps, kt_ps = sem("qk_ps"), sem("chunk_end_s"), sem("chunk_end_ps"), sem("k_tok_ps")
        expin_s, expout_s = sem("exp_in_s"), sem("exp_out_s")
        wm_s, wexp_s, dec_s = sem("decay_log_s"), sem("decay_exp_s"), sem("decay_qk_s")
        dt_ps, decT_s, kw_s, c_ps, c_s = sem("decT_ps"), sem("decT_s"), sem("kw_s"), sem("c_ps"), sem("c_s")
        numer_ps = sem("numerators_ps")
        hsq_s, hstd_s, yml_s, yT_ps, yT_hi, yT_lo = (sem("head_sq_s"), sem("head_std_s"), sem("y_ml_s"),
                                                     sem("y_ml_T_ps"), sem("y_ml_T_hi"), sem("y_ml_T_lo"))
        lamn_s, lame_s, conv_s = sem("lam_neg_s"), sem("lam_exp_s"), sem("conv_s")
        ga_ps, ga_read, gx_ps, gx_read = sem("rg_a_ps"), sem("rg_a_read"), sem("rg_x_ps"), sem("rg_x_read")
        a_s, sqrt_in, sqrt_out = sem("decay_s"), sem("sqrt_in"), sem("sqrt_out")
        ix_s, y_s = sem("gated_input_s"), sem("y_rg_raw_s")
        ysq_s, ssq_ps, rgstd_s = sem("y_rg_sq_s"), sem("y_rg_ssq_ps"), sem("rg_std_s")
        yrg_s, yr_hi, yr_lo = sem("y_rg_s"), sem("y_rg_hi"), sem("y_rg_lo")
        silu_done, hid_s, hT_hi, hT_lo = sem("silu_done"), sem("hidden_s"), sem("hidden_hi"), sem("hidden_lo")
        logit_ps, gdiff_s, gexp_s, chosen_s = sem("logit_ps"), sem("gate_diff_s"), sem("gate_exp_s"), sem("chosen_s")
        pos_ps, tab_s, slots_s, moe_zero = sem("pos_ps"), sem("table_ready"), sem("slots_ready"), sem("moe_zero")
        mhT_ps, msilu, mhid, mhT_hi, mhT_lo = (sem("moe_hT_ps"), sem("moe_silu"), sem("moe_hid"),
                                               sem("moe_hT_hi"), sem("moe_hT_lo"))
        gat_ps, g_hi, g_lo = sem("gather_ps"), sem("gather_hi"), sem("gather_lo")
        sT_ps, sT_s, yh_s, yl_s = sem("slotT_ps"), sem("slotT_s"), sem("y_hi_s"), sem("y_lo_s")
        sc_ps, sc_add = sem("scatter_ps"), sem("scatter_added")
        fin_s, out_s = sem("final_ready"), sem("out_stored")

        x_v = x[0].rearrange("(t p) d -> p t d", p=P)
        out_v = out[0].rearrange("(t p) d -> p t d", p=P)
        deep = lambda w: w.rearrange("(k p) n -> p k n", p=P)

        def mix_cols(l, j):
            starts = [4 * ML + 2 * H, 0, ML, 2 * ML, 4 * ML + 2 * H + RG, 3 * ML]
            if j < MIX_UNITS:
                c = starts[j // 2] + COLS * (j % 2)
                return deep(w_in[l])[:, :, c:c + COLS]
            r = ((j - MIX_UNITS) * 2 + ML // P) % KD
            return deep(w_out[l])[:, r:r + 2, :]

        MORE0 = MOE0 + RAW + SPLIT
        ring = lambda n: n if n < MORE0 else n - MORE

        def raw_of(n):
            return RAW + n - MORE0 if MORE0 <= n < MORE0 + MORE else ring(n) % RAW

        def pair(n):
            for base in (MIX0, MIX1):
                if 0 <= n - base < MIX_UNITS + OUT_UNITS:
                    return (1, 2, 0, SPLIT)[(n - base) % (SPLIT + 1)]
            return n % SPLIT

        def pair_free(n):
            for base in (MIX0, MIX1):
                if SPLIT <= n - base < MIX_UNITS + OUT_UNITS:
                    return n - SPLIT
            return n - SPLIT + 1

        unit3 = lambda t, k: t[:, :].rearrange("p (k n) -> p k n", k=k)

        def load_blocks(eng, l):
            for h in range(2):
                for w, t in ((rg_w_a, block_a), (rg_w_x, block_x)):
                    eng.dma_start(t[GB * h:GB * h + GB, :, GB * h:GB * h + GB],
                                  w[l].rearrange("(k h) i j -> h i k j", h=2)[h]).then_inc(block_loaded, 16)

        small_cols = lambda i: small_raw[:, i * KD * E:(i + 1) * KD * E].rearrange("p (k n) -> p k n", k=KD)

        block = ctx.enter_context(nc.Block())

        @block.sync
        def _(sp):
            def load(n, src, k, extra=0):
                if raw_of(n) >= RAW:
                    sp.wait_ge(used, MIX1 + 14)
                elif n >= RAW:
                    before = n - RAW - (MORE if MORE0 + MORE <= n < MORE0 + MORE + RAW else 0)
                    sp.wait_ge(lo_done, extra + (before + 1))
                sp.dma_start(unit3(raw[raw_of(n)], k), src).then_inc(loaded[raw_of(n)], 16)

            def mixer(l, base):
                for j in range(MIX_UNITS + OUT_UNITS):
                    load(base + j, mix_cols(l, j), KD if j < MIX_UNITS else 2)

            for t in range(TT):
                sp.dma_start(resid[:, t, :], x_v[:, t, :]).then_inc(x_loaded[t], 16)
            at = 0
            for _, src, n in PARAMS:
                flat = src.rearrange("l j c -> (l j c)") if len(src.shape) == 3 else src.rearrange("l c -> (l c)")
                sp.dma_start(prow[at:at + LAYERS * n, :], flat.rearrange("(k p) -> k p", p=P)).then_inc(rows_loaded, 16)
                at += LAYERS * n
            for l in range(LAYERS):
                sp.dma_start(small_cols(l), deep(w_in[l])[:, :, 4 * ML:4 * ML + 2 * H]).then_inc(small_loaded, 16)
            sp.dma_start(small_cols(LAYERS), deep(moe_w_router[0])).then_inc(small_loaded, 16)
            mixer(0, MIX0)

            gate_v, up_v, down_v = deep(ffn_w_gate[0]), deep(ffn_w_up[0]), deep(ffn_w_down[0])
            load(FFN0, gate_v[:, :, 0:COLS], KD)
            load(FFN0 + 1, up_v[:, :, 0:COLS], KD)
            with sp.Fori(0, FFN_STEPS // 2) as it:
                for a in range(2):
                    n, i = FFN0 + 2 + 3 * a, it * 2 + (1 + a)
                    load(n, gate_v[:, :, bass.ds(i * COLS, COLS)], KD, it * 6)
                    load(n + 1, up_v[:, :, bass.ds(i * COLS, COLS)], KD, it * 6)
                    load(n + 2, down_v[:, bass.ds(it * 4 + 2 * a, 2), :], 2, it * 6)
            load(MIX1 - 1, down_v[:, 2 * FFN_STEPS - 2:2 * FFN_STEPS, :], 2)

            mixer(1, MIX1)
            sp.wait_ge(yml_s, LAYERS)
            sp.dma_start(gain_row[:, :], norm_final_g.partition_broadcast(P)).then_inc(final_loaded, 16)

            half = KD // 2

            def expert_units(first, e, extra=0, straight=1):
                g_v = moe_w_gate[0].rearrange("e (k p) n -> p e k n", p=P)
                u_v = moe_w_up[0].rearrange("e (k p) n -> p e k n", p=P)
                d_v = moe_w_down[0].rearrange("e (k p) n -> p e k n", p=P)

                def gate_up(n, i, extra):
                    for m, v in enumerate((g_v, u_v)):
                        for a in range(2):
                            load(n + 2 * m + a, v[:, bass.ds(e, 1), half * a:half * a + half, bass.ds(i * BANK, BANK)]
                                 .rearrange("p e k n -> p (e k) n"), half, extra)

                def down(n, i, extra):
                    for a in range(2):
                        load(n + a, d_v[:, bass.ds(e, 1), bass.ds(i * 4 + 2 * a, 2), :]
                             .rearrange("p e k n -> p (e k) n"), 2, extra)

                gate_up(first, 0, extra)
                for i in range(straight):
                    gate_up(first + 6 * i + 4, i + 1, extra)
                    down(first + 6 * i + 8, i, extra)
                with sp.Fori(1 + straight, FB) as i:
                    n = first + 6 * straight
                    gate_up(n + 4, i, extra + (i - (1 + straight)) * 6)
                    down(n + 8, i - 1, extra + (i - (1 + straight)) * 6)
                down(first + ITEM_UNITS - 2, FB - 1, extra)

            expert_units(MOE0, 0, straight=3)
            with sp.Fori(1, E) as j:
                expert_units(MOE1, j, (j - 1) * ITEM_UNITS)
            sp.wait_ge(tab_s, 1)
            n_over = sp.value_load(tab[0:1, TAB_N:TAB_N + 1], min_val=0, max_val=E)
            with sp.If(n_over > 0):
                with sp.Fori(0, n_over) as j:
                    e = sp.value_load(tab[0:1, bass.ds(j + TAB_E, 1)], min_val=0, max_val=E - 1)
                    expert_units(MOE1, e, (j + (E - 1)) * ITEM_UNITS)
            for a in range(3):
                load(MOE1 + a, deep(moe_w_gate[0, 0])[:, 0:half, 0:BANK], half, (n_over + (E - 1)) * ITEM_UNITS)
            sp.wait_ge(fin_s, 2)
            for t in range(TT):
                sp.dma_start(out_v[:, t, :], xn[:, t, :]).then_inc(out_s, 16)
            sp.wait_ge(out_s, 16 * TT)

        @block.gpsimd
        def _(pool):
            g = nc.gpsimd
            g.memset(small_raw[:, SMALL:], 0.0).then_inc(small_zero, 1)
            g.memset(block_a[:, :, :], 0.0).then_inc(block_zero, 1)
            g.memset(block_x[:, :, :], 0.0).then_inc(block_zero, 1)
            g.memset(ident[:, :], 0.0)
            g.memset(tri[:, :], 1.0)
            g.memset(ones[:, :], 1.0)
            g.memset(last[:, :], 0.0)
            g.memset(eps_c, EPS)
            g.memset(zero8, 0.0)
            g.memset(x_pad[:, :, 0:CONV_PAD], 0.0)
            pool_own.after(pool, g.memset(acausal[:, :], 0.0))
            sel = lambda t, **kw: g.affine_select(out=t[:, :], in_=t[:, :], **kw)
            sel(ident, compare_op=ALU.not_equal, fill=1.0, base=0, pattern=[[-1, P]], channel_multiplier=1)
            sel(tri, compare_op=ALU.is_ge, fill=0.0, base=0, pattern=[[1, P]], channel_multiplier=-1)
            sel(last, compare_op=ALU.not_equal, fill=1.0, base=1 - P, pattern=[[0, P]], channel_multiplier=1)
            sel(acausal, compare_op=ALU.is_ge, fill=NEG, base=0, pattern=[[-1, P]], channel_multiplier=1)
            g.iota(iota[:, :], pattern=[[1, P]], base=0, channel_multiplier=0,
                   allow_small_or_imprecise_dtypes=True).then_inc(consts_s, 1)
            for l in range(LAYERS):
                pool.dma_start(if_bias[:, l, :], ml_b_if[l].partition_broadcast(P)).then_inc(bias_loaded, 16)
            pool.wait_ge(block_zero, 2)
            load_blocks(pool, 0)
            for l in range(LAYERS):
                pool.dma_start(gain_row[:, l * ML:(l + 1) * ML], ml_norm_g[l].partition_broadcast(P)).then_inc(gain_loaded, 16)
            for l in range(LAYERS):
                pool.wait_ge(conv_s, l + 1)
                pool.wait_ge(gx_read, l + 1)
                g.tensor_tensor(rv(i_g), rv(i_g), xc, ALU.mult).then_inc(ix_s, 1)
                pool.wait_ge(y_s, l + 1)
                g.tensor_tensor(r_g[:, :], i_g[:, :], i_g[:, :], ALU.mult).then_inc(ysq_s, 1)
                if l == 0:
                    pool.wait_ge(gx_ps, 1)
                    load_blocks(pool, 1)
            pool.wait_ge(used, MOE0)
            g.memset(y_hi.bitcast(F32), 0.0)
            g.memset(y_lo.bitcast(F32), 0.0)
            g.memset(slotT[:, :, :].bitcast(F32), 0.0).then_inc(moe_zero, 1)

        @block.scalar
        def _(act):
            a = nc.scalar

            def hi(n, extra=0, turns=0):
                turn = 0 if raw_of(n) >= RAW else ring(n) // RAW
                act.wait_ge(loaded[raw_of(n)], turns * 16 + 16 * (turn + 1))
                if pair_free(n) > 0:
                    act.wait_ge(used, extra + pair_free(n))
                a.copy(w_hi[pair(n)][:, :], raw[raw_of(n)][:, :]).then_inc(hi_done, 1)

            def norm_std(m):
                for t in range(TT):
                    if t == 0:
                        if m == 0:
                            act.wait_ge(small_zero, 1)
                        act_own.after(act, a.activation(std[:, 0:1], small_raw[:, SMALL:SMALL + 1], ACT.Sqrt))
                    if m == 0:
                        act.wait_ge(x_loaded[t], 16)
                        if t == 0:
                            act.wait_ge(consts_s, 1)
                        std_tile(t)
                    else:
                        std_tile(t, lambda h: act.wait_ge(resid_ready, 4 * (m - 1) + 2 * t + h + 1))

            def std_tile(t, wait_half=None):
                for h in range(2):
                    if wait_half is not None:
                        wait_half(h)
                    act_own.after(act, a.activation(xn[:, t, h * BANK:(h + 1) * BANK], resid[:, t, h * BANK:(h + 1) * BANK],
                                                    ACT.Square, scale=float(D) ** -0.5, accum_out=msq[:, t, h]))
                    if h == 0:
                        act_own.after(act, a.activation(msq_eps[:, t:t + 1], msq[:, t, 0], ACT.Identity, bias=eps_c))
                a.activation(std[:, t:t + 1], msq[:, t, 1], ACT.Sqrt, bias=msq_eps[:, t:t + 1]).then_inc(std_ready, 1)

            def norm_hi(m, l, which):
                act.wait_ge(pcol_s, 1)
                for b in range(4):
                    act.wait_ge(xT_ps, 4 * m + b + 1)
                    for k in (2 * b, 2 * b + 1):
                        ins = a.activation(u_hi[:, k, :], ps[:, 4 + b, (k % 2) * S:(k % 2) * S + S], ACT.Copy,
                                           scale=pc(l, which, k))
                    ins.then_inc(u_hi_s, 1)

            def mixer(l, base):
                if l == 0:
                    norm_std(0)
                    act.wait_ge(small_loaded, 16 * (LAYERS + 1))
                    act.wait_ge(small_zero, 1)
                    a.copy(small_hi[:, :], small_raw[:, :]).then_inc(small_hi_s, 1)
                    norm_hi(0, 0, "mix")
                    hi(base)
                    hi(base + 1)
                else:
                    hi(base + 1)
                    norm_std(2 * l)
                    norm_hi(2 * l, l, "mix")
                hi(base + 2)
                hi(base + 3)

                def evac(j):
                    act.wait_ge(used, base + j + 1)
                    bank, part, second = ps[:, j % 2, :], j // 2, j % 2
                    tiles = bank.rearrange("p (k s) -> p k s", k=2)
                    by_tok = lambda t: t[:, :].rearrange("p (c n) -> p c n", c=TT)[:, :, second * COLS:(second + 1) * COLS]
                    if part == 0:
                        ins = a.copy(x_pad[:, 2 * second:2 * second + 2, CONV_PAD:], tiles)
                    elif part in (1, 2):
                        ins = a.copy((qT, kT)[part - 1][:, second * BANK:(second + 1) * BANK], bank)
                    elif part == 3:
                        ins = a.copy(by_tok(v_tok), tiles)
                    elif part == 4:
                        ins = a.activation(gate_g[:, 2 * second:2 * second + 2, :], tiles, ACT.Gelu_apprx_tanh)
                    else:
                        ins = a.activation(by_tok(sig_o), tiles, ACT.Sigmoid)
                    ins.then_inc(proj_out, 1)

                def recurrent_gate(out_t, bias):
                    for k in range(KR):
                        ins = a.activation(rv(out_t)[:, k, :], ps[:, 4 + k // 2, (k % 2) * S:(k % 2) * S + S], ACT.Sigmoid,
                                           bias=pc(l, bias, k))
                    return ins

                evac(0)
                hi(base + 4)
                act.wait_ge(nabs_s, l + 1)
                a.activation(e_f, nabs, ACT.Exp).then_inc(ef_s, 1)
                act.wait_ge(lamn_s, l + 1)
                a.activation(lam_e, lam_n, ACT.Exp).then_inc(lame_s, 1)
                for j in range(1, 5):
                    evac(j)
                    hi(base + j + 4)
                evac(5)
                act.wait_ge(expin_s, l + 1)
                a.activation(exp_out, exp_in, ACT.Exp).then_inc(expout_s, 1)
                act.wait_ge(wm_s, l + 1)
                a.activation(w_dec[:, :], w_dec[:, :], ACT.Exp).then_inc(wexp_s, 1)
                hi(base + 9)
                act.wait_ge(ga_ps, l + 1)
                recurrent_gate(r_g, "b_a").then_inc(ga_read, 1)
                evac(6)
                hi(base + 10)
                act.wait_ge(gx_ps, l + 1)
                recurrent_gate(i_g, "b_x").then_inc(gx_read, 1)
                act.wait_ge(conv_s, l + 1)
                for k in range(KR):
                    ins = a.activation(x_pad[:, k, CONV_PAD:], rv(r_g)[:, k, :], ACT.Tanh, scale=decay[:, k:k + 1])
                act_own.after(act, ins)
                for k in range(KR):
                    ins = a.activation(rv(r_g)[:, k, :], rv(r_g)[:, k, :], ACT.Exp, scale=lam_c[:, k:k + 1])
                ins.then_inc(a_s, 1)
                evac(7)
                hi(base + 11)
                for c in range(TT):
                    act.wait_ge(dt_ps, 2 * l + c + 1)
                    ins = a.copy(decT[:, c * BANK:(c + 1) * BANK], ps[:, 4 + c, :])
                ins.then_inc(decT_s, 1)
                act.wait_ge(c_ps, l + 1)
                a.copy(c_st, ps[:, 3, :].rearrange("p (h s) -> p h s", h=H))
                a.copy(n_st, ps[:, SM, 32:32 + H]).then_inc(c_s, 1)
                act.wait_ge(sqrt_in, l + 1)
                a.activation(kT[:, :], kT[:, :], ACT.Sqrt).then_inc(sqrt_out, 1)
                evac(8)
                hi(base + 12)
                evac(9)
                hi(base + 13)
                act.wait_ge(hsq_s, l + 1)
                a.activation(hstd, hsq, ACT.Sqrt, bias=eps_c, scale=1.0 / DH).then_inc(hstd_s, 1)
                evac(10)
                act.wait_ge(yrg_s, l + 1)
                a.copy(yr[0], rv(kT)).then_inc(yr_hi, 1)
                hi(base + 14)
                evac(11)
                hi(base + 15)
                act.wait_ge(ssq_ps, l + 1)
                a.activation(std_rg, ps[:, SM, 48:48 + TT], ACT.Sqrt, bias=eps_c, scale=1.0 / RG).then_inc(rgstd_s, 1)
                for b in range(2):
                    act.wait_ge(yT_ps, 2 * l + b + 1)
                    a.copy(u_hi[:, 2 * b:2 * b + 2, :], ps[:, b, :].rearrange("p (k s) -> p k s", k=2)).then_inc(yT_hi, 1)

            mixer(0, MIX0)

            hi(FFN0)
            hi(FFN0 + 1)
            norm_std(1)
            norm_hi(1, 0, "ffn")

            def ffn_step(n, par, i, extra, turns, has_down):
                hi(n + 2, extra, turns)
                act.wait_ge(used, extra + n + 1)
                if has_down:
                    act.wait_ge(hid_s, i)
                a.activation(silu_s[:, par, :], ps[:, par, :], ACT.Silu).then_inc(silu_done, 1)
                if has_down:
                    hi(n + 3, extra, turns)
                act.wait_ge(hid_s, i + 2)
                if has_down:
                    act.wait_ge(used, extra + n)
                a.copy(hid_hi[:, par, :], hid[:, par, :]).then_inc(hT_hi, 1)
                hi(n + (4 if has_down else 3), extra, turns)

            ffn_step(FFN0, 0, 0, 0, 0, False)
            with act.Fori(0, FFN_STEPS // 2) as it:
                for b in range(2):
                    ffn_step(FFN0 + 2 + 3 * b, (1 + b) % 2, it * 2 + (1 + b), it * 6, it, True)

            mixer(1, MIX1)
            hi(MOE0)
            hi(MOE0 + 1)
            norm_std(3)
            norm_hi(3, 1, "ffn")
            hi(MOE0 + 2)
            act.wait_ge(gdiff_s, 1)
            a.activation(gexp, gdiff, ACT.Exp).then_inc(gexp_s, 1)

            def gather_hi(count):
                for b in range(2):
                    act.wait_ge(gat_ps, count * 2 + (b + 1))
                    for k in range(4 * b, 4 * b + 4):
                        ins = a.activation(u_hi[:, k, 0:P], ps[:, 5 + b, (k % 4) * P:(k % 4) * P + P], ACT.Copy,
                                           scale=pc(1, "ffn", k))
                    ins.then_inc(g_hi, 1)

            gather_hi(0)
            act.wait_ge(tab_s, 1)
            n_over = act.value_load(tab[0:1, TAB_N:TAB_N + 1], min_val=0, max_val=E)
            act.sem_inc(msilu, 1)
            act.sem_inc(sT_s, 1)
            def item(j, first, ju, jt):
                def silu(n, k, extra=0):
                    act.wait_ge(used, ju + extra + (n + 1))
                    act.wait_ge(mhid, j * FB + (k + 1))
                    a.activation(silu_s[:, 0, :], ps[:, 0, :], ACT.Silu).then_inc(msilu, 1)

                def hT(k):
                    act.wait_ge(mhT_ps, j * FB + k + 1)
                    a.copy(hid_hi[:, 0, :], ps[:, 2, :]).then_inc(mhT_hi, 1)

                h = lambda n, extra=0, turns=0: hi(first + n, ju + extra, jt + turns)
                h(3)
                h(4)
                silu(first + 1, 0)
                h(5)
                h(6)
                h(7)
                hT(0)
                h(8)
                silu(first + 5, 1)
                h(9)
                act.wait_ge(sT_ps, j + 1)
                a.copy(slotT[:, :, :], ps[:, 7, 0:TT * P].rearrange("p (t s) -> p t s", t=TT)).then_inc(sT_s, 1)
                h(10)
                h(11)
                with act.Fori(2, FB) as i:
                    x6, t1 = (i - 2) * 6, i - 2
                    h(12, x6, t1)
                    h(13, x6, t1)
                    hT(i - 1)
                    h(14, x6, t1)
                    silu(first + 11, i, x6)
                    h(15, x6, t1)
                    h(16, x6, t1)
                    h(17, x6, t1)
                hT(FB - 1)
                gather_hi(j + 1)
                h(42)
                h(43)
                for b in range(2):
                    act.wait_ge(used, ju + (first + ITEM_UNITS))
                    a.copy(y_hi[:, b * BANK:(b + 1) * BANK], ps[:, 3 + b, :]).then_inc(yh_s, 1)
                h(44)

            item(0, MOE0, 0, 0)
            with act.Fori(1, n_over + E) as j:
                item(j, MOE1, (j - 1) * ITEM_UNITS, (j - 1) * (ITEM_UNITS // RAW))
            act_own.after(act, a.activation(std[:, 0:1], eps_c, ACT.Sqrt))
            for t in range(TT):
                std_tile(t, lambda h: act.wait_ge(sc_add, (n_over + E) * 4 + (2 * t + h + 1)))

        @block.vector
        def _(dve):
            v = nc.vector
            own = lambda ins: dve_own.after(dve, ins)
            bc = lambda ap, axis, shape: ap.unsqueeze(axis).broadcast_to(shape)

            def lo(n, extra=0):
                dve.wait_ge(hi_done, extra + (n + 1))
                v.tensor_tensor(w_lo[pair(n)][:, :], raw[raw_of(n)][:, :], w_hi[pair(n)][:, :].bitcast(F32),
                                ALU.subtract).then_inc(lo_done, 1)

            def norm_tile(m, t):
                dve.wait_ge(std_ready, 2 * m + t + 1)
                own(v.reciprocal(rstd[:, t:t + 1], std[:, t:t + 1]))
                v.tensor_scalar(xn[:, t, :], resid[:, t, :], rstd[:, t:t + 1], None, ALU.mult).then_inc(xn_ready, 1)

            def norm_lo(m, l, which):
                for b in range(4):
                    dve.wait_ge(u_hi_s, 4 * m + b + 1)
                    for k in (2 * b, 2 * b + 1):
                        ins = v.scalar_tensor_tensor(u_lo[:, k, :], ps[:, 4 + b, (k % 2) * S:(k % 2) * S + S],
                                                     pc(l, which, k), u_hi[:, k, :].bitcast(F32), ALU.mult, ALU.subtract)
                    ins.then_inc(u_lo_s, 1)

            def log1p(z, s_, s2, p):
                own(v.tensor_scalar(s_, z, 2.0, None, ALU.add))
                own(v.reciprocal(s_, s_))
                own(v.tensor_tensor(s_, z, s_, ALU.mult))
                own(v.tensor_tensor(s2, s_, s_, ALU.mult))
                own(v.tensor_scalar(p, s2, 1.0 / 15, None, ALU.mult))
                for n in (13, 11, 9, 7, 5, 3):
                    own(v.scalar_tensor_tensor(p, p, 1.0 / n, s2, ALU.add, ALU.mult))
                own(v.scalar_tensor_tensor(p, p, 1.0, s_, ALU.add, ALU.mult))

            def transpose_small(i):
                dve.wait_ge(small_ps, i)
                v.tensor_copy(smallT[:, :], ps[0:E, 3, 0:S]).then_inc(smallT_s, 1)

            def add_and_norm(m, last_unit, bank):
                def add(t, h):
                    r = resid[:, t, h * BANK:(h + 1) * BANK]
                    v.tensor_tensor(r, ps[:, bank + 2 * t + h, :], r, ALU.add).then_inc(resid_ready, 1)

                dve.wait_ge(acc_part, 2 * m - 1)
                add(0, 0)
                add(0, 1)
                dve.wait_ge(acc_part, 2 * m)
                add(1, 0)
                dve.wait_ge(resid_ready, 4 * m - 1)
                norm_tile(m, 0)
                dve.wait_ge(used, last_unit + 1)
                add(1, 1)
                dve.wait_ge(resid_ready, 4 * m)
                norm_tile(m, 1)

            def mixer(l, base):
                if l == 0:
                    for t in range(TT):
                        norm_tile(0, t)
                    dve.wait_ge(small_hi_s, 1)
                    v.tensor_tensor(small_lo[:, :], small_raw[:, :], small_hi[:, :].bitcast(F32),
                                    ALU.subtract).then_inc(small_lo_s, 1)
                    norm_lo(0, 0, "mix")
                    lo(base)
                else:
                    norm_lo(2 * l, l, "mix")
                lo(base + 1)
                transpose_small(l + 1)
                lo(base + 2)
                lo(base + 3)
                dve.wait_ge(gates_ps, l + 1)
                if l == 0:
                    dve.wait_ge(bias_loaded, 16 * LAYERS)
                own(v.tensor_tensor(z_if, ps[:, SM, 0:TT * 2 * H].rearrange("p (c n) -> p c n", c=TT),
                                    bc(if_bias[:, l, :], 1, [P, TT, 2 * H]), ALU.add))
                ig, fg = z_if[:, :, 0:H], z_if[:, :, H:2 * H]
                c2 = lambda t: t.rearrange("p (c h) -> p c h", c=TT)
                v.scalar_tensor_tensor(c2(nabs), fg, -1.0, fg, ALU.mult, ALU.min).then_inc(nabs_s, 1)
                v.scalar_tensor_tensor(lam_n, pcs(l, "lam"), -1.0, pcs(l, "lam"), ALU.mult, ALU.min).then_inc(lamn_s, 1)
                lo(base + 4)
                dve.wait_ge(ef_s, l + 1)
                log1p(e_f, ls_a, ls_b, ls_c)
                own(v.tensor_scalar(c2(ls_a), fg, 0.0, None, ALU.min))
                v.scalar_tensor_tensor(log_f, ls_c, -2.0, ls_a, ALU.mult, ALU.add).then_inc(logf_s, 1)
                lo(base + 5)
                dve.wait_ge(lame_s, l + 1)
                log1p(lam_e, lam_a, lam_b, decay)
                own(v.tensor_scalar(lam_a, pcs(l, "lam"), -1.0, 0.0, ALU.mult, ALU.max))
                own(v.scalar_tensor_tensor(lam_b, decay, 2.0, lam_a, ALU.mult, ALU.add))
                v.tensor_scalar(decay, lam_b, 8.0, None, ALU.mult)
                v.tensor_scalar(lam_c, lam_b, -8.0, None, ALU.mult)
                lo(base + 6)
                dve.wait_ge(cum_ps, l + 1)
                own(v.tensor_copy(b_cum, ps[:, SM, 16:16 + TT * H]))
                own(v.tensor_tensor(c2(r_in), ig, c2(b_cum), ALU.subtract))
                v.tensor_tensor(decT[:, :].rearrange("p (n s) -> p n s", s=P), bc(ident[:, :], 1, [P, TT * H, P]),
                                bc(r_in, 2, [P, TT * H, P]), ALU.mult).then_inc(diag_s, 1)
                dve.wait_ge(proj_out, l * MIX_UNITS + 2)
                for j in range(TAPS):
                    for k in range(KR):
                        row = x_pad[:, k, j:j + S]
                        tap = pc(l, "conv", j * KR + k)
                        if j == 0:
                            ins = v.tensor_scalar(xc[:, k, :], row, tap, pc(l, "conv_b", k), ALU.mult, ALU.add)
                        else:
                            ins = v.scalar_tensor_tensor(xc[:, k, :], row, tap, xc[:, k, :], ALU.mult, ALU.add)
                    if j < TAPS - 1:
                        own(ins)
                ins.then_inc(conv_s, 1)
                lo(base + 7)
                dve.wait_ge(r_ps, l + 1)
                for c in range(TT):
                    ins = v.tensor_tensor(c4(w_dec)[:, c], hv4(ps[:, 4 + c, :]), bc(acausal[:, :], 1, [P, H, P]), ALU.add)
                own(ins)
                own(v.tensor_reduce(cmax, w_dec[:, :].rearrange("p (n s) -> p n s", s=P), AX.X, ALU.max))
                own(v.tensor_scalar(m_run[:, 0:H], cmax[:, 0:H], 0.0, None, ALU.max))
                v.tensor_copy(sel_in[:, 0:H], m_run[:, 0:H])
                v.tensor_copy(sel_in[:, H:2 * H], b_cum[:, 0:H]).then_inc(sel_s, 1)
                lo(base + 8)
                dve.wait_ge(sel_ps, l + 1)
                own(v.tensor_copy(sel_out, ps[:, SM, 24:24 + 2 * H]))
                own(v.tensor_tensor(m_prev, sel_out[:, 0:H], sel_out[:, H:2 * H], ALU.add))
                own(v.tensor_tensor(m_run[:, H:2 * H], cmax[:, H:2 * H], m_prev, ALU.max))
                v.tensor_tensor(exp_in[:, 0:H], r_in[:, 0:H], sel_out[:, 0:H], ALU.subtract)
                v.tensor_tensor(exp_in[:, H:2 * H], m_prev, m_run[:, H:2 * H], ALU.subtract)
                v.scalar_tensor_tensor(exp_in[:, 2 * H:4 * H], b_cum, -1.0, m_run, ALU.mult,
                                       ALU.subtract).then_inc(expin_s, 1)
                v.tensor_tensor(w_dec[:, :].rearrange("p (n s) -> p n s", s=P), w_dec[:, :].rearrange("p (n s) -> p n s", s=P),
                                bc(m_run, 2, [P, TT * H, P]), ALU.subtract).then_inc(wm_s, 1)
                lo(base + 9)
                dve.wait_ge(wexp_s, l + 1)
                dve.wait_ge(qk_ps, l + 1)
                for c in range(TT):
                    w = w_dec[:, c * BANK:(c + 1) * BANK]
                    ins = v.scalar_tensor_tensor(w, ps[:, 6 + c, :], float(DH) ** -0.5, w, ALU.mult, ALU.mult)
                ins.then_inc(dec_s, 1)
                dve.wait_ge(kt_ps, l + 1)
                dve.wait_ge(expout_s, l + 1)
                own(v.tensor_scalar(exp_out[:, 0:H], exp_out[:, 0:H], float(DH) ** -0.5, None, ALU.mult))
                v.tensor_tensor(kw_tok, hv4(ps[:, 3, :]), bc(exp_out[:, 0:H], 2, [P, H, P]), ALU.mult).then_inc(kw_s, 1)
                lo(base + 10)
                dve.wait_ge(dec_s, l + 1)
                own(v.tensor_reduce(den, w_dec[:, :].rearrange("p (n s) -> p n s", s=P), AX.X, ALU.add))
                dve.wait_ge(a_s, l + 1)
                own(v.tensor_tensor(kT[:, :], r_g[:, :], r_g[:, :], ALU.mult))
                v.scalar_tensor_tensor(rv(kT), rv(kT), 1.0, x_pad[:, :, CONV_PAD:], ALU.add, ALU.mult).then_inc(sqrt_in, 1)
                lo(base + 11)
                dve.wait_ge(sqrt_out, l + 1)
                dve.wait_ge(ix_s, l + 1)
                own(v.tensor_tensor(i_g[:, :], i_g[:, :], kT[:, :], ALU.mult))
                for k in range(KR):
                    ins = v.tensor_tensor_scan(rv(kT)[:, k, :], rv(r_g)[:, k, :], rv(i_g)[:, k, :], 0.0, ALU.mult, ALU.add)
                own(ins)
                lo(base + 12)
                dve.wait_ge(numer_ps, l + 1)
                isc = exp_out[:, H:2 * H]
                v.tensor_tensor(qn, ps[:, SM, 36:36 + H], isc, ALU.mult)
                own(v.tensor_tensor(hv(num_s_half(1)), hv4(ps[:, 4, :]), bc(isc, 2, [P, H, P]), ALU.mult))
                v.tensor_tensor(num_s_half(1), ps[:, 7, :], num_s_half(1), ALU.add)
                own(v.tensor_tensor(den[:, H:2 * H], den[:, H:2 * H], qn, ALU.add))
                own(v.scalar_tensor_tensor(den, den, -1.0, den, ALU.mult, ALU.max))
                own(v.tensor_tensor(den, den, exp_out[:, 2 * H:4 * H], ALU.max))
                own(v.reciprocal(den, den))
                v.tensor_tensor(hv(num_s_half(0)), hv4(ps[:, 6, :]), bc(den[:, 0:H], 2, [P, H, P]), ALU.mult)
                own(v.tensor_tensor(hv(num_s_half(1)), hv(num_s_half(1)), bc(den[:, H:2 * H], 2, [P, H, P]), ALU.mult))
                own(v.tensor_tensor(decT[:, :], num_s[:, :], num_s[:, :], ALU.mult))
                v.tensor_reduce(hsq, decT[:, :].rearrange("p (n s) -> p n s", s=P), AX.X, ALU.add).then_inc(hsq_s, 1)
                lo(base + 13)
                dve.wait_ge(proj_out, l * MIX_UNITS + 10)
                v.tensor_tensor(rv(i_g), rv(kT), gate_g, ALU.mult).then_inc(y_s, 1)
                dve.wait_ge(y_s, l + 1)
                v.tensor_tensor(rv(kT), rv(i_g), bc(pcs(l, "rgn"), 2, [P, KR, S]), ALU.mult).then_inc(yrg_s, 1)
                dve.wait_ge(hstd_s, l + 1)
                if l == 0:
                    dve.wait_ge(gain_loaded, 16 * LAYERS)
                own(v.reciprocal(hrstd, hstd))
                own(v.tensor_tensor(num_s[:, :].rearrange("p (n s) -> p n s", s=P), num_s[:, :].rearrange("p (n s) -> p n s", s=P),
                                    bc(hrstd, 2, [P, TT * H, P]), ALU.mult))
                nv = num_s[:, :].rearrange("p (c n) -> p c n", c=TT)
                own(v.tensor_tensor(nv, nv, bc(gain_row[:, l * ML:(l + 1) * ML], 1, [P, TT, ML]), ALU.mult))
                dve.wait_ge(yr_hi, l + 1)
                v.tensor_tensor(yr[1], rv(kT), yr[0].bitcast(F32), ALU.subtract).then_inc(yr_lo, 1)
                lo(base + 14)
                lo(base + 15)
                dve.wait_ge(proj_out, (l + 1) * MIX_UNITS)
                v.tensor_tensor(num_s[:, :], num_s[:, :], sig_o[:, :], ALU.mult).then_inc(yml_s, 1)
                dve.wait_ge(rgstd_s, l + 1)
                own(v.reciprocal(rstd_rg, std_rg))
                for b in range(2):
                    dve.wait_ge(yT_hi, 2 * l + b + 1)
                    v.tensor_tensor(u_lo[:, 2 * b:2 * b + 2, :], ps[:, b, :].rearrange("p (k s) -> p k s", k=2),
                                    u_hi[:, 2 * b:2 * b + 2, :].bitcast(F32), ALU.subtract).then_inc(yT_lo, 1)
                lo(base + 16)
                dve.wait_ge(used, base + 14)
                for t in range(TT):
                    for h in range(2):
                        r = resid[:, t, h * BANK:(h + 1) * BANK]
                        ins = v.scalar_tensor_tensor(r, ps[:, 4 + 2 * t + h, :], rstd_rg[:, t:t + 1], r, ALU.mult, ALU.add)
                own(ins)
                add_and_norm(2 * l + 1, base + 15, 0)

            dve.wait_ge(rows_T, 1)
            v.tensor_copy(pcol[:, :], ps[:, 4, 0:PROWS]).then_inc(pcol_s, 1)
            dve.wait_ge(pcol_s, 1)
            mixer(0, MIX0)
            norm_lo(1, 0, "ffn")
            lo(FFN0 + 1)
            dve.sem_inc(hid_s, 1)

            def ffn_step(n, par, i, extra, has_down):
                lo(n + 2, extra)
                dve.wait_ge(used, extra + (n + 2))
                dve.wait_ge(silu_done, i + 1)
                v.tensor_tensor(hid[:, par, :], silu_s[:, par, :], ps[:, 2 + par, :], ALU.mult).then_inc(hid_s, 1)
                if has_down:
                    lo(n + 3, extra)
                dve.wait_ge(hT_hi, i + 1)
                v.tensor_tensor(hid_lo[:, par, :], hid[:, par, :], hid_hi[:, par, :].bitcast(F32),
                                ALU.subtract).then_inc(hT_lo, 1)
                lo(n + (4 if has_down else 3), extra)

            ffn_step(FFN0, 0, 0, 0, False)
            with dve.Fori(0, FFN_STEPS // 2) as it:
                for b in range(2):
                    ffn_step(FFN0 + 2 + 3 * b, (1 + b) % 2, it * 2 + (1 + b), it * 6, True)
            add_and_norm(2, MIX1 - 1, 4)
            mixer(1, MIX1)
            norm_lo(3, 1, "ffn")
            transpose_small(LAYERS + 1)

            def slots(q):
                for t in range(TT):
                    ins = v.tensor_scalar(slot1h[:, t, :], iota[:, :], slot_of[:, t, q], None, ALU.is_equal)
                ins.then_inc(slots_s, 1)

            dve.wait_ge(logit_ps, 1)
            own(v.tensor_copy(logit, ps[:, SM, 0:TT * E].rearrange("p (t e) -> p t e", t=TT)))
            for t in range(TT):
                ins = v.max(top8[:, t, :], logit[:, t, :])
            own(ins)
            v.tensor_tensor(gdiff.unsqueeze(2), top8[:, :, 1:2], top8[:, :, 0:1], ALU.subtract).then_inc(gdiff_s, 1)
            for t in range(TT):
                ins = v.max_index(topi[:, t, :], top8[:, t, :], logit[:, t, :])
            own(ins)
            own(v.tensor_copy(topf, topi[:, :, :]))
            for t in range(TT):
                v.tensor_scalar(hot1[:, t, :], iota[:, 0:E], topf[:, t, 0:1], None, ALU.is_equal)
                ins = v.tensor_scalar(hot2[:, t, :], iota[:, 0:E], topf[:, t, 1:2], None, ALU.is_equal)
            own(ins)
            v.tensor_tensor(chosen, hot1, hot2, ALU.add).then_inc(chosen_s, 1)
            dve.wait_ge(chosen_s, 1)
            lo(MOE0 + 1)
            dve.wait_ge(pos_ps, 1)
            own(v.tensor_tensor(topf, ps[:, SM, 16:16 + TT * E].rearrange("p (t e) -> p t e", t=TT), chosen, ALU.mult))
            own(v.tensor_scalar(slot_of[:, :, 0:E], topf, -1.0, None, ALU.add))
            slots(slice(0, 1))
            v.tensor_scalar(slot_of[:, :, E:2 * E], topf, -1.0 - P, None, ALU.add)
            v.memset(tabf, 0.0)
            own(v.tensor_scalar(ov, ps[:, SM, 32:32 + E], float(P), None, ALU.is_gt))
            own(v.tensor_tensor_scan(ovc, ov, zero8, 0.0, ALU.add, ALU.add))
            row = [1, E, E]
            own(v.tensor_tensor(ovm[:, :, :], bc(ovc[0:1, :], 1, row), bc(iota[0:1, 1:1 + E], 2, row), ALU.is_equal))
            own(v.tensor_tensor(ovm[:, :, :], ovm[:, :, :], bc(ov[0:1, :], 1, row), ALU.mult))
            own(v.tensor_tensor(ovm[:, :, :], ovm[:, :, :], bc(iota[0:1, 0:E], 1, row), ALU.mult))
            own(v.tensor_reduce(tabf[0:1, TAB_E:TAB_E + E], ovm[:, :, :], AX.X, ALU.add))
            v.tensor_copy(tabf[0:1, 1:1 + E], iota[0:1, 0:E])
            v.tensor_scalar(tabf[0:1, 1 + E:1 + 2 * E], tabf[0:1, TAB_E:TAB_E + E], float(OVER), None, ALU.add)
            own(v.tensor_copy(tabf[0:1, TAB_N:TAB_N + 1], ovc[0:1, E - 1:E]))
            v.tensor_copy(tab[:, :], tabf[0:1, :]).then_inc(tab_s, 1)
            dve.wait_ge(tab_s, 1)
            dve.wait_ge(gexp_s, 1)
            own(v.tensor_scalar(gw1, gexp, 1.0, None, ALU.add))
            own(v.reciprocal(gw1, gw1))
            own(v.tensor_tensor(gw2, gexp, gw1, ALU.mult))
            for t in range(TT):
                v.tensor_scalar(hot1[:, t, :], hot1[:, t, :], gw1[:, t:t + 1], None, ALU.mult)
                ins = v.tensor_scalar(hot2[:, t, :], hot2[:, t, :], gw2[:, t:t + 1], None, ALU.mult)
            own(ins)
            for q in range(2):
                ins = v.tensor_tensor(gate2[:, :, q * E:(q + 1) * E], hot1, hot2, ALU.add)
            own(ins)
            n_over = dve.value_load(tab[0:1, TAB_N:TAB_N + 1], min_val=0, max_val=E)

            def gather_lo(count):
                for b in range(2):
                    dve.wait_ge(g_hi, count * 2 + (b + 1))
                    for k in range(4 * b, 4 * b + 4):
                        ins = v.scalar_tensor_tensor(u_lo[:, k, 0:P], ps[:, 5 + b, (k % 4) * P:(k % 4) * P + P],
                                                     pc(1, "ffn", k), u_hi[:, k, 0:P].bitcast(F32), ALU.mult, ALU.subtract)
                    ins.then_inc(g_lo, 1)

            SCATTER = (5, 6, 7, 2)

            def scatter_add(j, q):
                for n, b in enumerate(SCATTER):
                    t, h = n // 2, n % 2
                    r = resid[:, t, h * BANK:(h + 1) * BANK]
                    dve.wait_ge(sc_ps, j * 4 + (n + 1))
                    v.scalar_tensor_tensor(r, ps[:, b, :], gate2[:, t, q], r, ALU.mult, ALU.add).then_inc(sc_add, 1)

            gather_lo(0)
            lo(MOE0 + 2)
            for done in (mhid, mhT_lo, yl_s):
                dve.sem_inc(done, 1)
            def item(j, first, ju):
                q_prev = dve.value_load(tab[0:1, bass.ds(j, 1)], min_val=0, max_val=2 * E - 1)
                q_next = dve.value_load(tab[0:1, bass.ds(j + 2, 1)], min_val=0, max_val=2 * E - 1)

                def mult(n, k, extra=0):
                    dve.wait_ge(used, ju + extra + (n + 1))
                    dve.wait_ge(msilu, j * FB + (k + 2))
                    v.tensor_tensor(hid[:, 0, :], silu_s[:, 0, :], ps[:, 1, :], ALU.mult).then_inc(mhid, 1)

                def hT(k):
                    dve.wait_ge(mhT_hi, j * FB + (k + 1))
                    v.tensor_tensor(hid_lo[:, 0, :], ps[:, 2, :], hid_hi[:, 0, :].bitcast(F32), ALU.subtract).then_inc(mhT_lo, 1)

                l_ = lambda n, extra=0: lo(first + n, ju + extra)
                l_(3)
                scatter_add(j, bass.ds(q_prev, 1))
                l_(4)
                l_(5)
                mult(first + 3, 0)
                l_(6)
                l_(7)
                hT(0)
                l_(8)
                l_(9)
                mult(first + 7, 1)
                l_(10)
                l_(11)
                dve.wait_ge(sT_ps, j + 1)
                slots(bass.ds(q_next, 1))
                with dve.Fori(2, FB) as i:
                    x6 = (i - 2) * 6
                    l_(12, x6)
                    l_(13, x6)
                    hT(i - 1)
                    l_(14, x6)
                    l_(15, x6)
                    mult(first + 13, i, x6)
                    l_(16, x6)
                    l_(17, x6)
                hT(FB - 1)
                gather_lo(j + 1)
                l_(42)
                l_(43)
                for b in range(2):
                    dve.wait_ge(yh_s, j * 2 + (b + 1))
                    v.tensor_tensor(y_lo[:, b * BANK:(b + 1) * BANK], ps[:, 3 + b, :],
                                    y_hi[:, b * BANK:(b + 1) * BANK].bitcast(F32), ALU.subtract).then_inc(yl_s, 1)
                l_(44)

            item(0, MOE0, 0)
            with dve.Fori(1, n_over + E) as j:
                item(j, MOE1, (j - 1) * ITEM_UNITS)
            q_last = dve.value_load(tab[0:1, bass.ds(n_over + E, 1)], min_val=0, max_val=2 * E - 1)
            scatter_add(n_over + E, bass.ds(q_last, 1))
            dve.wait_ge(final_loaded, 16)
            for t in range(TT):
                dve.wait_ge(std_ready, 9 + t)
                own(v.reciprocal(rstd[:, t:t + 1], std[:, t:t + 1]))
                v.scalar_tensor_tensor(xn[:, t, :], resid[:, t, :], rstd[:, t:t + 1], gain_row[:, :],
                                       ALU.mult, ALU.mult).then_inc(fin_s, 1)

        @block.tensor
        def _(pe):
            T = nc.tensor
            PASSES = 3

            def triple(out_ap, x_of, w_of, first, final, x_stationary=True):
                for n, (xa, wa) in enumerate(((0, 0), (1, 0), (0, 1))):
                    xs, ws = x_of(xa), w_of(wa)
                    lhsT, rhs = (xs, ws) if x_stationary else (ws, xs)
                    ins = T.matmul(out_ap, lhsT, rhs, start=first and n == 0, stop=final and n == PASSES - 1)
                return ins

            u_ = (u_hi, u_lo)
            hid_ = (hid_hi, hid_lo)

            def split(n, k):
                w = unit3(w_hi[pair(n)], k), unit3(w_lo[pair(n)], k)
                return lambda a: w[a]

            def ready(n, extra=0):
                pe.wait_ge(lo_done, extra + (n + 1))

            def keep_warm(bank, n):
                for _ in range(n):
                    T.matmul(ps[:, bank, 3 * P:], ident[:, :], ident[:, :], start=True, stop=True)

            def norm_T(m):
                for t in range(TT):
                    if m > 0 and t == 1:
                        keep_warm(7, 6)
                    pe.wait_ge(xn_ready, 2 * m + t + 1)
                    for k in range(KD):
                        if m == 2 and t == 0 and k == KD // 2:
                            pe.wait_ge(resid_ready, 4 * m)
                        c = (k % 2) * S + t * P
                        ins = T.transpose(ps[:, 4 + k // 2, c:c + P], xn[:, t, k * P:(k + 1) * P], ident[:, :])
                        if t == TT - 1 and k % 2:
                            ins.then_inc(xT_ps, 1)

            def small_product(which, m):
                keep_warm(3, 6)
                for k in range(KD):
                    if k % 2 == 0:
                        pe.wait_ge(u_lo_s, 4 * m + k // 2 + 1)
                    c = (which * KD + k) * E
                    ins = triple(ps[:, 3, 0:S], lambda a: u_[a][:, k, :],
                                 lambda a: (small_hi, small_lo)[a][:, c:c + P], k == 0, k == KD - 1, False)
                ins.then_inc(small_ps, 1)

            def small_back(i, signal):
                pe.wait_ge(smallT_s, i)
                for t in range(TT):
                    ins = T.transpose(ps[:, SM, t * E:(t + 1) * E], smallT[:, t * P:(t + 1) * P], ident[0:E, 0:E])
                ins.then_inc(signal, 1)

            def by_column(n, bank, extra=0, norm=None):
                ready(n, extra)
                w = split(n, KD)
                for c in range(2):
                    for k in range(KD):
                        if norm is not None and c == 0 and k % 2 == 0:
                            pe.wait_ge(u_lo_s, 4 * norm + k // 2 + 1)
                        ins = triple(ps[:, bank, c * S:(c + 1) * S], lambda a: u_[a][:, k, :],
                                     lambda a: w(a)[:, k, c * P:(c + 1) * P], k == 0, k == KD - 1, False)
                ins.then_inc(used, 1)

            def by_token(n, bank):
                ready(n)
                w = split(n, KD)
                for t in range(TT):
                    for k in range(KD):
                        ins = triple(ps[:, bank, t * COLS:(t + 1) * COLS], lambda a: u_[a][:, k, t * P:(t + 1) * P],
                                     lambda a: w(a)[:, k, :], k == 0, k == KD - 1)
                ins.then_inc(used, 1)

            def rows_product(n, x_of, bank, first, final, tiles=TT, parts=False):
                w = split(n, 2)
                for t in range(tiles):
                    for h in range(2):
                        for r in range(2):
                            ins = triple(ps[:, bank + 2 * t + h, :], lambda a: x_of(a, r, t),
                                         lambda a: w(a)[:, r, h * BANK:(h + 1) * BANK],
                                         first and r == 0, final and r == 1)
                        if parts and (t, h) in ((0, 1), (1, 0)):
                            ins.then_inc(acc_part, 1)
                ins.then_inc(used, 1)

            def mixer(l, base):
                norm_T(2 * l)
                if l == 0:
                    pe.wait_ge(small_lo_s, 1)
                small_product(l, 2 * l)

                def unit(j):
                    if j >= 2:
                        pe.wait_ge(proj_out, l * MIX_UNITS + j - 1)
                    (by_token if j // 2 in (3, 5) else by_column)(base + j, j % 2)

                unit(0)
                small_back(l + 1, gates_ps)
                unit(1)
                unit(2)
                pe.wait_ge(logf_s, l + 1)
                T.matmul(ps[:, SM, 16:16 + TT * H], tri[:, :], log_f, start=True, stop=True).then_inc(cum_ps, 1)
                unit(3)
                unit(4)
                pe.wait_ge(diag_s, l + 1)
                for c in range(TT):
                    ins = T.matmul(ps[:, 4 + c, :], ones[:, :], decT[:, c * BANK:(c + 1) * BANK], start=True, stop=True)
                ins.then_inc(r_ps, 1)
                unit(5)
                pe.wait_ge(sel_s, l + 1)
                T.matmul(ps[:, SM, 24:24 + 2 * H], last[:, :], sel_in, start=True, stop=True).then_inc(sel_ps, 1)
                pe.wait_ge(proj_out, l * MIX_UNITS + 6)
                head = lambda t, h, c: t[:, h * S + c * P:h * S + (c + 1) * P]
                col = lambda b, h: ps[:, b, h * P:(h + 1) * P]
                for c in range(TT):
                    for h in range(H):
                        ins = T.matmul(col(6 + c, h), head(qT, h, c), head(kT, h, c), start=True, stop=True)
                ins.then_inc(qk_ps, 1)
                for h in range(H):
                    ins = T.transpose(col(3, h), head(kT, h, 0), ident[:, :])
                ins.then_inc(kt_ps, 1)
                pe.wait_ge(conv_s, l + 1)
                pe.wait_ge(block_loaded, 64 * (l + 1))
                rg = lambda k: ps[:, 4 + k // 2, (k % 2) * S:(k % 2) * S + S]
                for k in range(KR):
                    ins = T.matmul(rg(k), block_a[:, k, :], xc[:, k, :], start=True, stop=True)
                ins.then_inc(ga_ps, 1)
                unit(6)
                pe.wait_ge(ga_read, l + 1)
                for k in range(KR):
                    ins = T.matmul(rg(k), block_x[:, k, :], xc[:, k, :], start=True, stop=True)
                ins.then_inc(gx_ps, 1)
                unit(7)
                pe.wait_ge(dec_s, l + 1)
                pe.wait_ge(gx_read, l + 1)
                for c in range(TT):
                    for h in range(H):
                        ins = T.transpose(col(4 + c, h), c4(w_dec)[:, c, h, :], ident[:, :])
                    ins.then_inc(dt_ps, 1)
                pe.wait_ge(kw_s, l + 1)
                pe.wait_ge(proj_out, l * MIX_UNITS + 8)
                vt = lambda c, h: v_tok[:, c * ML + h * P:c * ML + (h + 1) * P]
                for h in range(H):
                    T.matmul(col(3, h), kw_tok[:, h, :], vt(0, h), start=True, stop=True)
                for h in range(H):
                    ins = T.matmul(ps[:, SM, 32 + h:33 + h], kw_tok[:, h, :], ones[:, 0:1], start=True, stop=True)
                ins.then_inc(c_ps, 1)
                unit(8)
                pe.wait_ge(decT_s, l + 1)
                for c in range(TT):
                    for h in range(H):
                        T.matmul(col(6 + c, h), c4(decT)[:, c, h, :], vt(c, h), start=True, stop=True)
                pe.wait_ge(c_s, l + 1)
                for h in range(H):
                    T.matmul(col(4, h), head(qT, h, 1), c_st[:, h, :], start=True, stop=True)
                for h in range(H):
                    ins = T.matmul(ps[:, SM, 36 + h:37 + h], head(qT, h, 1), n_st[:, h:h + 1], start=True, stop=True)
                ins.then_inc(numer_ps, 1)
                unit(9)
                unit(10)
                unit(11)
                def out_unit(j, x_of, bank):
                    ready(base + j)
                    rows_product(base + j, x_of, bank, j % 2 == 0, j % 2 == 1, parts=j == MIX_UNITS + OUT_UNITS - 1)

                rg_rows = lambda j: lambda a, r, t: yr[a][:, 2 * (j - 12) + r, t * P:(t + 1) * P]
                pe.wait_ge(yr_lo, l + 1)
                out_unit(12, rg_rows(12), 4)
                pe.wait_ge(ysq_s, l + 1)
                for t in range(TT):
                    for k in range(KR):
                        ins = T.matmul(ps[:, SM, 48 + t:49 + t], rv(r_g)[:, k, t * P:(t + 1) * P], ones[:, 0:1],
                                       start=k == 0, stop=k == KR - 1)
                ins.then_inc(ssq_ps, 1)
                pe.wait_ge(yml_s, l + 1)
                for b in range(2):
                    for k in (2 * b, 2 * b + 1):
                        for t in range(TT):
                            c = (k % 2) * S + t * P
                            ins = T.transpose(ps[:, b, c:c + P], num_s[:, t * ML + k * P:t * ML + (k + 1) * P], ident[:, :])
                    ins.then_inc(yT_ps, 1)
                out_unit(13, rg_rows(13), 4)
                ml_rows = lambda j: lambda a, r, t: u_[a][:, 2 * (j - 14) + r, t * P:(t + 1) * P]
                pe.wait_ge(yT_lo, 2 * l + 2)
                pe.wait_ge(rgstd_s, l + 1)
                out_unit(14, ml_rows(14), 0)
                out_unit(15, ml_rows(15), 0)

            pe.wait_ge(consts_s, 1)
            pe.wait_ge(rows_loaded, 16 * len(PARAMS))
            T.transpose(ps[:, 4, 0:PROWS], prow[0:PROWS, :], ident[0:PROWS, 0:PROWS]).then_inc(rows_T, 1)
            pe.wait_ge(pcol_s, 1)
            mixer(0, MIX0)

            norm_T(1)

            def down(n, par, i, first=False, final=False, extra=0):
                ready(n, extra)
                pe.wait_ge(hT_lo, i + 1)
                rows_product(n, lambda a, r, t: hid_[a][:, par, r * S + t * P:r * S + (t + 1) * P], 4, first, final,
                             parts=final)

            def ffn_step(n, par, i, first, extra=0):
                if not first:
                    pe.wait_ge(silu_done, i - 1)
                by_column(n, par, extra)
                if not first:
                    pe.wait_ge(hid_s, i)
                by_column(n + 1, 2 + par, extra)
                down(n + 2, 1 - par, i - 1, first=first, extra=extra)

            by_column(FFN0, 0, norm=1)
            by_column(FFN0 + 1, 2)
            ffn_step(FFN0 + 2, 1, 1, True)
            ffn_step(FFN0 + 5, 0, 2, False)
            with pe.Fori(1, FFN_STEPS // 2) as it:
                for b in range(2):
                    ffn_step(FFN0 + 2 + 3 * b, 1 - b, it * 2 + (1 + b), False, it * 6)
            down(MIX1 - 1, 0, FFN_STEPS - 1, final=True)

            mixer(1, MIX1)
            norm_T(3)
            small_product(2, 3)
            small_back(LAYERS + 1, logit_ps)
            keep_warm(3, 9)
            pe.wait_ge(chosen_s, 1)
            T.matmul(ps[:, SM, 16:16 + E], tri[:, :], chosen[:, 0, :], start=True, stop=True)
            T.matmul(ps[:, SM, 16 + E:16 + 2 * E], ones[:, :], chosen[:, 0, :], start=True, stop=False)
            T.matmul(ps[:, SM, 16 + E:16 + 2 * E], tri[:, :], chosen[:, 1, :], start=False, stop=True)
            T.matmul(ps[:, SM, 32:32 + E], ones[:, :], chosen[:, 0, :], start=True, stop=False)
            T.matmul(ps[:, SM, 32:32 + E], ones[:, :], chosen[:, 1, :], start=False, stop=True).then_inc(pos_ps, 1)

            def gather(count):
                pe.wait_ge(slots_s, count + 1)
                for b in range(2):
                    for k in range(4 * b, 4 * b + 4):
                        for t in range(TT):
                            ins = T.matmul(ps[:, 5 + b, (k % 4) * P:(k % 4) * P + P], xn[:, t, k * P:(k + 1) * P],
                                           slot1h[:, t, :], start=t == 0, stop=t == TT - 1)
                    ins.then_inc(gat_ps, 1)

            def scatter():
                for n, b in enumerate((5, 6, 7, 2)):
                    t, h = n // 2, n % 2
                    T.matmul(ps[:, b, :], slotT[:, t, :], y_hi[:, h * BANK:(h + 1) * BANK], start=True, stop=False)
                    T.matmul(ps[:, b, :], slotT[:, t, :], y_lo[:, h * BANK:(h + 1) * BANK], start=False,
                             stop=True).then_inc(sc_ps, 1)

            keep_warm(7, 6)
            gather(0)
            pe.wait_ge(tab_s, 1)
            n_over = pe.value_load(tab[0:1, TAB_N:TAB_N + 1], min_val=0, max_val=E)
            pe.wait_ge(moe_zero, 1)
            def item(j, first, ju):
                half = KD // 2

                def half_depth(n, bank, a, extra):
                    ready(n, ju + extra)
                    w = split(n, half)
                    for k in range(half):
                        ins = triple(ps[:, bank, :], lambda x_: u_[x_][:, half * a + k, 0:P], lambda x_: w(x_)[:, k, :],
                                     a == 0 and k == 0, a == 1 and k == half - 1)
                    ins.then_inc(used, 1)

                def gate(n, k, extra=0, gathered=False):
                    pe.wait_ge(msilu, j * FB + (k + 1))
                    for a in range(2):
                        if gathered:
                            pe.wait_ge(g_lo, j * 2 + (a + 1))
                        half_depth(n + a, 0, a, extra)

                def up(n, k, extra=0):
                    pe.wait_ge(mhid, j * FB + (k + 1))
                    for a in range(2):
                        half_depth(n + a, 1, a, extra)

                def hidden_T(k):
                    pe.wait_ge(mhid, j * FB + (k + 2))
                    pe.wait_ge(mhT_lo, j * FB + (k + 1))
                    for c in range(4):
                        ins = T.transpose(ps[:, 2, c * P:(c + 1) * P], hid[:, 0, c * P:(c + 1) * P], ident[:, :])
                    ins.then_inc(mhT_ps, 1)

                def down_block(n, k, first=False, final=False, extra=0):
                    pe.wait_ge(mhT_lo, j * FB + (k + 2))
                    for a in range(2):
                        ready(n + a, ju + extra)
                        rows_product(n + a, lambda x_, r, t: hid_[x_][:, 0, (2 * a + r) * P:(2 * a + r + 1) * P], 3,
                                     first and a == 0, final and a == 1, tiles=1)

                gate(first, 0, gathered=True)
                pe.wait_ge(yl_s, j * 2 + 1)
                pe.wait_ge(sT_s, j + 1)
                pe.wait_ge(mhT_lo, j * FB + 1)
                scatter()
                up(first + 2, 0)
                gate(first + 4, 1)
                pe.wait_ge(sc_add, j * 4 + 4)
                hidden_T(0)
                up(first + 6, 1)
                for t in range(TT):
                    ins = T.transpose(ps[:, 7, t * P:(t + 1) * P], slot1h[:, t, :], ident[:, :])
                ins.then_inc(sT_ps, 1)
                down_block(first + 8, 0, first=True)
                with pe.Fori(2, FB) as i:
                    x6 = (i - 2) * 6
                    gate(first + 10, i, x6)
                    hidden_T(i - 1)
                    up(first + 12, i, x6)
                    down_block(first + 14, i - 1, extra=x6)
                hidden_T(FB - 1)
                gather(j + 1)
                down_block(first + 40, FB - 1, final=True)

            item(0, MOE0, 0)
            with pe.Fori(1, n_over + E) as j:
                item(j, MOE1, (j - 1) * ITEM_UNITS)
            pe.wait_ge(yl_s, (n_over + E) * 2 + 1)
            pe.wait_ge(sT_s, n_over + (E + 1))
            pe.wait_ge(g_lo, (n_over + (E + 1)) * 2)
            scatter()


_INS = ["x", "norm_mix_g", "w_in", "ml_b_if", "ml_norm_g", "rg_conv_w", "rg_conv_b", "rg_w_a", "rg_b_a", "rg_w_x",
        "rg_b_x", "rg_lam", "rg_norm_g", "w_out", "norm_ffn_g", "ffn_w_gate", "ffn_w_up", "ffn_w_down", "moe_w_router",
        "moe_w_gate", "moe_w_up", "moe_w_down", "norm_final_g"]


def kernel(**inputs):
    import concourse.bacc as bacc
    from concourse.bass_utils import run_bass_kernel_spmd

    nc = bacc.Bacc("TRN2", target_bir_lowering=False, num_devices=1)
    arrays, args = {}, {}
    for name in _INS:
        a = np.ascontiguousarray(inputs[name])
        arrays[f"in_{name}"] = a
        args[name] = nc.dram_tensor(f"in_{name}", a.shape, mybir.dt.from_np(a.dtype), kind="ExternalInput").ap()
    out = nc.dram_tensor("out_y", inputs["x"].shape, F32, kind="ExternalOutput").ap()
    hybrid_kernel(nc, out=out, **args)
    r = run_bass_kernel_spmd(nc, [arrays], core_ids=[0])
    return r.results[0]["out_y"]
```
